# Optimizing a Trainium2 kernel written in Bass

```python
import math
import jax, jax.numpy as jnp
from jax import lax
import numpy as np

D_MODEL = 1024
BATCH = 1
SEQ = 256
DEPTH = 2

N_A_LAYERS = DEPTH // 2
N_B_LAYERS = DEPTH - N_A_LAYERS
D_FF = 2816
FFN_HALF = 0.5
SSM_EXPAND = 2
SSM_D_INNER = SSM_EXPAND * D_MODEL
SSM_HEAD_DIM = 64
SSM_HEADS = SSM_D_INNER // SSM_HEAD_DIM
SSM_GROUPS = 4
SSM_STATE = 128
SSM_CONV = 4
SSM_CHUNK = 256
SSM_CONV_DIM = SSM_D_INNER + 2 * SSM_GROUPS * SSM_STATE
SSM_IN_DIM = SSM_D_INNER + SSM_CONV_DIM + SSM_HEADS
ATT_HEAD_DIM = 64
ATT_HEADS = D_MODEL // ATT_HEAD_DIM
ATT_KV_HEADS = ATT_HEADS // 8
ATT_GROUP = ATT_HEADS // ATT_KV_HEADS
ATT_WINDOW = 128
ATT_BLOCK = ATT_WINDOW
REL_BUCKETS = 32
REL_MAX_DIST = ATT_WINDOW
EPS = 1e-6


def rmsnorm(x, g):
    xf = x.astype(jnp.float32)
    y = xf * lax.rsqrt(jnp.mean(xf * xf, axis=-1, keepdims=True) + EPS)
    return (y * g.astype(jnp.float32)).astype(x.dtype)

def swiglu_half_step(h, g, w1, w3, w2):
    u = rmsnorm(h, g)
    return h + FFN_HALF * ((jax.nn.silu(u @ w1) * (u @ w3)) @ w2)

def causal_depthwise_conv(x, w, b):
    c = x.shape[-1]
    y = lax.conv_general_dilated(
        x, w.astype(x.dtype)[:, None, :], window_strides=(1,),
        padding=[(SSM_CONV - 1, 0)], dimension_numbers=('NWC', 'WIO', 'NWC'),
        feature_group_count=c)
    return y + b.astype(x.dtype)

def ssd_chunked_scan(x, dt, a, b_in, c_in):
    bsz, t, h, p = x.shape
    g, n = b_in.shape[2], b_in.shape[3]
    r = h // g
    L = SSM_CHUNK
    nc = -(-t // L)
    pad = nc * L - t
    f32 = jnp.float32

    def chunks(z):
        z = z.astype(f32)
        z = jnp.pad(z, [(0, 0), (0, pad)] + [(0, 0)] * (z.ndim - 2))
        z = z.reshape((bsz, nc, L) + z.shape[2:])
        return jnp.moveaxis(z, 1, 0)

    xc = chunks(x.reshape(bsz, t, g, r, p))
    dtc = chunks(dt.reshape(bsz, t, g, r))
    bc = chunks(b_in)
    cc = chunks(c_in)
    a_gr = a.astype(f32).reshape(g, r)
    causal = jnp.tril(jnp.ones((L, L), bool))[:, :, None, None]

    def step(state, inp):
        xk, dtk, bk, ck = inp
        acum = jnp.cumsum(dtk * a_gr, axis=1)
        seg = acum[:, :, None] - acum[:, None, :]
        decay = jnp.exp(jnp.where(causal, seg, -jnp.inf))
        cb = jnp.einsum('blgn,bsgn->blsg', ck, bk)
        scores = cb[..., None] * decay
        y_diag = jnp.einsum('blsgr,bsgr,bsgrp->blgrp', scores, dtk, xk)
        y_off = jnp.einsum('blgn,bgrpn,blgr->blgrp', ck, state, jnp.exp(acum))
        w_end = jnp.exp(acum[:, -1:] - acum) * dtk
        state = (state * jnp.exp(acum[:, -1])[..., None, None]
                 + jnp.einsum('bsgn,bsgr,bsgrp->bgrpn', bk, w_end, xk))
        return state, y_diag + y_off

    state0 = jnp.zeros((bsz, g, r, p, n), f32)
    _, y = lax.scan(step, state0, (xc, dtc, bc, cc))
    y = jnp.moveaxis(y, 0, 1).reshape(bsz, nc * L, h, p)[:, :t]
    return y.astype(x.dtype)

def mamba2_mixer(u, w_in, conv_w, conv_b, dt_bias, a_log, d_skip, gate_norm, w_out):
    bsz, t, _ = u.shape
    zxbcdt = u @ w_in
    z, xbc, dt = jnp.split(zxbcdt, [SSM_D_INNER, SSM_D_INNER + SSM_CONV_DIM], axis=-1)
    xbc = jax.nn.silu(causal_depthwise_conv(xbc, conv_w, conv_b))
    xs, b_in, c_in = jnp.split(xbc, [SSM_D_INNER, SSM_D_INNER + SSM_GROUPS * SSM_STATE], axis=-1)
    xs = xs.reshape(bsz, t, SSM_HEADS, SSM_HEAD_DIM)
    b_in = b_in.reshape(bsz, t, SSM_GROUPS, SSM_STATE)
    c_in = c_in.reshape(bsz, t, SSM_GROUPS, SSM_STATE)
    dt = jax.nn.softplus((dt + dt_bias).astype(jnp.float32))
    a = -jnp.exp(a_log.astype(jnp.float32))
    y = ssd_chunked_scan(xs, dt, a, b_in, c_in) + d_skip[:, None].astype(xs.dtype) * xs
    y = y.reshape(bsz, t, SSM_D_INNER) * jax.nn.silu(z)
    y = rmsnorm(y.reshape(bsz, t, SSM_GROUPS, SSM_D_INNER // SSM_GROUPS),
                gate_norm.reshape(SSM_GROUPS, SSM_D_INNER // SSM_GROUPS))
    return y.reshape(bsz, t, SSM_D_INNER) @ w_out

def shared_kv(h, kv_norm, w_kv, k_norm):
    bsz, t, _ = h.shape
    kv = rmsnorm(h, kv_norm) @ w_kv
    k, v = jnp.split(kv, 2, axis=-1)
    k = rmsnorm(k.reshape(bsz, t, ATT_KV_HEADS, ATT_HEAD_DIM), k_norm)
    v = v.reshape(bsz, t, ATT_KV_HEADS, ATT_HEAD_DIM)
    return k, v

def t5_bucket(dist):
    n = jnp.maximum(dist, 0)
    max_exact = REL_BUCKETS // 2
    nf = jnp.maximum(n, 1).astype(jnp.float32)
    large = max_exact + (jnp.log(nf / max_exact) / math.log(REL_MAX_DIST / max_exact)
                         * (REL_BUCKETS - max_exact)).astype(jnp.int32)
    large = jnp.minimum(large, REL_BUCKETS - 1)
    return jnp.where(n < max_exact, n, large)

def sliding_window_attention(u, k, v, w_q, q_norm, sinks, rel_bias, w_o):
    bsz, t, _ = u.shape
    blk = ATT_BLOCK
    nb = t // blk
    q = rmsnorm((u @ w_q).reshape(bsz, t, ATT_KV_HEADS, ATT_GROUP, ATT_HEAD_DIM), q_norm)
    qb = jnp.moveaxis(q.reshape(bsz, nb, blk, ATT_KV_HEADS, ATT_GROUP, ATT_HEAD_DIM), 1, 0)

    def band(z):
        prev = jnp.pad(z, [(0, 0), (blk, 0), (0, 0), (0, 0)])[:, :t]
        zz = jnp.concatenate([prev.reshape(bsz, nb, blk, ATT_KV_HEADS, ATT_HEAD_DIM),
                              z.reshape(bsz, nb, blk, ATT_KV_HEADS, ATT_HEAD_DIM)], axis=2)
        return jnp.moveaxis(zz, 1, 0)

    kb, vb = band(k), band(v)
    qi = jnp.arange(blk)[:, None] + blk
    kj = jnp.arange(2 * blk)[None, :]
    dist = qi - kj
    in_window = (dist >= 0) & (dist < ATT_WINDOW)
    bias = rel_bias[t5_bucket(dist)]
    bias = jnp.transpose(bias.reshape(blk, 2 * blk, ATT_KV_HEADS, ATT_GROUP),
                         (2, 3, 0, 1)).astype(jnp.float32)
    sink = sinks.reshape(ATT_KV_HEADS, ATT_GROUP)[None, :, :, None, None].astype(jnp.float32)
    scale = ATT_HEAD_DIM ** -0.5

    def block(args):
        qk, kk, vk, bi = args
        s = jnp.einsum('bqkrd,bskd->bkrqs', qk, kk).astype(jnp.float32) * scale + bias
        valid = in_window & ((bi > 0) | (kj >= blk))
        s = jnp.where(valid, s, -jnp.inf)
        m = jnp.maximum(jnp.max(s, axis=-1, keepdims=True), sink)
        p = jnp.exp(s - m)
        denom = jnp.sum(p, axis=-1, keepdims=True) + jnp.exp(sink - m)
        return jnp.einsum('bkrqs,bskd->bqkrd', (p / denom).astype(vk.dtype), vk)

    o = lax.map(block, (qb, kb, vb, jnp.arange(nb)))
    o = jnp.moveaxis(o, 0, 1).reshape(bsz, t, ATT_HEADS * ATT_HEAD_DIM)
    return o @ w_o

def first_inputs(seed: int = 0) -> dict:
    key = jax.random.key(seed)
    ks = jax.random.split(key, 24)
    nrm = jax.random.normal
    f32 = jnp.float32
    x = nrm(ks[0], (BATCH, SEQ, D_MODEL), f32)
    ffn_norm = 1.0 + 0.05 * nrm(ks[1], (DEPTH, 2, D_MODEL), f32)
    ffn_w1 = nrm(ks[2], (DEPTH, 2, D_MODEL, D_FF), f32) * D_MODEL ** -0.5
    ffn_w3 = nrm(ks[3], (DEPTH, 2, D_MODEL, D_FF), f32) * D_MODEL ** -0.5
    ffn_w2 = nrm(ks[4], (DEPTH, 2, D_FF, D_MODEL), f32) * D_FF ** -0.5
    ssm_norm = 1.0 + 0.05 * nrm(ks[5], (N_A_LAYERS, D_MODEL), f32)
    ssm_w_in = nrm(ks[6], (N_A_LAYERS, D_MODEL, SSM_IN_DIM), f32) * D_MODEL ** -0.5
    ssm_conv_w = nrm(ks[7], (N_A_LAYERS, SSM_CONV, SSM_CONV_DIM), f32) * SSM_CONV ** -0.5
    ssm_conv_b = 0.01 * nrm(ks[8], (N_A_LAYERS, SSM_CONV_DIM), f32)
    dt0 = jnp.exp(jax.random.uniform(ks[9], (N_A_LAYERS, SSM_HEADS), f32,
                                     math.log(1e-3), math.log(1e-1)))
    ssm_dt_bias = dt0 + jnp.log(-jnp.expm1(-dt0))
    ssm_a_log = jnp.log(jax.random.uniform(ks[10], (N_A_LAYERS, SSM_HEADS), f32, 1.0, 16.0))
    ssm_d = 1.0 + 0.1 * nrm(ks[11], (N_A_LAYERS, SSM_HEADS), f32)
    ssm_gate_norm = 1.0 + 0.05 * nrm(ks[12], (N_A_LAYERS, SSM_D_INNER), f32)
    ssm_w_out = nrm(ks[13], (N_A_LAYERS, SSM_D_INNER, D_MODEL), f32) * SSM_D_INNER ** -0.5
    kv_norm = 1.0 + 0.05 * nrm(ks[14], (D_MODEL,), f32)
    w_kv = nrm(ks[15], (D_MODEL, 2 * ATT_KV_HEADS * ATT_HEAD_DIM), f32) * D_MODEL ** -0.5
    k_norm = 1.0 + 0.05 * nrm(ks[16], (ATT_HEAD_DIM,), f32)
    attn_norm = 1.0 + 0.05 * nrm(ks[17], (N_B_LAYERS, D_MODEL), f32)
    w_q = nrm(ks[18], (N_B_LAYERS, D_MODEL, ATT_HEADS * ATT_HEAD_DIM), f32) * D_MODEL ** -0.5
    q_norm = 1.0 + 0.05 * nrm(ks[19], (N_B_LAYERS, ATT_HEAD_DIM), f32)
    sinks = 0.5 * nrm(ks[20], (N_B_LAYERS, ATT_HEADS), f32)
    w_o = nrm(ks[21], (N_B_LAYERS, ATT_HEADS * ATT_HEAD_DIM, D_MODEL), f32) * (ATT_HEADS * ATT_HEAD_DIM) ** -0.5
    rel_bias = 0.5 * nrm(ks[22], (REL_BUCKETS, ATT_HEADS), f32)
    return {'x': x, 'ffn_norm': ffn_norm, 'ffn_w1': ffn_w1, 'ffn_w3': ffn_w3, 'ffn_w2': ffn_w2,
            'ssm_norm': ssm_norm, 'ssm_w_in': ssm_w_in, 'ssm_conv_w': ssm_conv_w,
            'ssm_conv_b': ssm_conv_b, 'ssm_dt_bias': ssm_dt_bias, 'ssm_a_log': ssm_a_log,
            'ssm_d': ssm_d, 'ssm_gate_norm': ssm_gate_norm, 'ssm_w_out': ssm_w_out,
            'kv_norm': kv_norm, 'w_kv': w_kv, 'k_norm': k_norm,
            'attn_norm': attn_norm, 'w_q': w_q, 'q_norm': q_norm, 'sinks': sinks, 'w_o': w_o,
            'rel_bias': rel_bias}

def first_block(x, ffn_norm, ffn_w1, ffn_w3, ffn_w2,
              ssm_norm, ssm_w_in, ssm_conv_w, ssm_conv_b, ssm_dt_bias, ssm_a_log,
              ssm_d, ssm_gate_norm, ssm_w_out,
              kv_norm, w_kv, k_norm,
              attn_norm, w_q, q_norm, sinks, w_o,
              rel_bias):
    h = x
    k_shared, v_shared = None, None
    for layer in range(DEPTH):
        h = swiglu_half_step(h, ffn_norm[layer, 0], ffn_w1[layer, 0], ffn_w3[layer, 0], ffn_w2[layer, 0])
        if layer < N_A_LAYERS:
            i = layer
            h = h + mamba2_mixer(rmsnorm(h, ssm_norm[i]), ssm_w_in[i], ssm_conv_w[i], ssm_conv_b[i],
                                 ssm_dt_bias[i], ssm_a_log[i], ssm_d[i], ssm_gate_norm[i], ssm_w_out[i])
        else:
            j = layer - N_A_LAYERS
            h = h + sliding_window_attention(rmsnorm(h, attn_norm[j]), k_shared, v_shared,
                                             w_q[j], q_norm[j], sinks[j], rel_bias, w_o[j])
        h = swiglu_half_step(h, ffn_norm[layer, 1], ffn_w1[layer, 1], ffn_w3[layer, 1], ffn_w2[layer, 1])
        if layer == N_A_LAYERS - 1:
            k_shared, v_shared = shared_kv(h, kv_norm, w_kv, k_norm)
    return h


DEPTH_2 = 1

CHUNK = 64

MLA_HEADS = 8
MLA_Q_RANK = 384
MLA_KV_RANK = 256
MLA_NOPE = 64
MLA_ROPE = 32
MLA_V = 64
MLA_QK = MLA_NOPE + MLA_ROPE
ROPE_THETA = 10000.0
Q_BLOCK = 128

RWKV_HEADS = 8
RWKV_HEAD = 64
RWKV_DIM = RWKV_HEADS * RWKV_HEAD
W_LORA = 64
A_LORA = 64
G_LORA = 128
LN_X_EPS = 64e-5

MIX_WIDTH = MLA_HEADS * MLA_V + RWKV_DIM
MLA_COLS = MLA_Q_RANK + MLA_KV_RANK + MLA_ROPE
RWKV_COLS = 3 * RWKV_DIM + W_LORA + A_LORA + G_LORA
IN_COLS = MLA_COLS + RWKV_COLS
MLA_SPLITS = (MLA_Q_RANK, MLA_Q_RANK + MLA_KV_RANK)
RWKV_SPLITS = (RWKV_DIM, 2 * RWKV_DIM, 3 * RWKV_DIM, 3 * RWKV_DIM + W_LORA, 3 * RWKV_DIM + W_LORA + A_LORA)

PEER_HEADS = 8
N_KEYS = 128
N_EXPERTS = N_KEYS * N_KEYS
PEER_DQ = 256
PEER_DHALF = PEER_DQ // 2
PEER_TOPK = 16
TOK_BLOCK = 128


def rms_norm(x, g, eps=EPS):
    xf = x.astype(jnp.float32)
    y = xf * lax.rsqrt(jnp.mean(xf * xf, axis=-1, keepdims=True) + eps)
    return (y * g.astype(jnp.float32)).astype(x.dtype)

def apply_rope(t, positions):
    half = MLA_ROPE // 2
    inv = ROPE_THETA ** (-jnp.arange(half, dtype=jnp.float32) / half)
    ang = positions.astype(jnp.float32)[..., None] * inv
    cos = jnp.cos(ang)[:, :, None, :]
    sin = jnp.sin(ang)[:, :, None, :]
    tf = t.astype(jnp.float32)
    t1, t2 = tf[..., :half], tf[..., half:]
    out = jnp.concatenate([t1 * cos - t2 * sin, t1 * sin + t2 * cos], axis=-1)
    return out.astype(t.dtype)

def mla_group(p_mla, positions, g_cq, g_ckv, w_uq, w_uk, w_uv, g_qnorm, g_knorm, g_attn_out):
    B, S, _ = p_mla.shape
    c_q, c_kv, k_rope = jnp.split(p_mla, MLA_SPLITS, axis=-1)
    q = (rms_norm(c_q, g_cq) @ w_uq).reshape(B, S, MLA_HEADS, MLA_QK)
    c_kv = rms_norm(c_kv, g_ckv)
    k_nope = (c_kv @ w_uk).reshape(B, S, MLA_HEADS, MLA_NOPE)
    v = (c_kv @ w_uv).reshape(B, S, MLA_HEADS, MLA_V)
    k = jnp.concatenate([k_nope, jnp.broadcast_to(k_rope[:, :, None, :], (B, S, MLA_HEADS, MLA_ROPE))], axis=-1)
    q = rms_norm(q, g_qnorm)
    k = rms_norm(k, g_knorm)
    q = jnp.concatenate([q[..., :MLA_NOPE], apply_rope(q[..., MLA_NOPE:], positions)], axis=-1)
    k = jnp.concatenate([k[..., :MLA_NOPE], apply_rope(k[..., MLA_NOPE:], positions)], axis=-1)
    scale = MLA_QK ** -0.5
    n_blk = S // Q_BLOCK
    q_blocks = q.reshape(B, n_blk, Q_BLOCK, MLA_HEADS, MLA_QK).transpose(1, 0, 2, 3, 4)
    key_chunk = jnp.arange(S) // CHUNK

    def attend(args):
        qb, bi = args
        q_chunk = (bi * Q_BLOCK + jnp.arange(Q_BLOCK)) // CHUNK
        s = jnp.einsum('bqhd,bkhd->bhqk', qb, k).astype(jnp.float32) * scale
        mask = key_chunk[None, :] <= q_chunk[:, None]
        s = jnp.where(mask[None, None], s, -jnp.inf)
        pr = jax.nn.softmax(s, axis=-1).astype(v.dtype)
        return jnp.einsum('bhqk,bkhd->bqhd', pr, v)

    o = lax.map(attend, (q_blocks, jnp.arange(n_blk)))
    o = o.transpose(1, 0, 2, 3, 4).reshape(B, S, MLA_HEADS, MLA_V)
    o = rms_norm(o, g_attn_out.reshape(MLA_HEADS, MLA_V))
    return o.reshape(B, S, MLA_HEADS * MLA_V)

def rwkv7_step(state, inp):
    r_t, w_t, k_t, v_t, kk_t, a_t = inp
    sk = jnp.einsum('bhij,bhj->bhi', state, kk_t)
    state = (state * w_t[:, :, None, :]
             - sk[..., None] * (kk_t * a_t)[:, :, None, :]
             + v_t[..., None] * k_t[:, :, None, :])
    y = jnp.einsum('bhij,bhj->bhi', state, r_t)
    return state, y

def rwkv7_group(p_rwkv, rwkv_mu, w0, w2, a0, a2, g2, k_k, k_a, r_k, ln_x_w, ln_x_b):
    B, S, _ = p_rwkv.shape
    prev = jnp.pad(p_rwkv, ((0, 0), (1, 0), (0, 0)))[:, :S]
    p = p_rwkv + (prev - p_rwkv) * rwkv_mu
    r, k, v, wl, al, gl = jnp.split(p, RWKV_SPLITS, axis=-1)
    w = -jax.nn.softplus(-(w0 + jnp.tanh(wl) @ w2)) - 0.5
    decay = jnp.exp(-jnp.exp(w.astype(jnp.float32)))
    a = jax.nn.sigmoid(a0 + al @ a2)
    g = jax.nn.sigmoid(gl) @ g2
    heads = lambda t: t.astype(jnp.float32).reshape(B, S, RWKV_HEADS, RWKV_HEAD)
    kk = heads(k * k_k)
    kk = kk / jnp.maximum(jnp.sqrt(jnp.sum(kk * kk, axis=-1, keepdims=True)), 1e-12)
    k = k * (1.0 + (a - 1.0) * k_a)
    r_h, k_h, v_h, a_h, w_h = heads(r), heads(k), heads(v), heads(a), heads(decay)
    xs = tuple(jnp.moveaxis(t, 1, 0) for t in (r_h, w_h, k_h, v_h, kk, a_h))
    state0 = jnp.zeros((B, RWKV_HEADS, RWKV_HEAD, RWKV_HEAD), jnp.float32)
    _, y = lax.scan(rwkv7_step, state0, xs)
    y = jnp.moveaxis(y, 0, 1)
    mu = jnp.mean(y, axis=-1, keepdims=True)
    var = jnp.mean(jnp.square(y - mu), axis=-1, keepdims=True)
    y = ((y - mu) * lax.rsqrt(var + LN_X_EPS) * ln_x_w.astype(jnp.float32).reshape(RWKV_HEADS, RWKV_HEAD)
         + ln_x_b.astype(jnp.float32).reshape(RWKV_HEADS, RWKV_HEAD))
    bonus = jnp.sum(r_h * k_h * r_k.astype(jnp.float32), axis=-1, keepdims=True) * v_h
    y = (y + bonus).reshape(B, S, RWKV_DIM).astype(p_rwkv.dtype)
    return y * g

def peer_ffn(h, w_pq, sub_keys, expert_u, expert_v):
    B, S, D = h.shape
    hb_all = h.reshape(B * S // TOK_BLOCK, TOK_BLOCK, D)

    def block(hb):
        q = (hb @ w_pq).reshape(TOK_BLOCK, PEER_HEADS, 2, PEER_DHALF)
        s = jnp.einsum('thpd,hpnd->thpn', q, sub_keys).astype(jnp.float32)
        s1, i1 = lax.top_k(s[:, :, 0], PEER_TOPK)
        s2, i2 = lax.top_k(s[:, :, 1], PEER_TOPK)
        cand_s = (s1[..., :, None] + s2[..., None, :]).reshape(TOK_BLOCK, PEER_HEADS, PEER_TOPK * PEER_TOPK)
        cand_i = (i1[..., :, None] * N_KEYS + i2[..., None, :]).reshape(TOK_BLOCK, PEER_HEADS, PEER_TOPK * PEER_TOPK)
        top_s, pos = lax.top_k(cand_s, PEER_TOPK)
        idx = jnp.take_along_axis(cand_i, pos, axis=-1)
        gate = jax.nn.softmax(top_s, axis=-1).astype(hb.dtype)
        u = expert_u[idx]
        act = jax.nn.gelu(jnp.einsum('thkd,td->thk', u, hb), approximate=False)
        vv = expert_v[idx]
        return jnp.einsum('thk,thkd->td', gate * act, vv)

    out = lax.map(block, hb_all)
    return out.reshape(B, S, D)

def second_inputs(seed: int = 0) -> dict:
    key = jax.random.key(seed)
    ks = iter(jax.random.split(key, 40))
    f32 = jnp.float32
    nrm = lambda shape, scale: jax.random.normal(next(ks), shape, f32) * scale
    gain = lambda shape: 1.0 + 0.02 * jax.random.normal(next(ks), shape, f32)
    L = DEPTH_2
    x = jax.random.normal(next(ks), (BATCH, SEQ, D_MODEL), f32)
    offset = jax.random.randint(next(ks), (BATCH, 1), 0, 64, dtype=jnp.int32) * CHUNK
    positions = offset + jnp.arange(SEQ, dtype=jnp.int32)[None, :]
    return {
        'x': x,
        'positions': positions,
        'g_mix': gain((L, D_MODEL)),
        'w_in': nrm((L, D_MODEL, IN_COLS), D_MODEL ** -0.5),
        'rwkv_mu': jax.random.uniform(next(ks), (L, RWKV_COLS), f32),
        'g_cq': gain((L, MLA_Q_RANK)),
        'g_ckv': gain((L, MLA_KV_RANK)),
        'w_uq': nrm((L, MLA_Q_RANK, MLA_HEADS * MLA_QK), MLA_Q_RANK ** -0.5),
        'w_uk': nrm((L, MLA_KV_RANK, MLA_HEADS * MLA_NOPE), MLA_KV_RANK ** -0.5),
        'w_uv': nrm((L, MLA_KV_RANK, MLA_HEADS * MLA_V), MLA_KV_RANK ** -0.5),
        'g_qnorm': gain((L, MLA_QK)),
        'g_knorm': gain((L, MLA_QK)),
        'g_attn_out': gain((L, MLA_HEADS * MLA_V)),
        'w0': -6.0 + 5.0 * jax.random.uniform(next(ks), (L, RWKV_DIM), f32),
        'w2': nrm((L, W_LORA, RWKV_DIM), 0.1),
        'a0': nrm((L, RWKV_DIM), 0.1),
        'a2': nrm((L, A_LORA, RWKV_DIM), 0.1),
        'g2': nrm((L, G_LORA, RWKV_DIM), G_LORA ** -0.5),
        'k_k': 0.85 + nrm((L, RWKV_DIM), 0.05),
        'k_a': 1.0 + nrm((L, RWKV_DIM), 0.05),
        'r_k': nrm((L, RWKV_HEADS, RWKV_HEAD), 0.1),
        'ln_x_w': gain((L, RWKV_DIM)),
        'ln_x_b': nrm((L, RWKV_DIM), 0.02),
        'w_o': nrm((L, MIX_WIDTH, D_MODEL), MIX_WIDTH ** -0.5),
        'g_ffn': gain((L, D_MODEL)),
        'w_pq': nrm((L, D_MODEL, PEER_HEADS * PEER_DQ), D_MODEL ** -0.5),
        'sub_keys': nrm((L, PEER_HEADS, 2, N_KEYS, PEER_DHALF), PEER_DHALF ** -0.5),
        'expert_u': nrm((L, N_EXPERTS, D_MODEL), D_MODEL ** -0.5),
        'expert_v': nrm((L, N_EXPERTS, D_MODEL), PEER_HEADS ** -0.5),
    }

def second_block(x, positions, g_mix, w_in, rwkv_mu, g_cq, g_ckv, w_uq, w_uk, w_uv, g_qnorm, g_knorm,
              g_attn_out, w0, w2, a0, a2, g2, k_k, k_a, r_k, ln_x_w, ln_x_b, w_o, g_ffn, w_pq,
              sub_keys, expert_u, expert_v):
    for l in range(DEPTH_2):
        h = rms_norm(x, g_mix[l])
        p = h @ w_in[l]
        y_a = mla_group(p[..., :MLA_COLS], positions, g_cq[l], g_ckv[l], w_uq[l], w_uk[l], w_uv[l],
                        g_qnorm[l], g_knorm[l], g_attn_out[l])
        y_b = rwkv7_group(p[..., MLA_COLS:], rwkv_mu[l], w0[l], w2[l], a0[l], a2[l], g2[l], k_k[l], k_a[l],
                          r_k[l], ln_x_w[l], ln_x_b[l])
        x = x + jnp.concatenate([y_a, y_b], axis=-1) @ w_o[l]
        x = x + peer_ffn(rms_norm(x, g_ffn[l]), w_pq[l], sub_keys[l], expert_u[l], expert_v[l])
    return x


def setup_inputs(seed=0):
    out = dict(first_inputs(seed))
    for name, value in second_inputs(seed + 1).items():
        if name != "x":
            out[name + "_2"] = value
    return out


def reference(
    x, ffn_norm, ffn_w1, ffn_w3, ffn_w2, ssm_norm, ssm_w_in, ssm_conv_w, ssm_conv_b,
    ssm_dt_bias, ssm_a_log, ssm_d, ssm_gate_norm, ssm_w_out, kv_norm, w_kv, k_norm, attn_norm,
    w_q, q_norm, sinks, w_o, rel_bias, positions_2, g_mix_2, w_in_2, rwkv_mu_2, g_cq_2, g_ckv_2,
    w_uq_2, w_uk_2, w_uv_2, g_qnorm_2, g_knorm_2, g_attn_out_2, w0_2, w2_2, a0_2, a2_2, g2_2,
    k_k_2, k_a_2, r_k_2, ln_x_w_2, ln_x_b_2, w_o_2, g_ffn_2, w_pq_2, sub_keys_2, expert_u_2,
    expert_v_2,
):
    x = first_block(
        x, ffn_norm, ffn_w1, ffn_w3, ffn_w2, ssm_norm, ssm_w_in, ssm_conv_w, ssm_conv_b,
        ssm_dt_bias, ssm_a_log, ssm_d, ssm_gate_norm, ssm_w_out, kv_norm, w_kv, k_norm,
        attn_norm, w_q, q_norm, sinks, w_o, rel_bias,
    )
    return second_block(
        x, positions_2, g_mix_2, w_in_2, rwkv_mu_2, g_cq_2, g_ckv_2, w_uq_2, w_uk_2, w_uv_2,
        g_qnorm_2, g_knorm_2, g_attn_out_2, w0_2, w2_2, a0_2, a2_2, g2_2, k_k_2, k_a_2, r_k_2,
        ln_x_w_2, ln_x_b_2, w_o_2, g_ffn_2, w_pq_2, sub_keys_2, expert_u_2, expert_v_2,
    )


_drawn_inputs = setup_inputs


def setup_inputs(seed=0):
    import zlib

    import numpy as np

    out = dict(_drawn_inputs(seed))
    spreads = {}
    factors = {'ssm_conv_b': 3.432,
     'kv_norm': 2.757,
     'k_norm': 4.32,
     'attn_norm': 4.977,
     'q_norm': 4.944,
     'sinks': 4.679,
     'g_mix_2': 3.111,
     'g_cq_2': 6.339,
     'g_ckv_2': 3.778,
     'g_qnorm_2': 6.551,
     'g_knorm_2': 5.996,
     'g_attn_out_2': 29.693,
     'w2_2': 3.633,
     'a0_2': 4.321,
     'k_k_2': 25.031,
     'k_a_2': 3.288,
     'ln_x_w_2': 53.821,
     'ln_x_b_2': 56.321,
     'g_ffn_2': 23.89}
    for name, (base, spread) in spreads.items():
        noise = np.random.default_rng([zlib.crc32(name.encode()), seed]).standard_normal(out[name].shape)
        drawn = base * np.exp(spread * noise) if base else spread * noise
        out[name] = __import__('jax').numpy.asarray(drawn.astype(out[name].dtype))
    for name, factor in factors.items():
        out[name] = (out[name] * factor).astype(out[name].dtype)
    return out
```

```python
import math
from contextlib import ExitStack

import numpy as np

import concourse.bass as bass
from concourse import mybir

F32 = mybir.dt.float32
BF16 = mybir.dt.bfloat16
I32 = mybir.dt.int32
U32 = mybir.dt.uint32
ALU = mybir.AluOpType
ACT = mybir.ActivationFunctionType
AX = mybir.AxisListType

P = 128
T = 256
TT = T // P
D = 1024
DC = D // P
FF = 2816
FC = FF // P
EPS = 1e-6
NEG = -1e30
GROUPS = 4
GHEADS = 8
HD = 64
GI = GHEADS * HD
CONV = 4
WINDOW = 128
BUCKETS = 32
MAX_DIST = WINDOW
MLA_Q, MLA_KV, ROPE, NOPE = 384, 256, 32, 64
QK = ROPE + NOPE
THETA = 10000.0
LN_EPS = 64e-5
RC = 4
CH = T // RC
PH = 8
TOPK = 16
NKEYS = 128
SLOTS = 8



def layout(items):
    at, out = 0, {}
    for name, n in items:
        out[name] = (at, n)
        at += n
    return out, at


CONSTS, N_CONSTS = layout([
    ("ident", P), ("ones", P), ("blk64", P), ("causal", 384), ("mla_mask", 384),
    ("up_strict", CH), ("up_incl", CH), ("low_strict", CH),
    ("u16", P), ("l16", P), ("u32", P), ("l32", P), ("l64", P),
    ("iota", P), ("rot", QK), ("onehot", 384), ("outside", 384), ("half", 1),
    ("inv_freq", 1), ("is_rope", 1), ("not_rope", 1),
])


def constants():
    c = np.zeros((P, N_CONSTS), np.float32)

    def put(name, a):
        at, n = CONSTS[name]
        a = np.asarray(a, np.float32).reshape(a.shape[0], n)
        c[:a.shape[0], at:at + n] = a

    i = np.arange(P)
    put("ident", np.eye(P))
    put("ones", np.ones((P, P)))
    same = (i[:, None] // HD) == (i[None, :] // HD)
    put("blk64", same)
    late = i[None, :] >= i[:, None]
    put("causal", np.concatenate([late, np.ones((P, P)), late], 1))
    tok = np.arange(T)
    mask = np.stack([np.where(tok[None, :] // 64 <= (b * P + i)[:, None] // 64, 0, NEG) for b in range(TT)], 1)
    put("mla_mask", np.concatenate([mask[:, 0, 0:P], mask[:, 1, :]], 1))
    r, t = (i % CH)[:, None], np.arange(CH)[None, :]
    put("up_strict", r < t)
    put("up_incl", r <= t)
    put("low_strict", r > t)
    a, b = i[:, None], i[None, :]
    for n, lo in ((16, 1), (32, 16), (64, 32)):
        level = (a // n == b // n) & ((a // lo != b // lo) if lo > 1 else True) & (a < b)
        put(f"l{n}", level.T)
        if n < 64:
            put(f"u{n}", level)
    put("iota", np.tile(np.arange(P), (P, 1)))
    half = ROPE // 2
    rot = np.zeros((QK, QK))
    for j in range(half):
        rot[NOPE + half + j, NOPE + j] = -1
        rot[NOPE + j, NOPE + half + j] = 1
    put("rot", rot)
    y = np.arange(384)
    dist = 255 - y
    inside = (dist >= 0) & (dist < WINDOW)
    exact = BUCKETS // 2
    nf = np.maximum(dist, 1).astype(np.float32)
    large = exact + (np.log(nf / np.float32(exact)) / np.float32(math.log(MAX_DIST / exact))
                     * np.float32(BUCKETS - exact)).astype(np.int32)
    bucket = np.where(np.maximum(dist, 0) < exact, np.maximum(dist, 0), np.minimum(large, BUCKETS - 1))
    put("onehot", (np.arange(BUCKETS)[:, None] == bucket[None, :]) & inside[None, :])
    put("outside", np.tile(np.where(inside, 0, NEG), (P, 1)))
    put("half", np.full((P, 1), math.pi / 2))
    inv = (np.float32(THETA) ** (-np.arange(half, dtype=np.float32) / np.float32(half))).astype(np.float32)
    put("inv_freq", np.concatenate([np.zeros(NOPE), inv, inv])[:, None])
    put("is_rope", (np.arange(QK) >= NOPE)[:, None])
    put("not_rope", (np.arange(QK) < NOPE)[:, None])
    return c


VECS, N_VECS = layout([
    ("g_ffn0", DC), ("g_ffn1", DC), ("g_ffn2", DC), ("g_ffn3", DC), ("g_ssm", DC), ("g_kv", DC),
    ("g_attn", DC), ("g_mix", DC), ("g_peer", DC),
    ("conv_w", GROUPS * 6 * CONV), ("conv_b", GROUPS * 6), ("d_skip", GROUPS * 4), ("g_gate", GROUPS * 4),
    ("dt_bias", 1), ("a_log", 1), ("k_norm", 1), ("q_norm", 1), ("sinks", 16),
    ("g_cq", 3), ("g_ckv", 2), ("g_qnorm", 1), ("g_knorm", 1), ("g_out", 4),
    ("mu", 14), ("w0", 4), ("a0", 4), ("k_k", 4), ("k_a", 4), ("r_k", 4), ("lnw", 4), ("lnb", 4),
])


def tiles(w, width=P):
    k, n = w.shape[0] // P, w.shape[1] // width
    return w.reshape(k, P, n, width).transpose(2, 1, 0, 3).reshape(n, P, k * width)


RING_PLAN = {
    "ffn0": (FC // 2, [1] * 6 + [0] * 2),
    "dt": (1, [1] + [0] * 7),
    "ssm": (GROUPS, [2] * 7 + [0]),
    "ffn1": (FC // 2, [1] * 6 + [0] * 2),
    "kv": (1, [1] * 3 + [0] * 5),
    "ffn2": (FC // 2, [1] * 6 + [0] * 2),
    "attn": (4, [1] * 4 + [0] * 4),
    "ffn3": (FC // 2, [1] * 6 + [0] * 2),
    "rwkv": (2, [1] * 7 + [0]),
    "rwkv_out": (1, [1] * 4 + [0] * 4),
    "mla": (1, [1] * 6 + [0] * 2),
    "mla_heads": (4, [0] * 6 + [1] * 2),
    "route": (PH, [1, 1] + [0] * 6),
    "peer": (NKEYS // 4, [1] * 8),
}


RING_OF = {"ssm": ("dt", "ssm"), "rwkv": ("rwkv", "rwkv_out"), "mla": ("mla", "mla_heads"), "mix": (),
           "peer": ("route", "peer")}
STAGES = ["ffn0", "ssm", "ffn1", "kv", "ffn2", "attn", "ffn3", "rwkv", "mla", "mix", "peer"]


def program(nc, io, stages=STAGES):
    norm_no = {s: n for n, s in enumerate([s for s in stages if s not in ("mla", "mix")])}
    sums = [s for s in stages if s not in ("kv", "rwkv", "mla")]
    upd = {s: len([x for x in stages[:stages.index(s)] if x in sums]) for s in stages}
    ffn_no = {s: n for n, s in enumerate([s for s in stages if s.startswith("ffn")])}
    ring_order = [r for s in stages for r in RING_OF.get(s, (s,))]

    def use(stage, slot, i=0, nth=0):
        before = sum(RING_PLAN[r][0] * RING_PLAN[r][1][slot] for r in ring_order[:ring_order.index(stage)])
        return before + nth + i * RING_PLAN[stage][1][slot]

    ctx = ExitStack()
    sems = {}

    def S(name):
        if name not in sems:
            sems[name] = ctx.enter_context(nc.semaphore(name))
        return sems[name]

    def sb(name, shape, dt=F32):
        return ctx.enter_context(nc.sbuf_tensor(name, shape, dt))

    with ctx:
        con = sb("con", [P, N_CONSTS])
        vec = sb("vec", [P, N_VECS])
        h = sb("h", [P, TT, D])
        u_t = sb("u_t", [P, DC, T])
        ring = [sb(f"ring{s}", [P, D]) for s in range(SLOTS)]
        zeros = sb("zeros", [P, 512], BF16)
        stat = sb("stat", [P, 16])
        credit = sb("credit", [P, 1])
        arena = sb("arena", [P, 32768])
        bank = [ctx.enter_context(nc.psum_tensor(f"bank{i}", [P, 512], F32)) for i in range(8)]
        ACC = bank[0:4]
        UP = bank[4:6]
        TP = bank[6:8]
        ROT = bank[4:8]

        def C(name, a=0, b=None):
            at, n = CONSTS[name]
            return con[:, at + a:at + (n if b is None else b)]

        def V(name, a=0, b=None):
            at, n = VECS[name]
            return vec[:, at + a:at + (n if b is None else b)]

        def VD(name, start, n=1):
            return vec[:, bass.ds(VECS[name][0] + start, n)]

        def area(at, *shape):
            n = int(np.prod(shape))
            a = arena[:, at:at + n]
            if len(shape) == 2:
                a = a.rearrange("p (a b) -> p a b", a=shape[0])
            if len(shape) == 3:
                a = a.rearrange("p (a b c) -> p a b c", a=shape[0], b=shape[1])
            return a

        def spread(col, n):
            return col.unsqueeze(2).broadcast_to([col.shape[0], col.shape[1], n])

        full = [S(f"slot_full{s}") for s in range(SLOTS)]
        freed = [S(f"slot_freed{s}") for s in range(SLOTS)]

        def load(sp, slot, src, stage, i=0, nth=0):
            sp.wait_ge(freed[slot], use(stage, slot, i, nth) + 1)
            sp.dma_start(ring[slot][:, 0:src.shape[-1]], src).then_inc(full[slot], 16)

        def arrived(pe, slot, stage, i=0, nth=0):
            pe.wait_ge(full[slot], (use(stage, slot, i, nth) + 1) * 16)

        def multiplied(eng, slot, stage, i=0, nth=0):
            eng.wait_ge(freed[slot], use(stage, slot, i, nth) + 2)

        def project(pe, out, slot, width=P):
            for c in range(DC):
                mm = pe.matmul(out, ring[slot][:, c * width:(c + 1) * width], u_t[:, c, :],
                               start=(c == 0), stop=(c == DC - 1))
            return mm

        def close_into(pe, left, right, last=False):
            for q in range(4):
                mm = pe.matmul(ACC[q][:, :], left[:, (q // 2) * P:(q // 2 + 1) * P],
                               right[:, (q % 2) * 512:(q % 2 + 1) * 512],
                               start=False, stop=last, skip_group_check=True)
            return mm

        def clear_acc(pe, updates):
            pe.wait_ge(S("h_updated"), 4 * updates + 1)
            for q in range(4):
                pe.matmul(ACC[q][:, :], zeros[:, 0:P], zeros[:, :], start=True, stop=False,
                          skip_group_check=True)

        norm_square = area(0, 2, D)
        norm_u = area(2 * D, 2, D)

        def norm_scalar(act, m, updates):
            act.wait_ge(S("h_loaded"), 16)
            act.wait_ge(S("in_loaded"), 32)
            act.wait_ge(S("h_updated"), 4 * updates + 1)
            for tt in range(TT):
                act.activation(norm_square[:, tt, :], h[:, tt, :], ACT.Square, accum_out=stat[:, tt:tt + 1])
            act.drain()
            act.activation(stat[:, 2:4], stat[:, 0:2], ACT.Sqrt, scale=1.0 / D,
                           bias=stat[:, 14:15]).then_inc(S("norm_root"), 1)

        def norm_vector(dve, m, gain):
            dve.wait_ge(S("norm_root"), m + 1)
            dve.reciprocal(stat[:, 4:6], stat[:, 2:4])
            dve.drain()
            for tt in range(TT):
                dve.tensor_scalar(norm_u[:, tt, :], h[:, tt, :], stat[:, 4 + tt:5 + tt], None,
                                  ALU.mult).then_inc(S("norm_rows"), 1)
            for q in range(4):
                tt, half = q // 2, q % 2
                dve.wait_ge(S("norm_turned"), 4 * m + q + 1)
                dve.tensor_tensor(u_t[:, 4 * half:4 * half + 4, tt * P:(tt + 1) * P],
                                  TP[q % 2][:, :].rearrange("p (c t) -> p c t", c=4),
                                  spread(V(gain, 4 * half, 4 * half + 4), P), ALU.mult).then_inc(S("u_ready"), 1)

        def norm_tensor(pe, m):
            for q in range(4):
                tt, half = q // 2, q % 2
                pe.wait_ge(S("norm_rows"), 2 * m + tt + 1)
                if q >= 2:
                    pe.wait_ge(S("u_ready"), 4 * m + q - 1)
                for c in range(4):
                    at = (4 * half + c) * P
                    mm = pe.transpose(TP[q % 2][:, c * P:(c + 1) * P], norm_u[:, tt, at:at + P], C("ident"))
                mm.then_inc(S("norm_turned"), 1)
            pe.wait_ge(S("u_ready"), 4 * m + 4)

        def update_h(dve, scale):
            for q in range(4):
                part = h[:, q // 2, (q % 2) * 512:(q % 2 + 1) * 512]
                dve.scalar_tensor_tensor(part, ACC[q][:, :], scale, part, ALU.mult,
                                         ALU.add).then_inc(S("h_updated"), 1)

        silu_buf = area(4 * D, 2, T)
        hid_buf = area(4 * D + 2 * T, 2, T)

        def ffn_sync(sp, k):
            with sp.Fori(0, FC // 2) as i:
                for b in range(2):
                    for n, w in enumerate(("w1", "w3", "w2")):
                        load(sp, 3 * b + n, io[w][k, bass.ds(2 * i + b, 1), :, :], f"ffn{k}", i)

        def ffn_tensor(pe, k, updates):
            stage = f"ffn{k}"
            base = FC * ffn_no[stage]

            def up(b, i):
                pe.wait_ge(S("hid_ready"), base + 2 * i + b + 1)
                for n in range(2):
                    arrived(pe, 3 * b + n, stage, i)
                    project(pe, UP[b][:, n * T:(n + 1) * T], 3 * b + n).then_inc(freed[3 * b + n], 1)

            def down(b, i, last=False):
                arrived(pe, 3 * b + 2, stage, i)
                pe.wait_ge(S("hid_ready"), base + 2 * i + b + 3)
                close_into(pe, hid_buf[:, b, :], ring[3 * b + 2], last).then_inc(freed[3 * b + 2], 1)

            clear_acc(pe, updates)
            up(0, 0)
            with pe.Fori(0, FC // 2 - 1) as i:
                up(1, i)
                down(0, i)
                up(0, i + 1)
                down(1, i)
            n = FC // 2 - 1
            up(1, n)
            down(0, n)
            down(1, n, last=True)

        def ffn_scalar(act, k):
            with act.Fori(0, FC // 2) as i:
                for b in range(2):
                    multiplied(act, 3 * b + 1, f"ffn{k}", i)
                    act.activation(silu_buf[:, b, :], UP[b][:, 0:T], ACT.Silu).then_inc(S("silu_ready"), 1)

        def ffn_vector(dve, k):
            base = FC * ffn_no[f"ffn{k}"]
            with dve.Fori(0, FC // 2) as i:
                for b in range(2):
                    dve.wait_ge(S("silu_ready"), base + 2 * i + b + 1)
                    dve.wait_ge(freed[3 * b + 2], use(f"ffn{k}", 3 * b + 2, i) + 1)
                    dve.tensor_tensor(hid_buf[:, b, :], silu_buf[:, b, :], UP[b][:, T:2 * T],
                                      ALU.mult).then_inc(S("hid_ready"), 1)
            multiplied(dve, 5, f"ffn{k}", FC // 2 - 1)
            update_h(dve, 0.5)

        GAIN = {"ffn0": "g_ffn0", "ssm": "g_ssm", "ffn1": "g_ffn1", "kv": "g_kv", "ffn2": "g_ffn2", "attn": "g_attn",
                "ffn3": "g_ffn3", "rwkv": "g_mix", "peer": "g_peer"}
        SYNC, POOL, SCALAR, VECTOR, TENSOR = {}, {}, {}, {}, {}

        x_pad = area(4096, 6, 260)
        conv = area(5696, 6, T)
        z_act = area(7232, 4, T)
        xdt = area(8256, TT, GI)
        cb = area(9280, 384)
        decay = area(9664, GHEADS, 384)
        y_grp = area(12736, 4, T)
        y_sq = area(13760, 4, T)
        y_out = area(14784, 4, T)
        y_root = area(15808, 2, T)
        acum_all = area(16384, 4 * GHEADS, T)
        dt_work = area(24576, 5, T)
        dt_cols = area(25856, 4, 32)
        acum_dram = nc.dram_tensor("acum_dram", (32, T), F32, kind="Internal").ap()
        H32 = slice(0, 32)

        def ssm_sync(sp):
            load(sp, 0, io["ssm_dt"], "dt")
            sp.wait_ge(S("acum_ready"), 1)
            sp.dma_start(acum_dram, dt_work[H32, 4, :]).then_inc(S("acum_stored"), 16)
            sp.wait_ge(S("acum_stored"), 16)
            sp.dma_start(acum_all[:, :, :], acum_dram.unsqueeze(0).broadcast_to([P, 32, T])).then_inc(S("acum_spread"), 16)
            with sp.Fori(0, GROUPS) as i:
                for n in range(14):
                    src = io["ssm_in"][bass.ds(i, 1), n, :, :] if n < 10 else io["ssm_out"][bass.ds(i, 1), n - 10, :, :]
                    load(sp, n % 7, src, "ssm", i, n // 7)

        def ssm_tensor(pe):
            arrived(pe, 0, "dt")
            project(pe, UP[0][H32, 0:T], 0, 32).then_inc(freed[0], 1)
            clear_acc(pe, upd["ssm"])
            pe.wait_ge(S("acum_ready"), 1)
            for n in range(4):
                src = dt_work[H32, 4 if n < 2 else 2, (n % 2) * P:(n % 2 + 1) * P]
                mm = pe.transpose(TP[0][:, n * 32:(n + 1) * 32], src, C("ident", 0, 32)[H32, :])
            mm.then_inc(S("dt_turned"), 1)
            pe.wait_ge(S("dt_cols_ready"), 1)
            with pe.Fori(0, GROUPS) as i:
                pe.wait_ge(S("y_taken"), 4 * i + 1)
                for n in range(10):
                    arrived(pe, n % 7, "ssm", i, n // 7)
                    pe.wait_ge(S("ssm_evicted"), 10 * i + n + 1)
                    project(pe, ROT[n % 4][:, 0:T], n % 7).then_inc(freed[n % 7], 1)
                pe.wait_ge(S("ssm_evicted"), 10 * i + 14)
                pe.wait_ge(S("conv_act"), 6 * i + 6)
                for tt in range(TT):
                    for k in range(4):
                        mm = pe.transpose(TP[tt][:, k * P:(k + 1) * P], conv[:, 2 + k, tt * P:(tt + 1) * P], C("ident"))
                    mm.then_inc(S("x_turned"), 1)
                pe.wait_ge(S("xdt_ready"), 2 * i + 1)
                pe.matmul(TP[0][:, 0:T], conv[:, 0, 0:P], conv[:, 1, :], start=True, stop=True)
                pe.matmul(TP[0][:, T:384], conv[:, 0, P:T], conv[:, 1, P:T], start=True,
                          stop=True).then_inc(S("cb_done"), 1)
                pe.wait_ge(S("xdt_ready"), 2 * i + 2)
                for r in range(GHEADS):
                    pe.wait_ge(S("scores_ready"), 2 * i + r // 4 + 1)
                    k, a = r // 2, (r % 2) * HD
                    out = ROT[k][a:a + HD, 0:T]
                    pe.matmul(out, xdt[:, 0, r * HD:(r + 1) * HD], decay[:, r, 0:T], start=True, stop=False,
                              skip_group_check=True)
                    mm = pe.matmul(out[:, P:T], xdt[:, 1, r * HD:(r + 1) * HD], decay[:, r, T:384], start=False,
                                   stop=True, skip_group_check=True)
                    if r % 2:
                        mm.then_inc(S("y_done"), 1)
                pe.wait_ge(S("y_squared"), i + 1)
                for k in range(4):
                    mm = pe.matmul(TP[1][:, 0:T], C("ones"), y_sq[:, k, :], start=(k == 0), stop=(k == 3))
                mm.then_inc(S("y_summed"), 1)
                for k in range(4):
                    arrived(pe, 3 + k, "ssm", i, 1)
                    pe.wait_ge(S("y_normed"), 4 * i + k + 1)
                    close_into(pe, y_out[:, k, :], ring[3 + k]).then_inc(freed[3 + k], 1)

        def ssm_scalar(act):
            act.wait_ge(S("dt_raw"), 1)
            act.activation(dt_work[H32, 1, :], dt_work[H32, 0, :], ACT.Abs)
            act.drain()
            act.activation(dt_work[H32, 1, :], dt_work[H32, 1, :], ACT.Exp, scale=-1.0)
            act.activation(stat[H32, 6:7], V("a_log")[H32, :], ACT.Exp)
            act.drain()
            act.activation(dt_work[H32, 1, :], dt_work[H32, 1, :], ACT.Ln, bias=C("ones", 0, 1)[H32, :]).then_inc(S("dt_log"), 1)
            act.wait_ge(S("dt_cols_ready"), 1)
            with act.Fori(0, GROUPS) as i:
                for n in range(10):
                    multiplied(act, n % 7, "ssm", i, n // 7)
                    src = ROT[n % 4][:, 0:T]
                    if n < 6:
                        act.activation(x_pad[:, n, CONV - 1:CONV - 1 + T], src, ACT.Copy).then_inc(S("ssm_evicted"), 1)
                    else:
                        act.activation(z_act[:, n - 6, :], src, ACT.Silu).then_inc(S("ssm_evicted"), 1)
                for n in range(6):
                    act.wait_ge(S("conv_done"), 6 * i + n + 1)
                    act.activation(conv[:, n, :], conv[:, n, :], ACT.Silu).then_inc(S("conv_act"), 1)
                for b in range(2):
                    act.wait_ge(S("decay_ready"), 2 * i + b + 1)
                    part = decay[:, 4 * b:4 * b + 4, :]
                    act.activation(part, part, ACT.Exp).then_inc(S("decay_exp"), 1)
                act.wait_ge(S("y_gated"), i + 1)
                act.activation(y_sq[:, :, :], y_grp[:, :, :], ACT.Square).then_inc(S("y_squared"), 1)
                act.wait_ge(S("y_summed"), i + 1)
                act.activation(y_root[:, 0, :], TP[1][:, 0:T], ACT.Sqrt, scale=1.0 / GI,
                               bias=stat[:, 14:15]).then_inc(S("y_rooted"), 1)

        def ssm_vector(dve):
            dve.memset(x_pad[:, :, 0:CONV - 1], 0.0)
            dve.memset(dt_work[H32, 3, :], 1.0)
            multiplied(dve, 0, "dt")
            dve.tensor_scalar(dt_work[H32, 0, :], UP[0][H32, 0:T], V("dt_bias")[H32, :], None,
                              ALU.add).then_inc(S("dt_raw"), 1)
            dve.drain()
            dve.tensor_scalar(dt_work[H32, 2, :], dt_work[H32, 0, :], 0.0, None, ALU.max)
            dve.wait_ge(S("dt_log"), 1)
            dve.drain()
            dve.tensor_tensor(dt_work[H32, 2, :], dt_work[H32, 2, :], dt_work[H32, 1, :], ALU.add)
            dve.drain()
            dve.tensor_scalar(dt_work[H32, 0, :], dt_work[H32, 2, :], stat[H32, 6:7], -1.0, ALU.mult, ALU.mult)
            dve.drain()
            dve.tensor_tensor_scan(dt_work[H32, 4, :], dt_work[H32, 3, :], dt_work[H32, 0, :], 0.0, ALU.mult,
                                   ALU.add).then_inc(S("acum_ready"), 1)
            dve.wait_ge(S("dt_turned"), 1)
            dve.tensor_copy(dt_cols[:, :, :], TP[0][:, 0:P].rearrange("p (a b) -> p a b", a=4)).then_inc(S("dt_cols_ready"), 1)
            dve.drain()
            dve.wait_ge(S("acum_spread"), 16)
            with dve.Fori(0, GROUPS) as i:
                for r in range(GHEADS):
                    row = acum_all[:, bass.ds(GHEADS * i + r, 1), :]
                    for tt in range(TT):
                        last = dve.tensor_scalar(decay[:, r:r + 1, 0:T] if tt == 0 else decay[:, r:r + 1, T:384],
                                                 row if tt == 0 else acum_all[:, bass.ds(GHEADS * i + r, 1), P:T],
                                                 dt_cols[:, tt, bass.ds(GHEADS * i + r, 1)], 0.0,
                                                 ALU.subtract, ALU.min)
                    if r % 4 == 3:
                        last.then_inc(S("decay_ready"), 1)
                for tiles_of in (range(0, 2), range(2, 6)):
                    for tap in range(CONV):
                        for n in tiles_of:
                            col = (i * 6 + n) * CONV + tap
                            if tap == 0:
                                dve.wait_ge(S("ssm_evicted"), 10 * i + n + 5)
                                dve.tensor_scalar(conv[:, n, :], x_pad[:, n, 0:T], VD("conv_w", col),
                                                  VD("conv_b", i * 6 + n), ALU.mult, ALU.add)
                            else:
                                ins = dve.scalar_tensor_tensor(conv[:, n, :], x_pad[:, n, tap:tap + T],
                                                               VD("conv_w", col), conv[:, n, :], ALU.mult, ALU.add)
                                if tap == CONV - 1:
                                    ins.then_inc(S("conv_done"), 1)
                        dve.drain()
                for tt in range(TT):
                    dve.wait_ge(S("x_turned"), 2 * i + tt + 1)
                    dt_of = dt_cols[:, 2 + tt, bass.ds(GHEADS * i, GHEADS)]
                    dve.tensor_tensor(xdt[:, tt, :].rearrange("p (r q) -> p r q", r=GHEADS),
                                      TP[tt][:, :].rearrange("p (r q) -> p r q", r=GHEADS),
                                      spread(dt_of, HD), ALU.mult).then_inc(S("xdt_ready"), 1)
                dve.wait_ge(S("cb_done"), i + 1)
                dve.tensor_tensor(cb[:, :], TP[0][:, 0:384], C("causal"), ALU.mult)
                dve.drain()
                for b in range(2):
                    dve.wait_ge(S("decay_exp"), 2 * i + b + 1)
                    part = decay[:, 4 * b:4 * b + 4, :]
                    dve.tensor_tensor(part, part, cb.unsqueeze(1).broadcast_to([P, 4, 384]),
                                      ALU.mult).then_inc(S("scores_ready"), 1)
                for k in range(4):
                    dve.wait_ge(S("y_done"), 4 * i + k + 1)
                    dve.scalar_tensor_tensor(y_grp[:, k, :], conv[:, 2 + k, :], VD("d_skip", 4 * i + k),
                                             ROT[k][:, 0:T], ALU.mult,
                                             ALU.add).then_inc(S("y_taken"), 1)
                dve.drain()
                dve.wait_ge(S("ssm_evicted"), 10 * i + 14)
                dve.tensor_tensor(y_grp[:, :, :], y_grp[:, :, :], z_act[:, :, :], ALU.mult).then_inc(S("y_gated"), 1)
                dve.wait_ge(S("y_rooted"), i + 1)
                dve.reciprocal(y_root[:, 1, :], y_root[:, 0, :])
                dve.drain()
                for k in range(4):
                    dve.scalar_tensor_tensor(y_out[:, k, :], y_grp[:, k, :], VD("g_gate", 4 * i + k),
                                             y_root[:, 1, :], ALU.mult, ALU.mult).then_inc(S("y_normed"), 1)
            multiplied(dve, 6, "ssm", GROUPS - 1, 1)
            update_h(dve, 1.0)

        SYNC["ssm"], TENSOR["ssm"], SCALAR["ssm"], VECTOR["ssm"] = ssm_sync, ssm_tensor, ssm_scalar, ssm_vector

        k_t = area(5200, 2, T)
        v_rows = area(5712, TT, P)
        k_sq = area(5968, 2, T)
        k_root = area(6480, 2, 2, T)
        rel = area(7504, 16)
        bias_line = area(7520, 384)
        bias_all = area(8192, 16, 384)
        line_dram = nc.dram_tensor("line_dram", (16, 384), F32, kind="Internal").ap()
        bias_dram = nc.dram_tensor("bias_dram", (16, P * 384), F32, kind="Internal").ap()

        def kv_sync(sp):
            sp.wait_ge(S("u_ready"), 4 * norm_no["kv"] + 1)
            sp.dma_start(rel[0:BUCKETS, :], io["rel_bias"]).then_inc(S("rel_loaded"), 16)
            for n in range(3):
                load(sp, n, io["w_kv"][n, :, :], "kv")
            sp.wait_ge(S("line_ready"), 1)
            sp.dma_start(line_dram, bias_line[0:16, :]).then_inc(S("line_stored"), 16)
            sp.wait_ge(S("line_stored"), 16)
            sp.dma_start(bias_all[:, :, :], line_dram.unsqueeze(0).broadcast_to([P, 16, 384])).then_inc(S("line_spread"), 16)
            sp.wait_ge(S("line_spread"), 16)
            sp.dma_start(bias_dram.rearrange("h (p y) -> p h y", p=P), bias_all[:, :, :]).then_inc(S("bias_stored"), 16)

        def kv_tensor(pe):
            for n in range(2):
                arrived(pe, n, "kv")
                project(pe, ROT[n][:, 0:T], n).then_inc(freed[n], 1)
            arrived(pe, 2, "kv")
            for tt in range(TT):
                for c in range(DC):
                    mm = pe.matmul(ROT[2][:, tt * P:(tt + 1) * P], u_t[:, c, tt * P:(tt + 1) * P],
                                   ring[2][:, c * P:(c + 1) * P], start=(c == 0), stop=(c == DC - 1))
            mm.then_inc(freed[2], 1)
            pe.wait_ge(S("rel_loaded"), 16)
            pe.matmul(ACC[0][0:16, 0:384], rel[0:BUCKETS, :], C("onehot")[0:BUCKETS, :], start=True,
                      stop=True).then_inc(S("line_done"), 1)
            pe.wait_ge(S("k_squared"), 2)
            pe.matmul(ROT[3][:, :], C("blk64"), k_sq.rearrange("p a b -> p (a b)"), start=True,
                      stop=True).then_inc(S("k_summed"), 1)

        def kv_scalar(act):
            for n in range(2):
                multiplied(act, n, "kv")
                act.activation(k_sq[:, n, :], ROT[n][:, 0:T], ACT.Square).then_inc(S("k_squared"), 1)
            act.wait_ge(S("k_summed"), 1)
            act.activation(k_root[:, 0, :, :], ROT[3][:, :].rearrange("p (a b) -> p a b", a=2), ACT.Sqrt,
                           scale=1.0 / HD, bias=stat[:, 14:15]).then_inc(S("k_rooted"), 1)

        def kv_vector(dve):
            dve.wait_ge(S("line_done"), 1)
            dve.tensor_tensor(bias_line[0:16, :], ACC[0][0:16, 0:384], C("outside")[0:16, :],
                              ALU.add).then_inc(S("line_ready"), 1)
            multiplied(dve, 2, "kv")
            dve.tensor_copy(v_rows[:, :, :], ROT[2][:, 0:T].rearrange("p (a b) -> p a b", a=TT))
            dve.wait_ge(S("k_rooted"), 1)
            dve.reciprocal(k_root[:, 1, :, :], k_root[:, 0, :, :])
            dve.drain()
            for n in range(2):
                dve.scalar_tensor_tensor(k_t[:, n, :], ROT[n][:, 0:T], V("k_norm"), k_root[:, 1, n, :],
                                         ALU.mult, ALU.mult).then_inc(S("k_ready"), 1)

        SYNC["kv"], TENSOR["kv"], SCALAR["kv"], VECTOR["kv"] = kv_sync, kv_tensor, kv_scalar, kv_vector

        at_sq = area(6400, 2, T)
        at_root = area(6912, 2, 2, T)
        q_t = area(7936, 2, T)
        bias_tile = area(8448, 2, 2, 384)
        prob = area(9984, 2, 2, 384)
        prob_t = area(11520, 2, 2, 384)
        o_t = area(13056, 2, T)
        at_stat = area(13568, 2, 6, 4)

        def attn_sync(sp):
            sp.wait_ge(S("bias_stored"), 16)
            sp.wait_ge(S("u_ready"), 4 * norm_no["attn"] + 1)
            with sp.Fori(0, 4) as i:
                for b in range(2):
                    load(sp, 2 * b, io["w_q"][bass.ds(2 * i + b, 1), :, :], "attn", i)
                    load(sp, 2 * b + 1, io["w_o"][bass.ds(2 * i + b, 1), :, :], "attn", i)
                    sp.wait_ge(S("scored"), 4 * i + 2 * b + 2)
                    for a in range(2):
                        table = bias_dram[bass.ds(4 * i + 2 * b + a, 1), 127:127 + P * 383].rearrange(
                            "h (q y) -> q (h y)", y=383)
                        sp.dma_start(bias_tile[:, b, a, 0:P], table[:, P:2 * P]).then_inc(S(f"bias_loaded{b}"), 16)
                        sp.dma_start(bias_tile[:, b, a, P:384], table[:, 0:2 * P]).then_inc(S(f"bias_loaded{b}"), 16)

        def attn_tensor(pe):
            clear_acc(pe, upd["attn"])
            pe.wait_ge(S("k_ready"), 2)
            for kv in range(2):
                with pe.Fori(0, 2) as ii:
                    i = 2 * kv + ii
                    for b in range(2):
                        j1 = 2 * i + b + 1
                        arrived(pe, 2 * b, "attn", i)
                        pe.wait_ge(S("p_turned_out"), 2 * j1)
                        project(pe, ROT[0][:, 0:T], 2 * b).then_inc(freed[2 * b], 1)
                        pe.wait_ge(S("q_squared"), j1)
                        pe.matmul(ROT[1][:, 0:T], C("blk64"), at_sq[:, b, :], start=True, stop=True).then_inc(S("q_summed"), 1)
                        pe.wait_ge(S("q_ready"), j1)
                        pe.wait_ge(S("o_ready"), j1)
                        for a in range(2):
                            hs = slice(a * HD, (a + 1) * HD)
                            pe.matmul(ROT[2 + a][:, 0:P], q_t[hs, b, 0:P], k_t[hs, kv, 0:P], start=True, stop=True)
                            pe.matmul(ROT[2 + a][:, P:384], q_t[hs, b, P:T], k_t[hs, kv, :], start=True,
                                      stop=True).then_inc(S("scores_done"), 1)
                        for a in range(2):
                            pe.wait_ge(S("prob_ready"), 2 * j1 - 1 + a)
                            for n in range(3):
                                mm = pe.transpose(ROT[a][:, n * P:(n + 1) * P], prob[:, b, a, n * P:(n + 1) * P], C("ident"))
                            mm.then_inc(S("p_turned"), 1)
                        for a in range(2):
                            pe.wait_ge(S("p_turned_out"), 2 * j1 + 1 + a)
                            vs = slice(kv * HD, (kv + 1) * HD)
                            out = ROT[2][a * HD:(a + 1) * HD, :]
                            pe.matmul(out[:, 0:P], v_rows[:, 0, vs], prob_t[:, b, a, 0:P], start=True, stop=True)
                            pe.matmul(out[:, P:T], v_rows[:, 0, vs], prob_t[:, b, a, P:2 * P], start=True, stop=False)
                            mm = pe.matmul(out[:, P:T], v_rows[:, 1, vs], prob_t[:, b, a, 2 * P:384], start=False, stop=True)
                        mm.then_inc(S("o_done"), 1)
                        arrived(pe, 2 * b + 1, "attn", i)
                        pe.wait_ge(S("o_ready"), j1 + 1)
                        close_into(pe, o_t[:, b, :], ring[2 * b + 1]).then_inc(freed[2 * b + 1], 1)

        def attn_scalar(act):
            with act.Fori(0, 4) as i:
                for b in range(2):
                    j1 = 2 * i + b + 1
                    multiplied(act, 2 * b, "attn", i)
                    act.activation(at_sq[:, b, :], ROT[0][:, 0:T], ACT.Square).then_inc(S("q_squared"), 1)
                    act.wait_ge(S("q_summed"), j1)
                    act.activation(at_root[:, b, 0, :], ROT[1][:, 0:T], ACT.Sqrt, scale=1.0 / HD,
                                   bias=stat[:, 14:15]).then_inc(S("q_rooted"), 1)
                    act.wait_ge(S("max_ready"), j1)
                    st = at_stat[:, b, :, :]
                    for n in range(4):
                        cols = slice(0, P) if n % 2 == 0 else slice(P, 384)
                        act.activation(prob[:, b, n // 2, cols], prob[:, b, n // 2, cols], ACT.Exp,
                                       bias=st[:, 1, n:n + 1], accum_out=st[:, 3, n:n + 1])
                    act.activation(st[:, 4, :], st[:, 2, :], ACT.Exp).then_inc(S("prob_exp"), 1)
                    for a in range(2):
                        act.wait_ge(S("p_turned"), 2 * j1 - 1 + a)
                        act.activation(prob_t[:, b, a, :], ROT[a][:, 0:384], ACT.Copy).then_inc(S("p_turned_out"), 1)
                    act.wait_ge(S("o_done"), j1)
                    act.activation(o_t[:, b, :], ROT[2][:, 0:T], ACT.Copy).then_inc(S("o_ready"), 1)

        def attn_vector(dve):
            with dve.Fori(0, 4) as i:
                for b in range(2):
                    j1 = 2 * i + b + 1
                    st = at_stat[:, b, :, :]
                    dve.wait_ge(S("q_rooted"), j1)
                    dve.reciprocal(at_root[:, b, 1, :], at_root[:, b, 0, :])
                    dve.drain()
                    dve.scalar_tensor_tensor(q_t[:, b, :], ROT[0][:, 0:T], V("q_norm"), at_root[:, b, 1, :],
                                             ALU.mult, ALU.mult).then_inc(S("q_ready"), 1)
                    dve.wait_ge(S(f"bias_loaded{b}"), 64 * i + 64)
                    for a in range(2):
                        dve.wait_ge(S("scores_done"), 2 * j1 - 1 + a)
                        dve.scalar_tensor_tensor(prob[:, b, a, :], ROT[2 + a][:, 0:384], HD ** -0.5,
                                                 bias_tile[:, b, a, :], ALU.mult, ALU.add).then_inc(S("scored"), 1)
                    dve.drain()
                    for n in range(4):
                        cols = slice(0, P) if n % 2 == 0 else slice(P, 384)
                        dve.reduce_max(st[:, 0, n:n + 1], prob[:, b, n // 2, cols], AX.X)
                    dve.drain()
                    sink = spread(VD("sinks", 4 * i + 2 * b, 2), 2)
                    view = st.rearrange("p s (a n) -> p s a n", a=2)
                    dve.tensor_tensor(view[:, 0, :, :], view[:, 0, :, :], sink, ALU.max)
                    dve.drain()
                    dve.tensor_tensor(view[:, 2, :, :], sink, view[:, 0, :, :], ALU.subtract)
                    dve.tensor_scalar(st[:, 1, :], st[:, 0, :], -1.0, None, ALU.mult)
                    dve.drain()
                    dve.sem_inc(S("max_ready"), 1)
                    dve.wait_ge(S("prob_exp"), j1)
                    dve.tensor_tensor(st[:, 3, :], st[:, 3, :], st[:, 4, :], ALU.add)
                    dve.drain()
                    dve.reciprocal(st[:, 5, :], st[:, 3, :])
                    dve.drain()
                    for n in range(4):
                        cols = slice(0, P) if n % 2 == 0 else slice(P, 384)
                        ins = dve.tensor_scalar(prob[:, b, n // 2, cols], prob[:, b, n // 2, cols],
                                                st[:, 5, n:n + 1], None, ALU.mult)
                        if n % 2:
                            ins.then_inc(S("prob_ready"), 1)
            multiplied(dve, 3, "attn", 3)
            update_h(dve, 1.0)

        SYNC["attn"], TENSOR["attn"], SCALAR["attn"], VECTOR["attn"] = attn_sync, attn_tensor, attn_scalar, attn_vector

        raw = area(5200, 14, 260)
        mixed = area(8840, 14, T)
        R_, K_, V_ = mixed[:, 0:4, :], mixed[:, 4:8, :], mixed[:, 8:12, :]
        wa_act, g_act = area(12424, T), area(12680, T)
        w_wa, w_g = area(12936, 512), area(13448, 512)
        log_decay, cum = area(13960, 4, T), area(14984, 4, T)
        p_now, p_prev, p_inv = area(16008, 4, T), area(17032, 4, T), area(18056, 4, T)
        a_gate, g_gate = area(19080, 4, T), area(20104, 4, T)
        kk, kk_a = area(21128, 4, T), area(22152, 4, T)
        rw_tmp, bonus, y_rw = area(23176, 4, T), area(24200, 4, T), area(25224, 4, T)
        alpha, beta, kappa, rho, v_now = (area(26248 + 256 * n, 4, CH) for n in range(5))
        (U, UL, A, AL, A2, AL2, A4) = (area(5200 + 512 * n, 4, P) for n in range(7))
        (AL4, A8, AL8, N, NL) = (area(27528 + 512 * n, 4, P) for n in range(5))
        v_st, kap_st, bet_st = (area(30088 + 256 * n, 4, CH) for n in range(3))
        lk_t, rk_t, rb_t = (area(30856 + 256 * n, 4, CH) for n in range(3))
        g_st, s_neg, z_st = (area(31624 + 256 * n, 4, CH) for n in range(3))
        halves = (slice(0, HD), slice(HD, P))

        def quarters(b, n=4):
            return b[:, :].rearrange("p (a b) -> p a b", a=n)

        def flat(t):
            return t.rearrange("p a b -> p (a b)")

        def rwkv_sync(sp):
            sp.wait_ge(S("u_ready"), 4 * norm_no["rwkv"] + 1)
            sp.dma_start(w_wa, io["w_wa"]).then_inc(S("lora_loaded"), 16)
            sp.dma_start(w_g, io["w_g"]).then_inc(S("lora_loaded"), 16)
            with sp.Fori(0, 2) as i:
                for n in range(7):
                    load(sp, n, io["rwkv_in"][bass.ds(7 * i + n, 1), :, :], "rwkv", i)
            for n in range(4):
                load(sp, n, io["w_o2"][4 + n, :, :], "rwkv_out")

        def rwkv_tensor(pe):
            pe.wait_ge(S("h_updated"), 4 * upd["rwkv"] + 1)
            with pe.Fori(0, 2) as i:
                for n in range(7):
                    arrived(pe, n, "rwkv", i)
                    pe.wait_ge(S("rw_evicted"), 7 * i + n + 1)
                    project(pe, bank[n][:, 0:T], n).then_inc(freed[n], 1)
            pe.wait_ge(S("rw_evicted"), 21)
            pe.wait_ge(S("lora_act"), 1)
            pe.wait_ge(S("lora_loaded"), 32)
            for kind in range(3):
                for p in range(4):
                    cols = slice(p * P, (p + 1) * P)
                    left, right = ((w_wa[0:HD, cols], wa_act[0:HD, :]), (w_wa[HD:P, cols], wa_act[HD:P, :]),
                                   (w_g[:, cols], g_act))[kind]
                    mm = pe.matmul(bank[2 * kind + p // 2][:, (p % 2) * T:(p % 2 + 1) * T], left, right,
                                   start=True, stop=True)
                mm.then_inc(S("lora_done"), 1)
            pe.wait_ge(S("kk_squared"), 1)
            for n in range(2):
                mm = pe.matmul(bank[6 + n][:, :], C("blk64"), flat(rw_tmp)[:, n * 512:(n + 1) * 512], start=True, stop=True)
            mm.then_inc(S("kk_summed"), 1)
            pe.wait_ge(S("rk_ready"), 1)
            pe.wait_ge(S("kk_rooted"), 1)
            for n in range(2):
                mm = pe.matmul(bank[6 + n][:, :], C("blk64"), flat(bonus)[:, n * 512:(n + 1) * 512], start=True, stop=True)
            mm.then_inc(S("rk_summed"), 1)
            with pe.Fori(0, RC) as c:
                pe.wait_ge(S("chunk_ready"), c + 1)
                pe.sem_inc(S("wait_held"), 1)
                for n, x in enumerate((v_now, kappa, beta)):
                    for p in range(4):
                        for a in halves:
                            at = (n % 2) * 256 + p * CH
                            mm = pe.matmul(bank[n // 2][a, at:at + CH], x[a, p, :], C("ident")[a, a], start=True, stop=True)
                mm.then_inc(S("rows_done"), 1)
                for n, (left, right) in enumerate(((beta, alpha), (alpha, beta), (kappa, alpha), (kappa, rho), (beta, rho))):
                    for p in range(4):
                        for a in halves:
                            at = (n % 2) * 256 + p * CH
                            mm = pe.matmul(bank[2 + n // 2][a, at:at + CH], left[a, p, :], right[a, p, :], start=True, stop=True)
                    if n % 2 or n == 4:
                        mm.then_inc(S("gram_done"), 1)

                def level(*products):
                    for b, left, right in products:
                        for p in range(4):
                            mm = pe.matmul(bank[b][:, p * P:(p + 1) * P], left[:, p, :], right[:, p, :], start=True, stop=True)
                    mm.then_inc(S("inv_done"), 1)

                pe.wait_ge(S("rows_ready"), c + 1)
                pe.wait_ge(S("inv_sum"), 6 * c + 1)
                level((0, AL, A), (1, A, AL))
                pe.wait_ge(S("lk_ready"), c + 1)
                pe.wait_ge(S("z_ready"), c + 1)
                pe.sem_inc(S("wait_held"), 1)
                for p in range(4):
                    for a in halves:
                        out = bank[4][a, 256 + p * CH:256 + (p + 1) * CH]
                        pe.matmul(out, alpha[a, p, :], z_st[a, p, :], start=True, stop=False)
                        mm = pe.matmul(out, lk_t[a, p, :], v_st[a, p, :], start=False, stop=True)
                mm.then_inc(S("g_done"), 1)
                pe.wait_ge(S("inv_copied"), 5 * c + 1)
                level((2, AL2, A2), (3, A2, AL2), (5, AL2, N), (6, A2, NL))
                pe.wait_ge(S("inv_copied"), 5 * c + 2)
                pe.wait_ge(S("inv_sum"), 6 * c + 2)
                level((0, AL4, A4), (1, A4, AL4), (5, AL4, N), (6, A4, NL))
                pe.wait_ge(S("inv_copied"), 5 * c + 3)
                pe.wait_ge(S("inv_sum"), 6 * c + 3)
                level((5, AL8, N), (6, A8, NL))
                pe.wait_ge(S("inv_sum"), 6 * c + 4)
                level((0, AL, N), (1, A, NL))
                pe.wait_ge(S("inv_copied"), 5 * c + 4)
                level((2, NL, A2), (3, N, A4))
                pe.wait_ge(S("inv_sum"), 6 * c + 5)
                level((0, AL, N))
                pe.wait_ge(S("inv_copied"), 5 * c + 5)
                level((1, NL, A2))
                pe.wait_ge(S("inv_sum"), 6 * c + 6)
                pe.wait_ge(S("g_ready"), c + 1)
                for p in range(4):
                    mm = pe.matmul(bank[5][:, p * CH:(p + 1) * CH], N[:, p, :], g_st[:, p, :], start=True, stop=True)
                mm.then_inc(S("s_done"), 1)
                pe.wait_ge(S("s_ready"), c + 1)
                pe.sem_inc(S("wait_held"), 1)
                for b, products in ((6, ((z_st, rho), (v_st, rk_t), (s_neg, rb_t))),
                                    (7, ((kap_st, v_st), (bet_st, s_neg)))):
                    for p in range(4):
                        for a in halves:
                            for n, (left, right) in enumerate(products):
                                mm = pe.matmul(bank[b][a, p * CH:(p + 1) * CH], left[a, p, :], right[a, p, :],
                                               start=(n == 0), stop=(n == len(products) - 1))
                    mm.then_inc(S("step_done"), 1)
            for n in range(2):
                pe.wait_ge(S("y_rw_ready"), n + 1)
                src = (y_rw, rw_tmp)[n]
                for b in range(2):
                    mm = pe.matmul(bank[2 * n + b][:, :], C("blk64"), flat(src)[:, b * 512:(b + 1) * 512], start=True, stop=True)
                mm.then_inc(S("y_rw_summed"), 1)
            pe.wait_ge(S("y_rw_ready"), 3)
            clear_acc(pe, upd["rwkv"])
            for p in range(4):
                arrived(pe, p, "rwkv_out")
                close_into(pe, y_rw[:, p, :], ring[p]).then_inc(freed[p], 1)

        def rwkv_scalar(act):
            with act.Fori(0, 2) as i:
                for n in range(7):
                    multiplied(act, n, "rwkv", i)
                    act.activation(raw[:, bass.ds(7 * i + n, 1), 1:1 + T], bank[n][:, 0:T].unsqueeze(1),
                                   ACT.Copy).then_inc(S("rw_evicted"), 1)
            act.wait_ge(S("rw_mixed"), 14)
            act.activation(wa_act[0:HD, :], mixed[0:HD, 12, :], ACT.Tanh)
            act.activation(wa_act[HD:P, :], mixed[HD:P, 12, :], ACT.Copy)
            act.activation(g_act, mixed[:, 13, :], ACT.Sigmoid).then_inc(S("lora_act"), 1)
            for kind, (dst, b0) in enumerate(((log_decay, "w0"), (a_gate, "a0"))):
                act.wait_ge(S("lora_done"), kind + 1)
                for p in range(4):
                    ins = act.activation(dst[:, p, :], bank[2 * kind + p // 2][:, (p % 2) * T:(p % 2 + 1) * T], ACT.Sigmoid,
                                         bias=V(b0, p, p + 1))
                ins.then_inc(S("gates_ready"), 1)
            act.wait_ge(S("lora_done"), 3)
            for b in range(2):
                act.activation(flat(g_gate)[:, b * 512:(b + 1) * 512], bank[4 + b][:, :], ACT.Copy)
            act.wait_ge(S("kk_raw"), 1)
            act.activation(rw_tmp, kk, ACT.Square).then_inc(S("kk_squared"), 1)
            act.wait_ge(S("cum_ready"), 1)
            act.activation(p_now, cum, ACT.Exp)
            act.activation(p_prev, p_prev, ACT.Exp)
            act.activation(p_inv, cum, ACT.Exp, scale=-1.0).then_inc(S("p_ready"), 1)
            act.wait_ge(S("kk_summed"), 1)
            for b in range(2):
                ins = act.activation(flat(rw_tmp)[:, b * 512:(b + 1) * 512], bank[6 + b][:, :], ACT.Sqrt)
            ins.then_inc(S("kk_rooted"), 1)
            with act.Fori(0, RC) as c:
                act.wait_ge(S("rows_done"), c + 1)
                act.activation(area(30088, 512), bank[0][:, :], ACT.Copy)
                act.activation(flat(bet_st), bank[1][:, 0:256], ACT.Copy).then_inc(S("rows_ready"), 1)
                for done, pairs in ((1, ((0, A2), (1, AL2))), (2, ((2, A4), (3, AL4))), (3, ((0, A8), (1, AL8))),
                                    (5, ((0, A2), (1, A4))), (7, ((0, A2),))):
                    act.wait_ge(S("inv_done"), 8 * c + done)
                    for b, dst in pairs:
                        ins = act.activation(flat(dst), bank[b][:, :], ACT.Copy)
                    ins.then_inc(S("inv_copied"), 1)
            act.wait_ge(S("y_centred"), 1)
            act.activation(rw_tmp, y_rw, ACT.Square).then_inc(S("y_rw_ready"), 1)
            act.wait_ge(S("y_rw_summed"), 2)
            for b in range(2):
                ins = act.activation(flat(rw_tmp)[:, b * 512:(b + 1) * 512], bank[2 + b][:, :], ACT.Sqrt, scale=1.0 / HD,
                                     bias=stat[:, 15:16])
            ins.then_inc(S("y_rw_rooted"), 1)

        def rwkv_vector(dve):
            def by_pair(out, x, gain, op1=None, off=None):
                for p in range(4):
                    ins = dve.tensor_scalar(out[:, p, :], x[:, p, :], V(gain, p, p + 1),
                                            V(off, p, p + 1) if off else None, ALU.mult, op1 or ALU.bypass)
                return ins

            dve.memset(raw[:, :, 0:1], 0.0)
            dve.drain()
            with dve.Fori(0, 2) as i:
                for n in range(7):
                    m = bass.ds(7 * i + n, 1)
                    dve.wait_ge(S("rw_evicted"), 7 * i + n + 8)
                    dve.tensor_tensor(mixed[:, m, :], raw[:, m, 0:T], raw[:, m, 1:1 + T], ALU.subtract)
                    dve.drain()
                    dve.scalar_tensor_tensor(mixed[:, m, :], mixed[:, m, :], VD("mu", 7 * i + n), raw[:, m, 1:1 + T],
                                             ALU.mult, ALU.add).then_inc(S("rw_mixed"), 1)
            dve.drain()
            dve.memset(y_rw, 1.0)
            by_pair(kk, K_, "k_k").then_inc(S("kk_raw"), 1)
            dve.drain()
            dve.memset(flat(y_rw).rearrange("p (c s) -> p c s", s=CH)[:, :, 0:1], 0.0)
            dve.wait_ge(S("gates_ready"), 1)
            dve.tensor_scalar(log_decay, log_decay, -math.exp(-0.5), None, ALU.mult)
            dve.drain()
            dve.tensor_tensor_scan(flat(cum), flat(y_rw), flat(log_decay), 0.0, ALU.mult, ALU.add)
            dve.drain()
            dve.tensor_tensor(p_prev, cum, log_decay, ALU.subtract).then_inc(S("cum_ready"), 1)
            dve.wait_ge(S("gates_ready"), 2)
            for p in range(4):
                dve.tensor_scalar(kk_a[:, p, :], a_gate[:, p, :], 1.0, V("k_a", p, p + 1), ALU.subtract, ALU.mult)
            dve.drain()
            dve.scalar_tensor_tensor(flat(K_), flat(kk_a), 1.0, flat(K_), ALU.add, ALU.mult)
            dve.drain()
            dve.tensor_tensor(bonus, R_, K_, ALU.mult)
            dve.drain()
            by_pair(bonus, bonus, "r_k").then_inc(S("rk_ready"), 1)
            dve.wait_ge(S("kk_rooted"), 1)
            dve.tensor_scalar(rw_tmp, rw_tmp, 1e-12, None, ALU.max)
            dve.drain()
            dve.reciprocal(rw_tmp, rw_tmp)
            dve.drain()
            dve.tensor_tensor(kk, kk, rw_tmp, ALU.mult)
            dve.drain()
            dve.tensor_tensor(kk_a, kk, a_gate, ALU.mult)
            dve.wait_ge(S("rk_summed"), 1)
            for b in range(2):
                dve.tensor_tensor(flat(bonus)[:, b * 512:(b + 1) * 512], bank[6 + b][:, :],
                                  flat(V_)[:, b * 512:(b + 1) * 512], ALU.mult)
            for m in (U, UL):
                dve.memset(m, 0.0)
            dve.memset(z_st, 0.0).then_inc(S("z_ready"), 1)
            dve.wait_ge(S("p_ready"), 1)
            dve.drain()

            def over_pairs(mask):
                return mask.unsqueeze(1).broadcast_to([mask.shape[0], 4, mask.shape[1]])

            with dve.Fori(0, RC) as c:
                now = bass.ds(c * CH, CH)
                dve.tensor_tensor(alpha, p_prev[:, :, now], kk[:, :, now], ALU.mult)
                dve.tensor_tensor(beta, p_inv[:, :, now], kk_a[:, :, now], ALU.mult)
                dve.tensor_tensor(kappa, p_inv[:, :, now], K_[:, :, now], ALU.mult)
                dve.tensor_tensor(rho, p_now[:, :, now], R_[:, :, now], ALU.mult)
                dve.tensor_copy(v_now, V_[:, :, now]).then_inc(S("chunk_ready"), 1)
                dve.wait_ge(S("gram_done"), 3 * c + 1)
                for a in halves:
                    for n, (m, mask) in enumerate(((U, "up_strict"), (UL, "low_strict"))):
                        dve.tensor_tensor(m[a, :, a], quarters(bank[2], 8)[a, 4 * n:4 * n + 4, :],
                                          over_pairs(C(mask)[a, :]), ALU.mult)
                dve.drain()
                dve.tensor_tensor(A, U, over_pairs(C("u16")), ALU.mult)
                dve.tensor_tensor(AL, UL, over_pairs(C("l16")), ALU.mult)
                dve.drain()
                dve.tensor_tensor(N, over_pairs(C("ident")), A, ALU.subtract)
                dve.tensor_tensor(NL, over_pairs(C("ident")), AL, ALU.subtract).then_inc(S("inv_sum"), 1)
                dve.wait_ge(S("gram_done"), 3 * c + 3)
                dve.tensor_tensor(lk_t, quarters(bank[3], 8)[:, 0:4, :], over_pairs(C("up_strict")), ALU.mult)
                dve.tensor_tensor(rk_t, quarters(bank[3], 8)[:, 4:8, :], over_pairs(C("up_incl")), ALU.mult)
                dve.tensor_tensor(rb_t, quarters(bank[4], 8)[:, 0:4, :], over_pairs(C("up_incl")), ALU.mult).then_inc(S("lk_ready"), 1)

                def add(done, op, *pairs):
                    dve.wait_ge(S("inv_done"), 8 * c + done)
                    for m, b in pairs:
                        ins = dve.tensor_tensor(m, m, quarters(bank[b]), op)
                    return ins

                add(2, ALU.add, (N, 5), (NL, 6)).then_inc(S("inv_sum"), 1)
                dve.wait_ge(S("g_done"), c + 1)
                dve.tensor_copy(flat(g_st), bank[4][:, 256:512]).then_inc(S("g_ready"), 1)
                add(3, ALU.add, (N, 5), (NL, 6)).then_inc(S("inv_sum"), 1)
                dve.tensor_tensor(A, U, over_pairs(C("u32")), ALU.mult)
                dve.tensor_tensor(AL, UL, over_pairs(C("l32")), ALU.mult)
                add(4, ALU.add, (N, 5), (NL, 6)).then_inc(S("inv_sum"), 1)
                add(6, ALU.subtract, (N, 2), (NL, 3))
                dve.tensor_tensor(AL, UL, over_pairs(C("l64")), ALU.mult).then_inc(S("inv_sum"), 1)
                add(8, ALU.subtract, (N, 1)).then_inc(S("inv_sum"), 1)
                dve.wait_ge(S("s_done"), c + 1)
                dve.tensor_scalar(flat(s_neg), bank[5][:, 0:256], -1.0, None, ALU.mult).then_inc(S("s_ready"), 1)
                dve.wait_ge(S("step_done"), 2 * c + 1)
                dve.tensor_copy(y_rw[:, :, now], bank[6][:, 0:256].rearrange("p (a b) -> p a b", a=4))
                dve.wait_ge(S("step_done"), 2 * c + 2)
                dve.tensor_tensor(flat(z_st), flat(z_st), bank[7][:, 0:256], ALU.add)
                dve.drain()
                end = p_now[:, :, bass.ds(c * CH + CH - 1, 1)]
                dve.tensor_tensor(z_st, z_st, end.broadcast_to([P, 4, CH]), ALU.mult).then_inc(S("z_ready"), 1)
            dve.drain()
            dve.sem_inc(S("y_rw_ready"), 1)
            dve.wait_ge(S("y_rw_summed"), 1)
            for b in range(2):
                part = flat(y_rw)[:, b * 512:(b + 1) * 512]
                ins = dve.scalar_tensor_tensor(part, bank[b][:, :], -1.0 / HD, part, ALU.mult, ALU.add)
            ins.then_inc(S("y_centred"), 1)
            dve.wait_ge(S("y_rw_rooted"), 1)
            dve.reciprocal(rw_tmp, rw_tmp)
            dve.drain()
            dve.tensor_tensor(y_rw, y_rw, rw_tmp, ALU.mult)
            dve.drain()
            by_pair(y_rw, y_rw, "lnw", ALU.add, "lnb")
            dve.drain()
            dve.tensor_tensor(y_rw, y_rw, bonus, ALU.add)
            dve.drain()
            dve.tensor_tensor(y_rw, y_rw, g_gate, ALU.mult).then_inc(S("y_rw_ready"), 1)

        SYNC["rwkv"], TENSOR["rwkv"], SCALAR["rwkv"], VECTOR["rwkv"] = rwkv_sync, rwkv_tensor, rwkv_scalar, rwkv_vector

        def mix_vector(dve):
            if "mla" in stages:
                multiplied(dve, 7, "mla_heads", 3)
            if "rwkv" in stages:
                multiplied(dve, 3, "rwkv_out")
            update_h(dve, 1.0)

        VECTOR["mix"] = mix_vector

        Q_, K2 = slice(0, QK), slice(NOPE, QK)
        uv_all = area(0, 4 * 2 * P)
        pos_i, pos_f = area(1024, T), area(1280, T)
        turns, cos_t, sin_t = area(1536, T), area(2048, T), area(2304, T)
        lat = area(4096, 6, T)
        lat_sq = area(5632, 5, T)
        lat_root = area(6912, 2, T)
        qk_sq, qk_root, qk_norm = (area(7424 + 1024 * n, 2, 512) for n in range(3))
        qk_cos, qk_sin, qk_rope = (area(10496 + 1024 * n, 2, 512) for n in range(3))
        m_prob, m_prob_t = area(13568, 2, 384), area(14336, 2, 384)
        v_pair = area(15104, TT, P)
        mo_sq, mo_root, mo_t = area(15360, T), area(15616, T), area(15872, T)
        m_stat = area(16128, 2, 3, 2)
        blocks = (slice(0, P), slice(P, 384))

        def mla_sync(sp):
            sp.wait_ge(S("u_ready"), 4 * norm_no["rwkv"] + 4)
            sp.dma_start(uv_all.rearrange("p (i n) -> p i n", i=4), io["mla_uv"].rearrange("i p n -> p i n")).then_inc(S("uv_loaded"), 16)
            sp.dma_start(pos_i.bitcast(I32), io["positions"].broadcast_to([P, T])).then_inc(S("pos_loaded"), 16)
            for n in range(6):
                load(sp, n, io["mla_in"][n, :, :], "mla")
            with sp.Fori(0, 4) as i:
                load(sp, 6, io["mla_u"][bass.ds(i, 1), :, :], "mla_heads", i)
                load(sp, 7, io["w_o2"][bass.ds(i, 1), :, :], "mla_heads", i)

        def mla_tensor(pe):
            if "rwkv" not in stages:
                clear_acc(pe, upd["mla"])
            for n in range(6):
                arrived(pe, n, "mla")
                if n >= 4:
                    pe.wait_ge(S("lat_out"), n - 3)
                project(pe, ROT[n % 4][:, 0:T], n).then_inc(freed[n], 1)
            pe.wait_ge(S("lat_out"), 6)
            pe.wait_ge(S("lat_squared"), 1)
            for b, part in enumerate((range(0, 3), range(3, 5))):
                for c in part:
                    mm = pe.matmul(ROT[b][:, 0:T], C("ones"), lat_sq[:, c, :], start=(c == part[0]), stop=(c == part[-1]))
            mm.then_inc(S("lat_summed"), 1)
            pe.wait_ge(S("lat_ready"), 1)
            pe.wait_ge(S("uv_loaded"), 16)
            with pe.Fori(0, 4) as i:
                arrived(pe, 6, "mla_heads", i)
                pe.wait_ge(S("mo_ready"), i + 1)
                for a in range(2):
                    for c in range(3):
                        at = (3 * a + c) * QK
                        mm = pe.matmul(ROT[a][Q_, 0:T], ring[6][:, at:at + QK], lat[:, c, :], start=(c == 0), stop=(c == 2))
                    pe.matmul(ROT[a][Q_, T:512], C("ident", 0, QK)[K2, :], lat[K2, 5, :], start=True, stop=False)
                    for c in range(2):
                        at = (6 + 2 * a + c) * QK
                        mm = pe.matmul(ROT[a][Q_, T:512], ring[6][:, at:at + QK], lat[:, 3 + c, :], start=False, stop=(c == 1))
                    mm.then_inc(S("mqk_done") if a == 0 else freed[6], 1)
                pe.wait_ge(S("mp_out"), 2 * i + 1)
                for tt in range(TT):
                    for c in range(2):
                        mm = pe.matmul(ROT[2][:, tt * P:(tt + 1) * P], lat[:, 3 + c, tt * P:(tt + 1) * P],
                                       uv_all[:, bass.ds(i * 2 * P + c * P, P)], start=(c == 0), stop=(c == 1))
                mm.then_inc(S("mv_done"), 1)
                for a in range(2):
                    pe.wait_ge(S("mqk_squared"), 2 * i + a + 1)
                    if a == 1:
                        pe.wait_ge(S("mv_out"), i + 1)
                    pe.matmul(ROT[3 - a][Q_, :], C("ones", 0, QK)[Q_, :], qk_sq[Q_, a, :], start=True,
                              stop=True).then_inc(S("mqk_summed"), 1)
                for a in range(2):
                    pe.wait_ge(S("mqk_normed"), 2 * i + a + 1)
                    pe.matmul(ROT[3 - a][Q_, :], C("rot")[Q_, :], qk_norm[Q_, a, :], start=True,
                              stop=True).then_inc(S("mqk_turned"), 1)
                for a in range(2):
                    pe.wait_ge(S("mqk_ready"), 2 * i + a + 1)
                    q, k = qk_rope[Q_, a, 0:T], qk_rope[Q_, a, T:512]
                    pe.matmul(ROT[a][:, 0:P], q[:, 0:P], k[:, 0:P], start=True, stop=True)
                    pe.matmul(ROT[a][:, P:384], q[:, P:T], k, start=True, stop=True).then_inc(S("m_scores"), 1)
                for a in range(2):
                    pe.wait_ge(S("mp_ready"), 2 * i + a + 1)
                    for n in range(3):
                        mm = pe.transpose(ROT[3 - a][:, n * P:(n + 1) * P], m_prob[:, a, n * P:(n + 1) * P], C("ident"))
                    mm.then_inc(S("mp_turned"), 1)
                for a in range(2):
                    pe.wait_ge(S("mp_out"), 2 * i + a + 2)
                    out, vs = ROT[0][a * HD:(a + 1) * HD, :], slice(a * HD, (a + 1) * HD)
                    pe.matmul(out[:, 0:P], v_pair[:, 0, vs], m_prob_t[:, a, 0:P], start=True, stop=True)
                    pe.matmul(out[:, P:T], v_pair[:, 0, vs], m_prob_t[:, a, P:2 * P], start=True, stop=False)
                    mm = pe.matmul(out[:, P:T], v_pair[:, 1, vs], m_prob_t[:, a, 2 * P:384], start=False, stop=True)
                mm.then_inc(S("mo_done"), 1)
                pe.wait_ge(S("mo_squared"), i + 1)
                pe.matmul(ROT[1][:, 0:T], C("blk64"), mo_sq, start=True, stop=True).then_inc(S("mo_summed"), 1)
                arrived(pe, 7, "mla_heads", i)
                pe.wait_ge(S("mo_ready"), i + 2)
                close_into(pe, mo_t, ring[7]).then_inc(freed[7], 1)

        def mla_scalar(act):
            for n in range(6):
                multiplied(act, n, "mla")
                act.activation(lat[:, n, :], ROT[n % 4][:, 0:T], ACT.Copy).then_inc(S("lat_out"), 1)
            act.wait_ge(S("lat_out"), 6)
            act.activation(lat_sq, lat[:, 0:5, :], ACT.Square).then_inc(S("lat_squared"), 1)
            act.wait_ge(S("angles_ready"), 1)
            act.activation(sin_t[Q_, :], sin_t[Q_, :], ACT.Sin)
            act.activation(cos_t[Q_, :], cos_t[Q_, :], ACT.Sin).then_inc(S("rope_ready"), 1)
            act.wait_ge(S("lat_summed"), 1)
            act.activation(lat_root[:, 0, :], ROT[0][:, 0:T], ACT.Sqrt, scale=1.0 / MLA_Q, bias=stat[:, 14:15])
            act.activation(lat_root[:, 1, :], ROT[1][:, 0:T], ACT.Sqrt, scale=1.0 / MLA_KV,
                           bias=stat[:, 14:15]).then_inc(S("lat_rooted"), 1)
            with act.Fori(0, 4) as i:
                for a in range(2):
                    if a == 0:
                        act.wait_ge(S("mqk_done"), i + 1)
                    else:
                        multiplied(act, 6, "mla_heads", i)
                    act.activation(qk_sq[Q_, a, :], ROT[a][Q_, :], ACT.Square).then_inc(S("mqk_squared"), 1)
                act.wait_ge(S("mv_done"), i + 1)
                act.activation(v_pair, ROT[2][:, 0:T].rearrange("p (a b) -> p a b", a=TT), ACT.Copy).then_inc(S("mv_out"), 1)
                for a in range(2):
                    act.wait_ge(S("mqk_summed"), 2 * i + a + 1)
                    act.activation(qk_root[Q_, a, :], ROT[3 - a][Q_, :], ACT.Sqrt, scale=1.0 / QK,
                                   bias=stat[Q_, 14:15]).then_inc(S("mqk_rooted"), 1)
                for a in range(2):
                    act.wait_ge(S("m_max"), 2 * i + a + 1)
                    for n, cols in enumerate(blocks):
                        ins = act.activation(m_prob[:, a, cols], m_prob[:, a, cols], ACT.Exp,
                                             bias=m_stat[:, a, 1, n:n + 1], accum_out=m_stat[:, a, 2, n:n + 1])
                    ins.then_inc(S("mp_exp"), 1)
                for a in range(2):
                    act.wait_ge(S("mp_turned"), 2 * i + a + 1)
                    act.activation(m_prob_t[:, a, :], ROT[3 - a][:, 0:384], ACT.Copy).then_inc(S("mp_out"), 1)
                act.wait_ge(S("mo_done"), i + 1)
                act.activation(mo_sq, ROT[0][:, 0:T], ACT.Square).then_inc(S("mo_squared"), 1)
                act.wait_ge(S("mo_summed"), i + 1)
                act.activation(mo_root, ROT[1][:, 0:T], ACT.Sqrt, scale=1.0 / HD, bias=stat[:, 14:15]).then_inc(S("mo_rooted"), 1)

        def mla_vector(dve):
            dve.wait_ge(S("pos_loaded"), 16)
            dve.tensor_copy(pos_f, pos_i.bitcast(I32))
            dve.drain()
            dve.tensor_scalar(pos_f, pos_f, C("inv_freq"), None, ALU.mult)
            dve.drain()
            dve.tensor_scalar(turns, pos_f, 1.0 / (2 * math.pi), 1.5 * 2.0 ** 23, ALU.mult, ALU.add)
            dve.drain()
            dve.tensor_scalar(turns, turns, -1.5 * 2.0 ** 23, None, ALU.add)
            c1 = 6.28125
            c2 = float(np.float32(np.round((2 * math.pi - c1) * 2 ** 21) / 2 ** 21))
            for c in (c1, c2, 2 * math.pi - c1 - c2):
                dve.drain()
                dve.scalar_tensor_tensor(pos_f, turns, -c, pos_f, ALU.mult, ALU.add)
            dve.drain()
            dve.tensor_scalar(sin_t, pos_f, 3.1415925, -3.1415925, ALU.min, ALU.max)
            dve.tensor_scalar(cos_t, pos_f, -1.0, None, ALU.mult)
            dve.drain()
            dve.tensor_tensor(cos_t, cos_t, pos_f, ALU.min)
            dve.drain()
            dve.tensor_scalar(cos_t, cos_t, C("half"), None, ALU.add).then_inc(S("angles_ready"), 1)
            dve.wait_ge(S("lat_rooted"), 1)
            dve.reciprocal(lat_root, lat_root)
            dve.drain()
            for c in range(5):
                gain = V("g_cq", c, c + 1) if c < 3 else V("g_ckv", c - 3, c - 2)
                ins = dve.scalar_tensor_tensor(lat[:, c, :], lat[:, c, :], gain, lat_root[:, c // 3, :], ALU.mult, ALU.mult)
            ins.then_inc(S("lat_ready"), 1)
            dve.wait_ge(S("rope_ready"), 1)

            def twice(t):
                return t[Q_, :].unsqueeze(1).broadcast_to([QK, 2, T])

            def two(t):
                return t.rearrange("p (a b) -> p a b", a=2)

            with dve.Fori(0, 4) as i:
                for a in range(2):
                    dve.wait_ge(S("mqk_rooted"), 2 * i + a + 1)
                    dve.reciprocal(qk_root[Q_, a, :], qk_root[Q_, a, :])
                    dve.drain()
                    for n, gain in enumerate(("g_qnorm", "g_knorm")):
                        cols = slice(n * T, (n + 1) * T)
                        ins = dve.scalar_tensor_tensor(qk_norm[Q_, a, cols], ROT[a][Q_, cols], V(gain)[Q_, :],
                                                       qk_root[Q_, a, cols], ALU.mult, ALU.mult)
                    ins.then_inc(S("mqk_normed"), 1)
                dve.drain()
                for a in range(2):
                    dve.tensor_tensor(two(qk_cos[Q_, a, :]), two(qk_norm[Q_, a, :]), twice(cos_t), ALU.mult)
                    dve.wait_ge(S("mqk_turned"), 2 * i + a + 1)
                    dve.tensor_tensor(two(qk_sin[Q_, a, :]), two(ROT[3 - a][Q_, :]), twice(sin_t), ALU.mult)
                    dve.drain()
                    dve.tensor_tensor(qk_rope[Q_, a, :], qk_cos[Q_, a, :], qk_sin[Q_, a, :], ALU.add).then_inc(S("mqk_ready"), 1)
                for a in range(2):
                    dve.wait_ge(S("m_scores"), 2 * i + a + 1)
                    dve.scalar_tensor_tensor(m_prob[:, a, :], ROT[a][:, 0:384], QK ** -0.5, C("mla_mask"), ALU.mult, ALU.add)
                    dve.drain()
                    for n, cols in enumerate(blocks):
                        dve.reduce_max(m_stat[:, a, 0, n:n + 1], m_prob[:, a, cols], AX.X)
                    dve.drain()
                    dve.tensor_scalar(m_stat[:, a, 1, :], m_stat[:, a, 0, :], -1.0, None, ALU.mult).then_inc(S("m_max"), 1)
                for a in range(2):
                    dve.wait_ge(S("mp_exp"), 2 * i + a + 1)
                    dve.reciprocal(m_stat[:, a, 2, :], m_stat[:, a, 2, :])
                    dve.drain()
                    for n, cols in enumerate(blocks):
                        ins = dve.tensor_scalar(m_prob[:, a, cols], m_prob[:, a, cols], m_stat[:, a, 2, n:n + 1], None, ALU.mult)
                    ins.then_inc(S("mp_ready"), 1)
                dve.wait_ge(S("mo_rooted"), i + 1)
                dve.reciprocal(mo_root, mo_root)
                dve.drain()
                dve.scalar_tensor_tensor(mo_t, ROT[0][:, 0:T], VD("g_out", i), mo_root, ALU.mult, ALU.mult).then_inc(S("mo_ready"), 1)

        SYNC["mla"], TENSOR["mla"], SCALAR["mla"], VECTOR["mla"] = mla_sync, mla_tensor, mla_scalar, mla_vector

        peer_sb = sb("peer_sb", [P, 3 * T + 2048])
        choice_t = peer_sb[:, 0:3 * T].rearrange("p (k t) -> p k t", k=3)
        one_a, one_b = (peer_sb[:, 3 * T + 1024 * n:3 * T + 1024 * (n + 1)].rearrange(
            "p (g t e) -> p g t e", g=2, t=4) for n in range(2))
        gelu_buf, gated_buf = (x.rearrange("p g t e -> p (g t e)")[:, 0:2 * T].rearrange("p (b t) -> p b t", b=2)
                               for x in (one_a, one_b))
        keys_all = area(4096, PH * 2 * NKEYS)
        pq_t = area(6144, 2, T)
        score = area(6656, 4, NKEYS)
        score2 = area(7168, 4, NKEYS)
        top, top_i, top_f = (area(7680 + 64 * n, 4, TOPK) for n in range(3))
        cand, cand2 = (area(8192 + 512 * n, TT, TOPK * TOPK) for n in range(2))
        best, best_i, best_a, best_b, best_af, best_bf, gate = (area(9216 + 32 * n, TT, TOPK) for n in range(7))
        gate_sum = area(9472, 2, TT)
        pick = area(9728, TT, TOPK, TOPK)
        choice = area(10240, 3, TT, P)
        gates_of = arena[:, :].rearrange("p (b t) -> p b t", b=NKEYS)

        def peer_sync(sp):
            sp.wait_ge(S("u_ready"), 4 * norm_no["peer"] + 1)
            sp.dma_start(keys_all.rearrange("p (h n) -> p h n", h=PH), io["keys"].rearrange("h p n -> p h n")).then_inc(S("keys_loaded"), 16)
            with sp.Fori(0, PH) as i:
                for n in range(2):
                    load(sp, n, io["w_pq"][bass.ds(2 * i + n, 1), :, :], "route", i)
            with sp.Fori(0, NKEYS // 4) as i:
                for b in range(4):
                    load(sp, 2 * b, io["expert_u"][bass.ds(4 * i + b, 1), :, :], "peer", i)
                    load(sp, 2 * b + 1, io["expert_v"][bass.ds(4 * i + b, 1), :, :], "peer", i)

        def peer_tensor(pe):
            pe.wait_ge(S("keys_loaded"), 16)
            with pe.Fori(0, PH) as i:
                pe.wait_ge(S("pq_out"), 2 * i + 2)
                for n in range(2):
                    arrived(pe, n, "route", i)
                    project(pe, ROT[n][:, 0:T], n).then_inc(freed[n], 1)
                pe.wait_ge(S("pq_out"), 2 * i + 4)
                pe.wait_ge(S("score_out"), i + 1)
                for tt in range(TT):
                    for n in range(2):
                        at = (2 * tt + n) * P
                        mm = pe.matmul(ROT[2][:, at:at + P], pq_t[:, n, tt * P:(tt + 1) * P],
                                       keys_all[:, bass.ds((2 * i + n) * NKEYS, NKEYS)], start=True, stop=True)
                mm.then_inc(S("score_done"), 1)
            pe.wait_ge(S("chosen"), 1)
            for k in range(3):
                for tt in range(TT):
                    mm = pe.transpose(ROT[k][:, tt * P:(tt + 1) * P], choice[:, k, tt, :], C("ident"))
            mm.then_inc(S("choice_turned"), 1)
            pe.wait_ge(S("choice_ready"), 1)
            with pe.Fori(0, T // 8) as i:
                for g in range(2):
                    pe.wait_ge(S("one_hot"), 2 * i + g + 3)
                    pe.wait_ge(S("gates_out"), 2 * i + g + 1)
                    for t in range(4):
                        mm = pe.matmul(ROT[g][:, t * P:(t + 1) * P], one_b[:, g, t, :], one_a[:, g, t, :], start=True, stop=True)
                    mm.then_inc(S("gates_done"), 1)
            clear_acc(pe, upd["peer"])

            def up(b, i):
                arrived(pe, 2 * b, "peer", i)
                pe.wait_ge(S("gelu_out"), 4 * i + b + 1)
                project(pe, ROT[b][:, 0:T], 2 * b).then_inc(freed[2 * b], 1)

            def down(b, i, last=False):
                arrived(pe, 2 * b + 1, "peer", i)
                pe.wait_ge(S("gated"), 4 * i + b + 3)
                close_into(pe, gated_buf[:, b % 2, :], ring[2 * b + 1], last).then_inc(freed[2 * b + 1], 1)

            pe.wait_ge(S("gates_out"), 2 + T // 4)
            up(0, 0)
            with pe.Fori(0, NKEYS // 4 - 1) as i:
                for b in range(4):
                    up((b + 1) % 4, i + (b + 1) // 4)
                    down(b, i)
            n = NKEYS // 4 - 1
            for b in range(4):
                if b < 3:
                    up(b + 1, n)
                down(b, n, last=(b == 3))

        def peer_scalar(act):
            with act.Fori(0, PH) as i:
                for n in range(2):
                    multiplied(act, n, "route", i)
                    act.activation(pq_t[:, n, :], ROT[n][:, 0:T], ACT.Copy).then_inc(S("pq_out"), 1)
                act.wait_ge(S("best_ready"), i + 1)
                act.activation(gate, gate, ACT.Exp).then_inc(S("gate_exp"), 1)
            with act.Fori(0, T // 8) as i:
                for g in range(2):
                    act.wait_ge(S("gates_done"), 2 * i + g + 3)
                    out = gates_of[:, :, bass.ds(8 * i + 4 * g, 4)].rearrange("p b t -> p t b")
                    act.activation(out, quarters(ROT[g]), ACT.Copy).then_inc(S("gates_out"), 1)
            with act.Fori(0, NKEYS // 4) as i:
                for b in range(4):
                    multiplied(act, 2 * b, "peer", i)
                    act.wait_ge(S("gated"), 4 * i + b + 1)
                    act.activation(gelu_buf[:, b % 2, :], ROT[b][:, 0:T], ACT.Gelu).then_inc(S("gelu_out"), 1)

        def peer_vector(dve):
            def as_int(t):
                return t.bitcast(U32)

            def top16(values, indices, src, less, rows):
                for r in rows:
                    dve.max(values[:, r, 0:8], src[:, r, :])
                dve.drain()
                for r in rows:
                    dve.max_index(as_int(indices)[:, r, 0:8], values[:, r, 0:8], src[:, r, :])
                    dve.match_replace(less[:, r, :], values[:, r, 0:8], src[:, r, :], -3e38)
                dve.drain()
                for r in rows:
                    dve.max(values[:, r, 8:16], less[:, r, :])
                dve.drain()
                for r in rows:
                    dve.max_index(as_int(indices)[:, r, 8:16], values[:, r, 8:16], less[:, r, :])
                dve.drain()

            with dve.Fori(0, PH) as i:
                dve.wait_ge(S("score_done"), i + 1)
                dve.tensor_copy(flat(score), ROT[2][:, :]).then_inc(S("score_out"), 1)
                dve.drain()
                top16(top, top_i, score, score2, range(4))
                dve.tensor_copy(flat(top_f), as_int(flat(top_i)))
                for tt in range(TT):
                    dve.tensor_tensor(cand[:, tt, :].rearrange("p (a b) -> p a b", a=TOPK), spread(top[:, 2 * tt, :], TOPK),
                                      top[:, 2 * tt + 1, :].unsqueeze(1).broadcast_to([P, TOPK, TOPK]), ALU.add)
                dve.drain()
                top16(best, best_i, cand, cand2, range(TT))
                dve.tensor_tensor(gate, best, best[:, :, 0:1].broadcast_to([P, TT, TOPK]), ALU.subtract).then_inc(S("best_ready"), 1)
                dve.tensor_scalar(as_int(flat(best_a)), as_int(flat(best_i)), 4, None, ALU.logical_shift_right)
                dve.tensor_scalar(as_int(flat(best_b)), as_int(flat(best_i)), 15, None, ALU.bitwise_and)
                dve.drain()
                dve.tensor_copy(flat(best_af), as_int(flat(best_a)))
                dve.tensor_copy(flat(best_bf), as_int(flat(best_b)))
                dve.drain()
                for n, at in enumerate((best_af, best_bf)):
                    for tt in range(TT):
                        dve.tensor_tensor(pick[:, tt, :, :], spread(at[:, tt, :], TOPK),
                                          C("iota", 0, TOPK).unsqueeze(1).broadcast_to([P, TOPK, TOPK]), ALU.is_equal)
                    dve.drain()
                    for tt in range(TT):
                        dve.tensor_tensor(pick[:, tt, :, :], pick[:, tt, :, :],
                                          top_f[:, 2 * tt + n, :].unsqueeze(1).broadcast_to([P, TOPK, TOPK]), ALU.mult)
                    dve.drain()
                    dve.reduce_sum(choice[:, n, :, bass.ds(TOPK * i, TOPK)], pick, AX.X)
                    dve.drain()
                dve.wait_ge(S("gate_exp"), i + 1)
                dve.reduce_sum(gate_sum[:, 0, :], gate, AX.X)
                dve.drain()
                dve.reciprocal(gate_sum[:, 1, :], gate_sum[:, 0, :])
                dve.drain()
                dve.tensor_tensor(choice[:, 2, :, bass.ds(TOPK * i, TOPK)], gate, spread(gate_sum[:, 1, :], TOPK), ALU.mult)
                dve.drain()
            dve.sem_inc(S("chosen"), 1)
            dve.wait_ge(S("choice_turned"), 1)
            for k in range(3):
                ins = dve.tensor_copy(choice_t[:, k, :], ROT[k][:, 0:T])
            ins.then_inc(S("choice_ready"), 1)
            dve.drain()
            with dve.Fori(0, T // 8) as i:
                for g in range(2):
                    dve.wait_ge(S("gates_done"), 2 * i + g + 1)
                    for t in range(4):
                        tok = bass.ds(8 * i + 4 * g + t, 1)
                        dve.tensor_scalar(one_a[:, g, t, :], C("iota"), choice_t[:, 0, tok], choice_t[:, 2, tok],
                                          ALU.is_equal, ALU.mult)
                        ins = dve.tensor_scalar(one_b[:, g, t, :], C("iota"), choice_t[:, 1, tok], None, ALU.is_equal)
                    ins.then_inc(S("one_hot"), 1)
            with dve.Fori(0, NKEYS // 4) as i:
                for b in range(4):
                    dve.wait_ge(S("gelu_out"), 4 * i + b + 5)
                    old = 2 * ((b + 2) % 4) + 1
                    dve.wait_ge(freed[old], use("peer", old, i) + (2 if b >= 2 else 1))
                    dve.tensor_tensor(gated_buf[:, b % 2, :], gelu_buf[:, b % 2, :], gates_of[:, bass.ds(4 * i + b, 1), :],
                                      ALU.mult).then_inc(S("gated"), 1)
            multiplied(dve, 7, "peer", NKEYS // 4 - 1)
            update_h(dve, 1.0)

        SYNC["peer"], TENSOR["peer"], SCALAR["peer"], VECTOR["peer"] = peer_sync, peer_tensor, peer_scalar, peer_vector
        block = ctx.enter_context(nc.Block())

        @block.sync
        def _(sp):
            sp.dma_start(con[:, :], io["consts"]).then_inc(S("in_loaded"), 16)
            sp.dma_start(vec[:, :], io["vecs"]).then_inc(S("in_loaded"), 16)
            sp.dma_start(h[:, :, :], io["x"].rearrange("(a p) d -> p a d", p=P)).then_inc(S("h_loaded"), 16)
            for s in stages:
                if s.startswith("ffn"):
                    ffn_sync(sp, int(s[3]))
                elif s in SYNC:
                    SYNC[s](sp)
            sp.wait_ge(S("h_updated"), 4 * len(sums) + 1)
            sp.dma_start(io["out"].rearrange("(a p) d -> p a d", p=P), h[:, :, :]).then_inc(S("out_stored"), 16)
            sp.wait_ge(S("out_stored"), 16)

        @block.gpsimd
        def _(pool):
            pool.memset(zeros[:, :], 0.0).then_inc(S("pool_setup"), 1)
            pool.wait_ge(S("pool_setup"), 1)
            for sem, n in [(f, 1) for f in freed] + [(S("hid_ready"), 2), (S("h_updated"), 1), (S("ssm_evicted"), 4), (S("y_taken"), 1),
                                                   (S("scored"), 4), (S("p_turned_out"), 2), (S("o_ready"), 1), (S("rw_evicted"), 7),
                                                   (S("mo_ready"), 1), (S("mp_out"), 1), (S("pq_out"), 2), (S("score_out"), 1),
                                                   (S("gates_out"), 2), (S("gates_done"), 2), (S("one_hot"), 2),
                                                   (S("gelu_out"), 4), (S("gated"), 2)]:
                pool.sem_inc(sem, n)
            for s in stages:
                if s in POOL:
                    POOL[s](pool)

        @block.scalar
        def _(act):
            act.wait_ge(S("stat_ready"), 1)
            for s in stages:
                if s in norm_no:
                    norm_scalar(act, norm_no[s], upd[s])
                if s.startswith("ffn"):
                    ffn_scalar(act, int(s[3]))
                elif s in SCALAR:
                    SCALAR[s](act)

        @block.vector
        def _(dve):
            dve.memset(stat[:, 14:15], EPS)
            dve.memset(stat[:, 15:16], LN_EPS).then_inc(S("stat_ready"), 1)
            dve.wait_ge(S("in_loaded"), 32)
            for s in stages:
                if s in norm_no:
                    norm_vector(dve, norm_no[s], GAIN[s])
                if s.startswith("ffn"):
                    ffn_vector(dve, int(s[3]))
                elif s in VECTOR:
                    VECTOR[s](dve)

        @block.tensor
        def _(pe):
            pe.wait_ge(S("in_loaded"), 32)
            for s in stages:
                if s in norm_no:
                    norm_tensor(pe, norm_no[s])
                if s.startswith("ffn"):
                    ffn_tensor(pe, int(s[3]), upd[s])
                elif s in TENSOR:
                    TENSOR[s](pe)


def pack(x):
    def cols(v):
        v = np.asarray(v).reshape(-1)
        return v.reshape(-1, P).T

    def pad(v):
        v = np.asarray(v).reshape(-1)
        return np.concatenate([v, np.zeros(P - len(v), v.dtype)]).reshape(P, 1)

    inner = GROUPS * GI
    order = []
    for g in range(GROUPS):
        order += [inner + g * P, inner + GROUPS * P + g * P] + [g * GI + k * P for k in range(4)]
    conv_w, conv_b = x["ssm_conv_w"][0], x["ssm_conv_b"][0]
    ffn_norm = x["ffn_norm"].reshape(4, D)
    v = {
        "g_ffn0": cols(ffn_norm[0]), "g_ffn1": cols(ffn_norm[1]), "g_ffn2": cols(ffn_norm[2]),
        "g_ffn3": cols(ffn_norm[3]), "g_ssm": cols(x["ssm_norm"]), "g_kv": cols(x["kv_norm"]),
        "g_attn": cols(x["attn_norm"]), "g_mix": cols(x["g_mix_2"]), "g_peer": cols(x["g_ffn_2"]),
        "conv_w": np.concatenate([conv_w[:, o:o + P].T for o in order], 1),
        "conv_b": np.stack([conv_b[o:o + P] for o in order], 1),
        "d_skip": cols(np.repeat(x["ssm_d"][0], HD)), "g_gate": cols(x["ssm_gate_norm"]),
        "dt_bias": pad(x["ssm_dt_bias"]), "a_log": pad(x["ssm_a_log"]),
        "k_norm": np.tile(x["k_norm"], 2)[:, None], "q_norm": np.tile(x["q_norm"][0], 2)[:, None],
        "sinks": np.tile(x["sinks"], (P, 1)),
        "g_cq": cols(x["g_cq_2"]), "g_ckv": cols(x["g_ckv_2"]),
        "g_qnorm": pad(x["g_qnorm_2"]), "g_knorm": pad(x["g_knorm_2"]), "g_out": cols(x["g_attn_out_2"]),
        "mu": cols(x["rwkv_mu_2"]), "w0": cols(x["w0_2"]), "a0": cols(x["a0_2"]), "k_k": cols(x["k_k_2"]),
        "k_a": cols(x["k_a_2"]), "r_k": cols(x["r_k_2"]), "lnw": cols(x["ln_x_w_2"]), "lnb": cols(x["ln_x_b_2"]),
    }
    for name, (_, n) in VECS.items():
        assert v[name].shape == (P, n), (name, v[name].shape)
    w_in = x["ssm_w_in"][0]
    xbc = tiles(w_in[:, inner:inner + inner + 2 * GROUPS * P])
    z = tiles(w_in[:, 0:inner])
    group_tiles = np.stack([
        np.concatenate([xbc[[16 + g, 20 + g] + [4 * g + k for k in range(4)]], z[4 * g:4 * g + 4]])
        for g in range(GROUPS)])
    w_kv = x["w_kv"]
    kv = np.concatenate([w_kv[:, 0:64], w_kv[:, 0:64], w_kv[:, 64:128], w_kv[:, 64:128], w_kv[:, 128:256]], 1)
    w_in2 = x["w_in_2"][0]
    rope_cols = np.concatenate([w_in2[:, 0:MLA_Q + MLA_KV], np.zeros((D, NOPE), np.float32),
                                w_in2[:, MLA_Q + MLA_KV:MLA_Q + MLA_KV + ROPE], np.zeros((D, ROPE), np.float32)], 1)
    uq = x["w_uq_2"][0].reshape(3, P, PH, QK).transpose(2, 1, 0, 3).reshape(PH, P, 3 * QK)
    uk = x["w_uk_2"][0].reshape(2, P, PH, NOPE).transpose(2, 1, 0, 3)
    uk = np.concatenate([uk, np.zeros((PH, P, 2, ROPE), uk.dtype)], 3).reshape(PH, P, 2 * QK)
    uv = x["w_uv_2"][0].reshape(2, P, 4, P).transpose(2, 1, 0, 3).reshape(4, P, 2 * P)
    return {
        "x": x["x"][0], "positions": x["positions_2"].reshape(1, T), "consts": constants(),
        "vecs": np.concatenate([v[name] for name in VECS], 1),
        "w1": np.stack([tiles(w) for w in x["ffn_w1"].reshape(4, D, FF)]),
        "w3": np.stack([tiles(w) for w in x["ffn_w3"].reshape(4, D, FF)]),
        "w2": x["ffn_w2"].reshape(4, FC, P, D),
        "ssm_in": group_tiles, "ssm_dt": tiles(w_in[:, 5120:5152], 32)[0],
        "ssm_out": x["ssm_w_out"].reshape(GROUPS, 4, P, D),
        "w_kv": tiles(kv), "w_q": tiles(x["w_q"][0]), "w_o": x["w_o"].reshape(8, P, D),
        "rel_bias": x["rel_bias"],
        "mla_in": tiles(rope_cols), "rwkv_in": tiles(w_in2[:, 672:]),
        "mla_u": np.concatenate([
            uq.reshape(4, 2, P, 3 * QK).transpose(0, 2, 1, 3).reshape(4, P, 6 * QK),
            uk.reshape(4, 2, P, 2 * QK).transpose(0, 2, 1, 3).reshape(4, P, 4 * QK)], 2),
        "mla_uv": uv,
        "w_wa": np.concatenate([x["w2_2"][0], x["a2_2"][0]], 0), "w_g": x["g2_2"][0],
        "w_o2": x["w_o_2"].reshape(8, P, D),
        "w_pq": tiles(x["w_pq_2"][0]),
        "keys": x["sub_keys_2"][0].transpose(0, 3, 1, 2).reshape(PH, P, 2 * NKEYS),
        "expert_u": x["expert_u_2"][0].reshape(NKEYS, NKEYS, DC, P).transpose(0, 3, 2, 1).reshape(NKEYS, P, D),
        "expert_v": x["expert_v_2"][0].reshape(NKEYS, NKEYS, D),
    }


def kernel(**inputs):
    import concourse.bacc as bacc
    from concourse.bass_utils import run_bass_kernel_spmd

    nc = bacc.Bacc("TRN2", target_bir_lowering=False, num_devices=1)
    arrays = {f"in_{k}": np.ascontiguousarray(v) for k, v in pack({k: np.asarray(v) for k, v in inputs.items()}).items()}
    io = {k[3:]: nc.dram_tensor(k, a.shape, mybir.dt.from_np(a.dtype), kind="ExternalInput").ap()
          for k, a in arrays.items()}
    io["out"] = nc.dram_tensor("out", (T, D), F32, kind="ExternalOutput").ap()
    program(nc, io)
    r = run_bass_kernel_spmd(nc, [arrays], core_ids=[0])
    return r.results[0]["out"].reshape(1, T, D)
```

```python
import math
from contextlib import ExitStack

import numpy as np

import concourse.bass as bass
from concourse import mybir

F32 = mybir.dt.float32
F32R = mybir.dt.float32r
BF16 = mybir.dt.bfloat16
I32 = mybir.dt.int32
U32 = mybir.dt.uint32
ALU = mybir.AluOpType
ACT = mybir.ActivationFunctionType
AX = mybir.AxisListType

P = 128
T = 256
TT = T // P
D = 1024
DC = D // P
FF = 2816
FC = FF // P
EPS = 1e-6
NEG = -1e30
GROUPS = 4
GHEADS = 8
HD = 64
GI = GHEADS * HD
CONV = 4
WINDOW = 128
BUCKETS = 32
MAX_DIST = WINDOW
MLA_Q, MLA_KV, ROPE, NOPE = 384, 256, 32, 64
QK = ROPE + NOPE
THETA = 10000.0
LN_EPS = 64e-5
RC = 4
CH = T // RC
PH = 8
TOPK = 16
NKEYS = 128
SLOTS = 4



def layout(items):
    at, out = 0, {}
    for name, n in items:
        out[name] = (at, n)
        at += n
    return out, at


CONSTS, N_CONSTS = layout([
    ("ident", P), ("ones", P), ("blk64", P), ("causal", 384), ("mla_mask", 384),
    ("up_strict", CH), ("up_incl", CH), ("low_strict", CH),
    ("u16", P), ("l16", P), ("u32", P), ("l32", P), ("l64", P),
    ("iota", P), ("rot", QK), ("onehot", 384), ("outside", 384), ("half", 1),
    ("inv_freq", 1), ("is_rope", 1), ("not_rope", 1),
])


def constants():
    c = np.zeros((P, N_CONSTS), np.float32)

    def put(name, a):
        at, n = CONSTS[name]
        a = np.asarray(a, np.float32).reshape(a.shape[0], n)
        c[:a.shape[0], at:at + n] = a

    i = np.arange(P)
    put("ident", np.eye(P))
    put("ones", np.ones((P, P)))
    same = (i[:, None] // HD) == (i[None, :] // HD)
    put("blk64", same)
    late = i[None, :] >= i[:, None]
    put("causal", np.concatenate([late, np.ones((P, P)), late], 1))
    tok = np.arange(T)
    mask = np.stack([np.where(tok[None, :] // 64 <= (b * P + i)[:, None] // 64, 0, NEG) for b in range(TT)], 1)
    put("mla_mask", np.concatenate([mask[:, 0, 0:P], mask[:, 1, :]], 1))
    r, t = (i % CH)[:, None], np.arange(CH)[None, :]
    put("up_strict", r < t)
    put("up_incl", r <= t)
    put("low_strict", r > t)
    a, b = i[:, None], i[None, :]
    for n, lo in ((16, 1), (32, 16), (64, 32)):
        level = (a // n == b // n) & ((a // lo != b // lo) if lo > 1 else True) & (a < b)
        put(f"l{n}", level.T)
        if n < 64:
            put(f"u{n}", level)
    put("iota", np.tile(np.arange(P), (P, 1)))
    half = ROPE // 2
    rot = np.zeros((QK, QK))
    for j in range(half):
        rot[NOPE + half + j, NOPE + j] = -1
        rot[NOPE + j, NOPE + half + j] = 1
    put("rot", rot)
    y = np.arange(384)
    dist = 255 - y
    inside = (dist >= 0) & (dist < WINDOW)
    exact = BUCKETS // 2
    nf = np.maximum(dist, 1).astype(np.float32)
    large = exact + (np.log(nf / np.float32(exact)) / np.float32(math.log(MAX_DIST / exact))
                     * np.float32(BUCKETS - exact)).astype(np.int32)
    bucket = np.where(np.maximum(dist, 0) < exact, np.maximum(dist, 0), np.minimum(large, BUCKETS - 1))
    put("onehot", (np.arange(BUCKETS)[:, None] == bucket[None, :]) & inside[None, :])
    put("outside", np.tile(np.where(inside, 0, NEG), (P, 1)))
    put("half", np.full((P, 1), math.pi / 2))
    inv = (np.float32(THETA) ** (-np.arange(half, dtype=np.float32) / np.float32(half))).astype(np.float32)
    put("inv_freq", np.concatenate([np.zeros(NOPE), inv, inv])[:, None])
    put("is_rope", (np.arange(QK) >= NOPE)[:, None])
    put("not_rope", (np.arange(QK) < NOPE)[:, None])
    return c


VECS, N_VECS = layout([
    ("g_ffn0", DC), ("g_ffn1", DC), ("g_ffn2", DC), ("g_ffn3", DC), ("g_ssm", DC), ("g_kv", DC),
    ("g_attn", DC), ("g_mix", DC), ("g_peer", DC),
    ("conv_w", GROUPS * 6 * CONV), ("conv_b", GROUPS * 6), ("d_skip", GROUPS * 4), ("g_gate", GROUPS * 4),
    ("dt_bias", 1), ("a_log", 1), ("k_norm", 1), ("q_norm", 1), ("sinks", 16),
    ("g_cq", 3), ("g_ckv", 2), ("g_qnorm", 1), ("g_knorm", 1), ("g_out", 4),
    ("mu", 14), ("w0", 4), ("a0", 4), ("k_k", 4), ("k_a", 4), ("r_k", 4), ("lnw", 4), ("lnb", 4),
])


def tiles(w, width=P):
    k, n = w.shape[0] // P, w.shape[1] // width
    return w.reshape(k, P, n, width).transpose(2, 1, 0, 3).reshape(n, P, k * width)


RING_PLAN = {
    "ffn0": (FC, [1, 1, 1, 0]), "ffn1": (FC, [1, 1, 1, 0]), "ffn2": (FC, [1, 1, 1, 0]), "ffn3": (FC, [1, 1, 1, 0]),
    "dt": (1, [1, 0, 0, 0]),
    "ssm": (GROUPS, [4, 4, 3, 3]),
    "kv": (1, [1, 1, 1, 0]),
    "attn": (4, [1, 1, 1, 1]),
    "rwkv": (2, [2, 2, 2, 1]),
    "rwkv_out": (1, [1, 1, 1, 1]),
    "mla": (1, [2, 2, 1, 1]),
    "mla_heads": (4, [1, 1, 0, 0]),
    "route": (PH, [1, 1, 0, 0]),
    "peer": (NKEYS // 2, [1, 1, 1, 1]),
}
SPLIT_STAGES = ("ffn0", "ffn1", "ffn2", "ffn3", "peer")
RING_OF = {"ssm": ("dt", "ssm"), "rwkv": ("rwkv", "rwkv_out"), "mla": ("mla", "mla_heads"), "mix": (),
           "peer": ("route", "peer")}
STAGES = ["ffn0", "ssm", "ffn1", "kv", "ffn2", "attn", "ffn3", "rwkv", "mla", "mix", "peer"]


def program(nc, io, stages=STAGES):
    norm_no = {s: n for n, s in enumerate([s for s in stages if s not in ("mla", "mix")])}
    sums = [s for s in stages if s not in ("kv", "rwkv", "mla")]
    upd = {s: len([x for x in stages[:stages.index(s)] if x in sums]) for s in stages}
    ffn_no = {s: n for n, s in enumerate([s for s in stages if s.startswith("ffn")])}
    split_norms = {norm_no[s]: len([x for x in SPLIT_STAGES if x in stages and norm_no[x] < norm_no[s]]) for s in norm_no}
    ring_order = [r for s in stages for r in RING_OF.get(s, (s,))]

    def use(stage, slot, i=0, nth=0):
        before = sum(RING_PLAN[r][0] * RING_PLAN[r][1][slot] for r in ring_order[:ring_order.index(stage)])
        return before + nth + i * RING_PLAN[stage][1][slot]

    def use_split(stage, slot, i=0):
        order = [r for r in ring_order if r in SPLIT_STAGES]
        before = sum(RING_PLAN[r][0] * RING_PLAN[r][1][slot] for r in order[:order.index(stage)])
        return before + i * RING_PLAN[stage][1][slot]

    ctx = ExitStack()
    sems = {}

    def S(name):
        if name not in sems:
            sems[name] = ctx.enter_context(nc.semaphore(name))
        return sems[name]

    def sb(name, shape, dt=F32):
        return ctx.enter_context(nc.sbuf_tensor(name, shape, dt))

    with ctx:
        con = sb("con", [P, N_CONSTS])
        vec = sb("vec", [P, N_VECS])
        h = sb("h", [P, TT, D])
        u_t = sb("u_t", [P, DC, T])
        ring = [sb(f"ring{s}", [P, D]) for s in range(SLOTS)]
        w_hi = [sb(f"w_hi{s}", [P, D], F32R) for s in range(SLOTS)]
        w_lo = [sb(f"w_lo{s}", [P, D], F32R) for s in range(SLOTS)]
        u_hi, u_lo = sb("u_hi", [P, DC, T], F32R), sb("u_lo", [P, DC, T], F32R)
        x_hi, x_lo = sb("x_hi", [P, 2, T], F32R), sb("x_lo", [P, 2, T], F32R)
        zeros = sb("zeros", [P, 512], BF16)
        stat = sb("stat", [P, 16])
        credit = sb("credit", [P, 1])
        arena = sb("arena", [P, 28128])
        bank = [ctx.enter_context(nc.psum_tensor(f"bank{i}", [P, 512], F32)) for i in range(8)]
        ACC = bank[0:4]
        UP = bank[4:6]
        TP = bank[6:8]
        ROT = bank[4:8]

        def C(name, a=0, b=None):
            at, n = CONSTS[name]
            return con[:, at + a:at + (n if b is None else b)]

        def V(name, a=0, b=None):
            at, n = VECS[name]
            return vec[:, at + a:at + (n if b is None else b)]

        def VD(name, start, n=1):
            return vec[:, bass.ds(VECS[name][0] + start, n)]

        def area(at, *shape):
            n = int(np.prod(shape))
            a = arena[:, at:at + n]
            if len(shape) == 2:
                a = a.rearrange("p (a b) -> p a b", a=shape[0])
            if len(shape) == 3:
                a = a.rearrange("p (a b c) -> p a b c", a=shape[0], b=shape[1])
            return a

        def spread(col, n):
            return col.unsqueeze(2).broadcast_to([col.shape[0], col.shape[1], n])

        full = [S(f"slot_full{s}") for s in range(SLOTS)]
        freed = [S(f"slot_freed{s}") for s in range(SLOTS)]
        hi_made = [S(f"hi_made{s}") for s in range(SLOTS)]
        split_read = [S(f"split_read{s}") for s in range(SLOTS)]

        def load(sp, slot, src, stage, i=0, nth=0):
            sp.wait_ge(freed[slot], use(stage, slot, i, nth) + 1)
            sp.dma_start(ring[slot][:, 0:src.shape[-1]], src).then_inc(full[slot], 16)

        def arrived(pe, slot, stage, i=0, nth=0):
            pe.wait_ge(full[slot], (use(stage, slot, i, nth) + 1) * 16)

        def multiplied(eng, slot, stage, i=0, nth=0):
            eng.wait_ge(freed[slot], use(stage, slot, i, nth) + 2)

        def make_hi(act, slot, stage, i):
            act.wait_ge(full[slot], (use(stage, slot, i) + 1) * 16)
            act.wait_ge(split_read[slot], use_split(stage, slot, i) + 1)
            act.activation(w_hi[slot][:, :], ring[slot][:, :], ACT.Copy).then_inc(hi_made[slot], 1)

        def make_lo(dve, slot, stage, i):
            dve.wait_ge(hi_made[slot], use_split(stage, slot, i) + 1)
            dve.tensor_tensor(w_lo[slot][:, :], ring[slot][:, :], w_hi[slot][:, :].bitcast(F32),
                              ALU.subtract).then_inc(freed[slot], 1)

        def split_done(eng, slot, stage, i):
            eng.wait_ge(split_read[slot], use_split(stage, slot, i) + 2)

        def passes(pe, out, left, right, start, stop):
            for n, (a, b) in enumerate(((0, 0), (0, 1), (1, 0))):
                mm = pe.matmul(out, left[a], right[b], start=start and n == 0, stop=stop and n == 2,
                               skip_group_check=True)
            return mm

        def project_split(pe, out, slot, stage, i):
            multiplied(pe, slot, stage, i)
            for c in range(DC):
                cols = slice(c * P, (c + 1) * P)
                mm = passes(pe, out, (w_hi[slot][:, cols], w_lo[slot][:, cols]), (u_hi[:, c, :], u_lo[:, c, :]),
                            c == 0, c == DC - 1)
            return mm.then_inc(split_read[slot], 1)

        def close_split(pe, b, slot, stage, i, last=False):
            multiplied(pe, slot, stage, i)
            for q in range(4):
                rows, cols = slice((q // 2) * P, (q // 2 + 1) * P), slice((q % 2) * 512, (q % 2 + 1) * 512)
                mm = passes(pe, ACC[q][:, :], (x_hi[:, b, rows], x_lo[:, b, rows]),
                            (w_hi[slot][:, cols], w_lo[slot][:, cols]), False, last)
            return mm.then_inc(split_read[slot], 1)

        def project(pe, out, slot, width=P):
            for c in range(DC):
                mm = pe.matmul(out, ring[slot][:, c * width:(c + 1) * width], u_t[:, c, :],
                               start=(c == 0), stop=(c == DC - 1))
            return mm

        def close_into(pe, left, right, last=False):
            for q in range(4):
                mm = pe.matmul(ACC[q][:, :], left[:, (q // 2) * P:(q // 2 + 1) * P],
                               right[:, (q % 2) * 512:(q % 2 + 1) * 512],
                               start=False, stop=last, skip_group_check=True)
            return mm

        def clear_acc(pe, updates):
            pe.wait_ge(S("h_updated"), 4 * updates + 1)
            for q in range(4):
                pe.matmul(ACC[q][:, :], zeros[:, 0:P], zeros[:, :], start=True, stop=False,
                          skip_group_check=True)

        norm_square = area(0, 2, D)
        norm_u = area(2 * D, 2, D)

        def norm_scalar(act, m, updates, split):
            act.wait_ge(S("h_loaded"), 16)
            act.wait_ge(S("in_loaded"), 32)
            for tt in range(TT):
                act.wait_ge(S("h_updated"), max(4 * updates - 2 + 2 * tt + 1, 1))
                act.activation(norm_square[:, tt, :], h[:, tt, :], ACT.Square, accum_out=stat[:, tt:tt + 1])
                act.drain()
                act.activation(stat[:, 2 + tt:3 + tt], stat[:, tt:tt + 1], ACT.Sqrt, scale=1.0 / D,
                               bias=stat[:, 14:15]).then_inc(S("norm_root"), 1)
            if split:
                for q in range(4):
                    act.wait_ge(S("u_ready"), 4 * m + q + 1)
                    act.activation(quarter(u_hi, q), quarter(u_t, q), ACT.Copy).then_inc(S("u_hi_made"), 1)

        def quarter(u, q):
            return u[:, 4 * (q % 2):4 * (q % 2) + 4, (q // 2) * P:(q // 2 + 1) * P]

        def norm_vector(dve, m, gain, split):
            def lo(q):
                dve.wait_ge(S("u_hi_made"), 4 * split_norms[m] + q + 1)
                dve.tensor_tensor(quarter(u_lo, q), quarter(u_t, q), quarter(u_hi, q).bitcast(F32),
                                  ALU.subtract).then_inc(S("u_split"), 1)

            for tt in range(TT):
                dve.wait_ge(S("norm_root"), 2 * m + tt + 1)
                dve.reciprocal(stat[:, 4 + tt:5 + tt], stat[:, 2 + tt:3 + tt])
                dve.drain()
                dve.tensor_scalar(norm_u[:, tt, :], h[:, tt, :], stat[:, 4 + tt:5 + tt], None,
                                  ALU.mult).then_inc(S("norm_rows"), 1)
            for q in range(4):
                half = q % 2
                dve.wait_ge(S("norm_turned"), 4 * m + q + 1)
                dve.tensor_tensor(quarter(u_t, q), TP[q % 2][:, :].rearrange("p (c t) -> p c t", c=4),
                                  spread(V(gain, 4 * half, 4 * half + 4), P), ALU.mult).then_inc(S("u_ready"), 1)
                if split and q:
                    lo(q - 1)
            if split:
                lo(3)

        def norm_tensor(pe, m, split):
            for q in range(4):
                tt, half = q // 2, q % 2
                pe.wait_ge(S("norm_rows"), 2 * m + tt + 1)
                if q >= 2:
                    pe.wait_ge(S("u_ready"), 4 * m + q - 1)
                for c in range(4):
                    at = (4 * half + c) * P
                    mm = pe.transpose(TP[q % 2][:, c * P:(c + 1) * P], norm_u[:, tt, at:at + P], C("ident"))
                mm.then_inc(S("norm_turned"), 1)
            if split:
                pe.wait_ge(S("u_split"), 4 * split_norms[m] + 4)
            else:
                pe.wait_ge(S("u_ready"), 4 * m + 4)

        def update_h(dve, scale):
            for q in range(4):
                part = h[:, q // 2, (q % 2) * 512:(q % 2 + 1) * 512]
                dve.scalar_tensor_tensor(part, ACC[q][:, :], scale, part, ALU.mult,
                                         ALU.add).then_inc(S("h_updated"), 1)

        silu_buf = area(4 * D, 2, T)
        hid_buf = area(4 * D + 2 * T, 2, T)

        def ffn_sync(sp, k):
            for slot, j in ((0, 0), (1, 0), (2, 0), (0, 1), (1, 1)):
                load(sp, slot, io[("w1", "w3", "w2")[slot]][k, j, :, :], f"ffn{k}", j)
            with sp.Fori(0, FC - 2) as j:
                for slot, ahead in ((0, 2), (1, 2), (2, 1)):
                    load(sp, slot, io[("w1", "w3", "w2")[slot]][k, bass.ds(j + ahead, 1), :, :], f"ffn{k}", j + ahead)
            load(sp, 2, io["w2"][k, FC - 1, :, :], f"ffn{k}", FC - 1)

        def ffn_tensor(pe, k, updates):
            stage = f"ffn{k}"
            base = FC * ffn_no[stage]

            def up(b, j):
                pe.wait_ge(S("hid_ready"), base + j + 1)
                for n in range(2):
                    project_split(pe, UP[b][:, n * T:(n + 1) * T], n, stage, j)

            def down(b, j, last=False):
                pe.wait_ge(S("hid_ready"), base + j + 3)
                close_split(pe, b, 2, stage, j, last)

            clear_acc(pe, updates)
            up(0, 0)
            with pe.Fori(0, FC // 2 - 1) as i:
                up(1, 2 * i + 1)
                down(0, 2 * i)
                up(0, 2 * i + 2)
                down(1, 2 * i + 1)
            up(1, FC - 1)
            down(0, FC - 2)
            down(1, FC - 1, last=True)

        def ffn_scalar(act, k):
            stage = f"ffn{k}"

            def silu(b, j):
                split_done(act, 1, stage, j)
                act.activation(silu_buf[:, b, :], UP[b][:, 0:T], ACT.Silu).then_inc(S("silu_ready"), 1)

            for slot, j in ((0, 0), (1, 0), (2, 0), (0, 1), (1, 1)):
                make_hi(act, slot, stage, j)
            with act.Fori(0, FC // 2 - 1) as i:
                for b in range(2):
                    silu(b, 2 * i + b)
                    for slot, ahead in ((0, 2), (1, 2), (2, 1)):
                        make_hi(act, slot, stage, 2 * i + b + ahead)
            silu(0, FC - 2)
            make_hi(act, 2, stage, FC - 1)
            silu(1, FC - 1)

        def ffn_vector(dve, k):
            stage = f"ffn{k}"
            base = FC * ffn_no[stage]

            def gate(b, j):
                dve.wait_ge(S("silu_ready"), base + j + 1)
                dve.wait_ge(split_read[2], use_split(stage, 2, j))
                dve.tensor_tensor(x_hi[:, b, :], silu_buf[:, b, :], UP[b][:, T:2 * T], ALU.mult)
                dve.tensor_tensor(hid_buf[:, b, :], silu_buf[:, b, :], UP[b][:, T:2 * T], ALU.mult)
                dve.drain()
                dve.tensor_tensor(x_lo[:, b, :], hid_buf[:, b, :], x_hi[:, b, :].bitcast(F32),
                                  ALU.subtract).then_inc(S("hid_ready"), 1)

            for slot, j in ((0, 0), (1, 0), (2, 0), (0, 1), (1, 1)):
                make_lo(dve, slot, stage, j)
            with dve.Fori(0, FC // 2 - 1) as i:
                for b in range(2):
                    gate(b, 2 * i + b)
                    for slot, ahead in ((0, 2), (1, 2), (2, 1)):
                        make_lo(dve, slot, stage, 2 * i + b + ahead)
            gate(0, FC - 2)
            make_lo(dve, 2, stage, FC - 1)
            gate(1, FC - 1)
            split_done(dve, 2, stage, FC - 1)
            update_h(dve, 0.5)

        GAIN = {"ffn0": "g_ffn0", "ssm": "g_ssm", "ffn1": "g_ffn1", "kv": "g_kv", "ffn2": "g_ffn2", "attn": "g_attn",
                "ffn3": "g_ffn3", "rwkv": "g_mix", "peer": "g_peer"}
        SYNC, POOL, SCALAR, VECTOR, TENSOR = {}, {}, {}, {}, {}

        x_pad = area(4096, 6, 260)
        conv = area(5696, 6, T)
        z_act = area(7232, 4, T)
        xdt = area(8256, TT, GI)
        cb = area(9280, 384)
        decay = area(9664, GHEADS, 384)
        y_grp = area(12736, 4, T)
        y_sq = area(13760, 4, T)
        y_out = area(14784, 4, T)
        y_root = area(15808, 2, T)
        acum_all = area(16384, 4 * GHEADS, T)
        dt_work = area(24576, 5, T)
        dt_cols = area(25856, 4, 32)
        acum_dram = nc.dram_tensor("acum_dram", (32, T), F32, kind="Internal").ap()
        H32 = slice(0, 32)

        def ssm_sync(sp):
            load(sp, 0, io["ssm_dt"], "dt")
            sp.wait_ge(S("acum_ready"), 1)
            sp.dma_start(acum_dram, dt_work[H32, 4, :]).then_inc(S("acum_stored"), 16)
            sp.wait_ge(S("acum_stored"), 16)
            sp.dma_start(acum_all[:, :, :], acum_dram.unsqueeze(0).broadcast_to([P, 32, T])).then_inc(S("acum_spread"), 16)
            with sp.Fori(0, GROUPS) as i:
                for n in range(14):
                    src = io["ssm_in"][bass.ds(i, 1), n, :, :] if n < 10 else io["ssm_out"][bass.ds(i, 1), n - 10, :, :]
                    load(sp, n % 4, src, "ssm", i, n // 4)

        def ssm_tensor(pe):
            arrived(pe, 0, "dt")
            project(pe, UP[0][H32, 0:T], 0, 32).then_inc(freed[0], 1)
            clear_acc(pe, upd["ssm"])
            pe.wait_ge(S("acum_ready"), 1)
            for n in range(4):
                src = dt_work[H32, 4 if n < 2 else 2, (n % 2) * P:(n % 2 + 1) * P]
                mm = pe.transpose(TP[0][:, n * 32:(n + 1) * 32], src, C("ident", 0, 32)[H32, :])
            mm.then_inc(S("dt_turned"), 1)
            pe.wait_ge(S("dt_cols_ready"), 1)
            with pe.Fori(0, GROUPS) as i:
                pe.wait_ge(S("y_taken"), 4 * i + 1)
                for n in range(10):
                    arrived(pe, n % 4, "ssm", i, n // 4)
                    pe.wait_ge(S("ssm_evicted"), 10 * i + n + 1)
                    project(pe, ROT[n % 4][:, 0:T], n % 4).then_inc(freed[n % 4], 1)
                pe.wait_ge(S("ssm_evicted"), 10 * i + 14)
                pe.wait_ge(S("conv_act"), 6 * i + 6)
                for tt in range(TT):
                    for k in range(4):
                        mm = pe.transpose(TP[tt][:, k * P:(k + 1) * P], conv[:, 2 + k, tt * P:(tt + 1) * P], C("ident"))
                    mm.then_inc(S("x_turned"), 1)
                pe.wait_ge(S("xdt_ready"), 2 * i + 1)
                pe.matmul(TP[0][:, 0:T], conv[:, 0, 0:P], conv[:, 1, :], start=True, stop=True)
                pe.matmul(TP[0][:, T:384], conv[:, 0, P:T], conv[:, 1, P:T], start=True,
                          stop=True).then_inc(S("cb_done"), 1)
                pe.wait_ge(S("xdt_ready"), 2 * i + 2)
                for r in range(GHEADS):
                    pe.wait_ge(S("scores_ready"), 2 * i + r // 4 + 1)
                    k, a = r // 2, (r % 2) * HD
                    out = ROT[k][a:a + HD, 0:T]
                    pe.matmul(out, xdt[:, 0, r * HD:(r + 1) * HD], decay[:, r, 0:T], start=True, stop=False,
                              skip_group_check=True)
                    mm = pe.matmul(out[:, P:T], xdt[:, 1, r * HD:(r + 1) * HD], decay[:, r, T:384], start=False,
                                   stop=True, skip_group_check=True)
                    if r % 2:
                        mm.then_inc(S("y_done"), 1)
                pe.wait_ge(S("y_squared"), i + 1)
                for k in range(4):
                    mm = pe.matmul(TP[1][:, 0:T], C("ones"), y_sq[:, k, :], start=(k == 0), stop=(k == 3))
                mm.then_inc(S("y_summed"), 1)
                for k in range(4):
                    arrived(pe, (10 + k) % 4, "ssm", i, (10 + k) // 4)
                    pe.wait_ge(S("y_normed"), 4 * i + k + 1)
                    close_into(pe, y_out[:, k, :], ring[(10 + k) % 4]).then_inc(freed[(10 + k) % 4], 1)

        def ssm_scalar(act):
            act.wait_ge(S("dt_raw"), 1)
            act.activation(dt_work[H32, 1, :], dt_work[H32, 0, :], ACT.Abs)
            act.drain()
            act.activation(dt_work[H32, 1, :], dt_work[H32, 1, :], ACT.Exp, scale=-1.0)
            act.activation(stat[H32, 6:7], V("a_log")[H32, :], ACT.Exp)
            act.drain()
            act.activation(dt_work[H32, 1, :], dt_work[H32, 1, :], ACT.Ln, bias=C("ones", 0, 1)[H32, :]).then_inc(S("dt_log"), 1)
            act.wait_ge(S("dt_cols_ready"), 1)
            with act.Fori(0, GROUPS) as i:
                for n in range(10):
                    multiplied(act, n % 4, "ssm", i, n // 4)
                    src = ROT[n % 4][:, 0:T]
                    if n < 6:
                        act.activation(x_pad[:, n, CONV - 1:CONV - 1 + T], src, ACT.Copy).then_inc(S("ssm_evicted"), 1)
                    else:
                        act.activation(z_act[:, n - 6, :], src, ACT.Silu).then_inc(S("ssm_evicted"), 1)
                for n in range(6):
                    act.wait_ge(S("conv_done"), 6 * i + n + 1)
                    act.activation(conv[:, n, :], conv[:, n, :], ACT.Silu).then_inc(S("conv_act"), 1)
                for b in range(2):
                    act.wait_ge(S("decay_ready"), 2 * i + b + 1)
                    part = decay[:, 4 * b:4 * b + 4, :]
                    act.activation(part, part, ACT.Exp).then_inc(S("decay_exp"), 1)
                act.wait_ge(S("y_gated"), i + 1)
                act.activation(y_sq[:, :, :], y_grp[:, :, :], ACT.Square).then_inc(S("y_squared"), 1)
                act.wait_ge(S("y_summed"), i + 1)
                act.activation(y_root[:, 0, :], TP[1][:, 0:T], ACT.Sqrt, scale=1.0 / GI,
                               bias=stat[:, 14:15]).then_inc(S("y_rooted"), 1)

        def ssm_vector(dve):
            dve.memset(x_pad[:, :, 0:CONV - 1], 0.0)
            dve.memset(dt_work[H32, 3, :], 1.0)
            multiplied(dve, 0, "dt")
            dve.tensor_scalar(dt_work[H32, 0, :], UP[0][H32, 0:T], V("dt_bias")[H32, :], None,
                              ALU.add).then_inc(S("dt_raw"), 1)
            dve.drain()
            dve.tensor_scalar(dt_work[H32, 2, :], dt_work[H32, 0, :], 0.0, None, ALU.max)
            dve.wait_ge(S("dt_log"), 1)
            dve.drain()
            dve.tensor_tensor(dt_work[H32, 2, :], dt_work[H32, 2, :], dt_work[H32, 1, :], ALU.add)
            dve.drain()
            dve.tensor_scalar(dt_work[H32, 0, :], dt_work[H32, 2, :], stat[H32, 6:7], -1.0, ALU.mult, ALU.mult)
            dve.drain()
            dve.tensor_tensor_scan(dt_work[H32, 4, :], dt_work[H32, 3, :], dt_work[H32, 0, :], 0.0, ALU.mult,
                                   ALU.add).then_inc(S("acum_ready"), 1)
            dve.wait_ge(S("dt_turned"), 1)
            dve.tensor_copy(dt_cols[:, :, :], TP[0][:, 0:P].rearrange("p (a b) -> p a b", a=4)).then_inc(S("dt_cols_ready"), 1)
            dve.drain()
            dve.wait_ge(S("acum_spread"), 16)
            with dve.Fori(0, GROUPS) as i:
                for r in range(GHEADS):
                    row = acum_all[:, bass.ds(GHEADS * i + r, 1), :]
                    for tt in range(TT):
                        last = dve.tensor_scalar(decay[:, r:r + 1, 0:T] if tt == 0 else decay[:, r:r + 1, T:384],
                                                 row if tt == 0 else acum_all[:, bass.ds(GHEADS * i + r, 1), P:T],
                                                 dt_cols[:, tt, bass.ds(GHEADS * i + r, 1)], 0.0,
                                                 ALU.subtract, ALU.min)
                    if r % 4 == 3:
                        last.then_inc(S("decay_ready"), 1)
                for tiles_of in (range(0, 2), range(2, 6)):
                    for tap in range(CONV):
                        for n in tiles_of:
                            col = (i * 6 + n) * CONV + tap
                            if tap == 0:
                                dve.wait_ge(S("ssm_evicted"), 10 * i + n + 5)
                                dve.tensor_scalar(conv[:, n, :], x_pad[:, n, 0:T], VD("conv_w", col),
                                                  VD("conv_b", i * 6 + n), ALU.mult, ALU.add)
                            else:
                                ins = dve.scalar_tensor_tensor(conv[:, n, :], x_pad[:, n, tap:tap + T],
                                                               VD("conv_w", col), conv[:, n, :], ALU.mult, ALU.add)
                                if tap == CONV - 1:
                                    ins.then_inc(S("conv_done"), 1)
                        dve.drain()
                for tt in range(TT):
                    dve.wait_ge(S("x_turned"), 2 * i + tt + 1)
                    dt_of = dt_cols[:, 2 + tt, bass.ds(GHEADS * i, GHEADS)]
                    dve.tensor_tensor(xdt[:, tt, :].rearrange("p (r q) -> p r q", r=GHEADS),
                                      TP[tt][:, :].rearrange("p (r q) -> p r q", r=GHEADS),
                                      spread(dt_of, HD), ALU.mult).then_inc(S("xdt_ready"), 1)
                dve.wait_ge(S("cb_done"), i + 1)
                dve.tensor_tensor(cb[:, :], TP[0][:, 0:384], C("causal"), ALU.mult)
                dve.drain()
                for b in range(2):
                    dve.wait_ge(S("decay_exp"), 2 * i + b + 1)
                    part = decay[:, 4 * b:4 * b + 4, :]
                    dve.tensor_tensor(part, part, cb.unsqueeze(1).broadcast_to([P, 4, 384]),
                                      ALU.mult).then_inc(S("scores_ready"), 1)
                for k in range(4):
                    dve.wait_ge(S("y_done"), 4 * i + k + 1)
                    dve.scalar_tensor_tensor(y_grp[:, k, :], conv[:, 2 + k, :], VD("d_skip", 4 * i + k),
                                             ROT[k][:, 0:T], ALU.mult,
                                             ALU.add).then_inc(S("y_taken"), 1)
                dve.drain()
                dve.wait_ge(S("ssm_evicted"), 10 * i + 14)
                dve.tensor_tensor(y_grp[:, :, :], y_grp[:, :, :], z_act[:, :, :], ALU.mult).then_inc(S("y_gated"), 1)
                dve.wait_ge(S("y_rooted"), i + 1)
                dve.reciprocal(y_root[:, 1, :], y_root[:, 0, :])
                dve.drain()
                for k in range(4):
                    dve.scalar_tensor_tensor(y_out[:, k, :], y_grp[:, k, :], VD("g_gate", 4 * i + k),
                                             y_root[:, 1, :], ALU.mult, ALU.mult).then_inc(S("y_normed"), 1)
            multiplied(dve, 1, "ssm", GROUPS - 1, 3)
            update_h(dve, 1.0)

        SYNC["ssm"], TENSOR["ssm"], SCALAR["ssm"], VECTOR["ssm"] = ssm_sync, ssm_tensor, ssm_scalar, ssm_vector

        k_t = area(5200, 2, T)
        v_rows = area(5712, TT, P)
        k_sq = area(5968, 2, T)
        k_root = area(6480, 2, 2, T)
        rel = area(7504, 16)
        bias_line = area(7520, 384)
        bias_all = area(8192, 16, 384)
        line_dram = nc.dram_tensor("line_dram", (16, 384), F32, kind="Internal").ap()
        bias_dram = nc.dram_tensor("bias_dram", (16, P * 384), F32, kind="Internal").ap()

        def kv_sync(sp):
            sp.wait_ge(S("u_ready"), 4 * norm_no["kv"] + 1)
            sp.dma_start(rel[0:BUCKETS, :], io["rel_bias"]).then_inc(S("rel_loaded"), 16)
            for n in range(3):
                load(sp, n, io["w_kv"][n, :, :], "kv")
            sp.wait_ge(S("line_ready"), 1)
            sp.dma_start(line_dram, bias_line[0:16, :]).then_inc(S("line_stored"), 16)
            sp.wait_ge(S("line_stored"), 16)
            sp.dma_start(bias_all[:, :, :], line_dram.unsqueeze(0).broadcast_to([P, 16, 384])).then_inc(S("line_spread"), 16)
            sp.wait_ge(S("line_spread"), 16)
            sp.dma_start(bias_dram.rearrange("h (p y) -> p h y", p=P), bias_all[:, :, :]).then_inc(S("bias_stored"), 16)

        def kv_tensor(pe):
            for n in range(2):
                arrived(pe, n, "kv")
                project(pe, ROT[n][:, 0:T], n).then_inc(freed[n], 1)
            arrived(pe, 2, "kv")
            for tt in range(TT):
                for c in range(DC):
                    mm = pe.matmul(ROT[2][:, tt * P:(tt + 1) * P], u_t[:, c, tt * P:(tt + 1) * P],
                                   ring[2][:, c * P:(c + 1) * P], start=(c == 0), stop=(c == DC - 1))
            mm.then_inc(freed[2], 1)
            pe.wait_ge(S("rel_loaded"), 16)
            pe.matmul(ACC[0][0:16, 0:384], rel[0:BUCKETS, :], C("onehot")[0:BUCKETS, :], start=True,
                      stop=True).then_inc(S("line_done"), 1)
            pe.wait_ge(S("k_squared"), 2)
            pe.matmul(ROT[3][:, :], C("blk64"), k_sq.rearrange("p a b -> p (a b)"), start=True,
                      stop=True).then_inc(S("k_summed"), 1)

        def kv_scalar(act):
            for n in range(2):
                multiplied(act, n, "kv")
                act.activation(k_sq[:, n, :], ROT[n][:, 0:T], ACT.Square).then_inc(S("k_squared"), 1)
            act.wait_ge(S("k_summed"), 1)
            act.activation(k_root[:, 0, :, :], ROT[3][:, :].rearrange("p (a b) -> p a b", a=2), ACT.Sqrt,
                           scale=1.0 / HD, bias=stat[:, 14:15]).then_inc(S("k_rooted"), 1)

        def kv_vector(dve):
            dve.wait_ge(S("line_done"), 1)
            dve.tensor_tensor(bias_line[0:16, :], ACC[0][0:16, 0:384], C("outside")[0:16, :],
                              ALU.add).then_inc(S("line_ready"), 1)
            multiplied(dve, 2, "kv")
            dve.tensor_copy(v_rows[:, :, :], ROT[2][:, 0:T].rearrange("p (a b) -> p a b", a=TT))
            dve.wait_ge(S("k_rooted"), 1)
            dve.reciprocal(k_root[:, 1, :, :], k_root[:, 0, :, :])
            dve.drain()
            for n in range(2):
                dve.scalar_tensor_tensor(k_t[:, n, :], ROT[n][:, 0:T], V("k_norm"), k_root[:, 1, n, :],
                                         ALU.mult, ALU.mult).then_inc(S("k_ready"), 1)

        SYNC["kv"], TENSOR["kv"], SCALAR["kv"], VECTOR["kv"] = kv_sync, kv_tensor, kv_scalar, kv_vector

        at_sq = area(6400, 2, T)
        at_root = area(6912, 2, 2, T)
        q_t = area(7936, 2, T)
        bias_tile = area(8448, 2, 2, 384)
        prob = area(9984, 2, 2, 384)
        prob_t = area(11520, 2, 2, 384)
        o_t = area(13056, 2, T)
        at_stat = area(13568, 2, 6, 4)

        def attn_sync(sp):
            sp.wait_ge(S("bias_stored"), 16)
            sp.wait_ge(S("u_ready"), 4 * norm_no["attn"] + 1)
            with sp.Fori(0, 4) as i:
                for b in range(2):
                    load(sp, 2 * b, io["w_q"][bass.ds(2 * i + b, 1), :, :], "attn", i)
                    load(sp, 2 * b + 1, io["w_o"][bass.ds(2 * i + b, 1), :, :], "attn", i)
                    sp.wait_ge(S("scored"), 4 * i + 2 * b + 2)
                    for a in range(2):
                        table = bias_dram[bass.ds(4 * i + 2 * b + a, 1), 127:127 + P * 383].rearrange(
                            "h (q y) -> q (h y)", y=383)
                        sp.dma_start(bias_tile[:, b, a, 0:P], table[:, P:2 * P]).then_inc(S(f"bias_loaded{b}"), 16)
                        sp.dma_start(bias_tile[:, b, a, P:384], table[:, 0:2 * P]).then_inc(S(f"bias_loaded{b}"), 16)

        def attn_tensor(pe):
            clear_acc(pe, upd["attn"])
            pe.wait_ge(S("k_ready"), 2)
            for kv in range(2):
                with pe.Fori(0, 2) as ii:
                    i = 2 * kv + ii
                    for b in range(2):
                        j1 = 2 * i + b + 1
                        arrived(pe, 2 * b, "attn", i)
                        pe.wait_ge(S("p_turned_out"), 2 * j1)
                        project(pe, ROT[0][:, 0:T], 2 * b).then_inc(freed[2 * b], 1)
                        pe.wait_ge(S("q_squared"), j1)
                        pe.matmul(ROT[1][:, 0:T], C("blk64"), at_sq[:, b, :], start=True, stop=True).then_inc(S("q_summed"), 1)
                        pe.wait_ge(S("q_ready"), j1)
                        pe.wait_ge(S("o_ready"), j1)
                        for a in range(2):
                            hs = slice(a * HD, (a + 1) * HD)
                            pe.matmul(ROT[2 + a][:, 0:P], q_t[hs, b, 0:P], k_t[hs, kv, 0:P], start=True, stop=True)
                            pe.matmul(ROT[2 + a][:, P:384], q_t[hs, b, P:T], k_t[hs, kv, :], start=True,
                                      stop=True).then_inc(S("scores_done"), 1)
                        for a in range(2):
                            pe.wait_ge(S("prob_ready"), 2 * j1 - 1 + a)
                            for n in range(3):
                                mm = pe.transpose(ROT[a][:, n * P:(n + 1) * P], prob[:, b, a, n * P:(n + 1) * P], C("ident"))
                            mm.then_inc(S("p_turned"), 1)
                        for a in range(2):
                            pe.wait_ge(S("p_turned_out"), 2 * j1 + 1 + a)
                            vs = slice(kv * HD, (kv + 1) * HD)
                            out = ROT[2][a * HD:(a + 1) * HD, :]
                            pe.matmul(out[:, 0:P], v_rows[:, 0, vs], prob_t[:, b, a, 0:P], start=True, stop=True)
                            pe.matmul(out[:, P:T], v_rows[:, 0, vs], prob_t[:, b, a, P:2 * P], start=True, stop=False)
                            mm = pe.matmul(out[:, P:T], v_rows[:, 1, vs], prob_t[:, b, a, 2 * P:384], start=False, stop=True)
                        mm.then_inc(S("o_done"), 1)
                        arrived(pe, 2 * b + 1, "attn", i)
                        pe.wait_ge(S("o_ready"), j1 + 1)
                        close_into(pe, o_t[:, b, :], ring[2 * b + 1]).then_inc(freed[2 * b + 1], 1)

        def attn_scalar(act):
            with act.Fori(0, 4) as i:
                for b in range(2):
                    j1 = 2 * i + b + 1
                    multiplied(act, 2 * b, "attn", i)
                    act.activation(at_sq[:, b, :], ROT[0][:, 0:T], ACT.Square).then_inc(S("q_squared"), 1)
                    act.wait_ge(S("q_summed"), j1)
                    act.activation(at_root[:, b, 0, :], ROT[1][:, 0:T], ACT.Sqrt, scale=1.0 / HD,
                                   bias=stat[:, 14:15]).then_inc(S("q_rooted"), 1)
                    act.wait_ge(S("max_ready"), j1)
                    st = at_stat[:, b, :, :]
                    for n in range(4):
                        cols = slice(0, P) if n % 2 == 0 else slice(P, 384)
                        act.activation(prob[:, b, n // 2, cols], prob[:, b, n // 2, cols], ACT.Exp,
                                       bias=st[:, 1, n:n + 1], accum_out=st[:, 3, n:n + 1])
                    act.activation(st[:, 4, :], st[:, 2, :], ACT.Exp).then_inc(S("prob_exp"), 1)
                    for a in range(2):
                        act.wait_ge(S("p_turned"), 2 * j1 - 1 + a)
                        act.activation(prob_t[:, b, a, :], ROT[a][:, 0:384], ACT.Copy).then_inc(S("p_turned_out"), 1)
                    act.wait_ge(S("o_done"), j1)
                    act.activation(o_t[:, b, :], ROT[2][:, 0:T], ACT.Copy).then_inc(S("o_ready"), 1)

        def attn_vector(dve):
            with dve.Fori(0, 4) as i:
                for b in range(2):
                    j1 = 2 * i + b + 1
                    st = at_stat[:, b, :, :]
                    dve.wait_ge(S("q_rooted"), j1)
                    dve.reciprocal(at_root[:, b, 1, :], at_root[:, b, 0, :])
                    dve.drain()
                    dve.scalar_tensor_tensor(q_t[:, b, :], ROT[0][:, 0:T], V("q_norm"), at_root[:, b, 1, :],
                                             ALU.mult, ALU.mult).then_inc(S("q_ready"), 1)
                    dve.wait_ge(S(f"bias_loaded{b}"), 64 * i + 64)
                    for a in range(2):
                        dve.wait_ge(S("scores_done"), 2 * j1 - 1 + a)
                        dve.scalar_tensor_tensor(prob[:, b, a, :], ROT[2 + a][:, 0:384], HD ** -0.5,
                                                 bias_tile[:, b, a, :], ALU.mult, ALU.add).then_inc(S("scored"), 1)
                    dve.drain()
                    for n in range(4):
                        cols = slice(0, P) if n % 2 == 0 else slice(P, 384)
                        dve.reduce_max(st[:, 0, n:n + 1], prob[:, b, n // 2, cols], AX.X)
                    dve.drain()
                    sink = spread(VD("sinks", 4 * i + 2 * b, 2), 2)
                    view = st.rearrange("p s (a n) -> p s a n", a=2)
                    dve.tensor_tensor(view[:, 0, :, :], view[:, 0, :, :], sink, ALU.max)
                    dve.drain()
                    dve.tensor_tensor(view[:, 2, :, :], sink, view[:, 0, :, :], ALU.subtract)
                    dve.tensor_scalar(st[:, 1, :], st[:, 0, :], -1.0, None, ALU.mult)
                    dve.drain()
                    dve.sem_inc(S("max_ready"), 1)
                    dve.wait_ge(S("prob_exp"), j1)
                    dve.tensor_tensor(st[:, 3, :], st[:, 3, :], st[:, 4, :], ALU.add)
                    dve.drain()
                    dve.reciprocal(st[:, 5, :], st[:, 3, :])
                    dve.drain()
                    for n in range(4):
                        cols = slice(0, P) if n % 2 == 0 else slice(P, 384)
                        ins = dve.tensor_scalar(prob[:, b, n // 2, cols], prob[:, b, n // 2, cols],
                                                st[:, 5, n:n + 1], None, ALU.mult)
                        if n % 2:
                            ins.then_inc(S("prob_ready"), 1)
            multiplied(dve, 3, "attn", 3)
            update_h(dve, 1.0)

        SYNC["attn"], TENSOR["attn"], SCALAR["attn"], VECTOR["attn"] = attn_sync, attn_tensor, attn_scalar, attn_vector

        raw = area(5200, 14, 260)
        mixed = area(8840, 14, T)
        R_, K_, V_ = mixed[:, 0:4, :], mixed[:, 4:8, :], mixed[:, 8:12, :]
        w_wa, w_g = area(0, 512), area(512, 512)
        wa_act, g_act = area(1024, T), area(1280, T)
        log_decay, cum = area(12424, 4, T), area(13448, 4, T)
        p_now, p_prev, p_inv = area(14472, 4, T), area(15496, 4, T), area(16520, 4, T)
        a_gate, g_gate = area(17544, 4, T), area(18568, 4, T)
        kk, kk_a = area(19592, 4, T), area(20616, 4, T)
        rw_tmp, bonus, y_rw = area(21640, 4, T), area(22664, 4, T), area(23688, 4, T)
        alpha, beta, kappa, rho, v_now = (area(24712 + 256 * n, 4, CH) for n in range(5))
        (U, UL, A, AL, A2, AL2, A4) = (area(5200 + 512 * n, 4, P) for n in range(7))
        (AL4, A8, AL8, N) = (area(12424 + 512 * n, 4, P) for n in range(4))
        NL = area(25992, 4, P)
        v_st, kap_st, bet_st = (area(1536 + 256 * n, 4, CH) for n in range(3))
        lk_t, rk_t, rb_t = (area(2304 + 256 * n, 4, CH) for n in range(3))
        g_st, s_neg, z_st = (area(3072 + 256 * n, 4, CH) for n in range(3))
        halves = (slice(0, HD), slice(HD, P))

        def quarters(b, n=4):
            return b[:, :].rearrange("p (a b) -> p a b", a=n)

        def flat(t):
            return t.rearrange("p a b -> p (a b)")

        def rwkv_sync(sp):
            sp.wait_ge(S("u_ready"), 4 * norm_no["rwkv"] + 4)
            sp.dma_start(w_wa, io["w_wa"]).then_inc(S("lora_loaded"), 16)
            sp.dma_start(w_g, io["w_g"]).then_inc(S("lora_loaded"), 16)
            with sp.Fori(0, 2) as i:
                for n in range(7):
                    load(sp, n % 4, io["rwkv_in"][bass.ds(7 * i + n, 1), :, :], "rwkv", i, n // 4)
            for n in range(4):
                load(sp, n, io["w_o2"][4 + n, :, :], "rwkv_out")

        def rwkv_tensor(pe):
            pe.wait_ge(S("h_updated"), 4 * upd["rwkv"] + 1)
            with pe.Fori(0, 2) as i:
                for n in range(7):
                    arrived(pe, n % 4, "rwkv", i, n // 4)
                    pe.wait_ge(S("rw_evicted"), 7 * i + n + 1)
                    project(pe, bank[n][:, 0:T], n % 4).then_inc(freed[n % 4], 1)
            pe.wait_ge(S("rw_evicted"), 21)
            pe.wait_ge(S("lora_act"), 1)
            pe.wait_ge(S("lora_loaded"), 32)
            for kind in range(3):
                for p in range(4):
                    cols = slice(p * P, (p + 1) * P)
                    left, right = ((w_wa[0:HD, cols], wa_act[0:HD, :]), (w_wa[HD:P, cols], wa_act[HD:P, :]),
                                   (w_g[:, cols], g_act))[kind]
                    mm = pe.matmul(bank[2 * kind + p // 2][:, (p % 2) * T:(p % 2 + 1) * T], left, right,
                                   start=True, stop=True)
                mm.then_inc(S("lora_done"), 1)
            pe.wait_ge(S("kk_squared"), 1)
            for n in range(2):
                mm = pe.matmul(bank[6 + n][:, :], C("blk64"), flat(rw_tmp)[:, n * 512:(n + 1) * 512], start=True, stop=True)
            mm.then_inc(S("kk_summed"), 1)
            pe.wait_ge(S("rk_ready"), 1)
            pe.wait_ge(S("kk_rooted"), 1)
            for n in range(2):
                mm = pe.matmul(bank[6 + n][:, :], C("blk64"), flat(bonus)[:, n * 512:(n + 1) * 512], start=True, stop=True)
            mm.then_inc(S("rk_summed"), 1)
            with pe.Fori(0, RC) as c:
                pe.wait_ge(S("chunk_ready"), c + 1)
                pe.sem_inc(S("wait_held"), 1)
                for n, x in enumerate((v_now, kappa, beta)):
                    for p in range(4):
                        for a in halves:
                            at = (n % 2) * 256 + p * CH
                            mm = pe.matmul(bank[n // 2][a, at:at + CH], x[a, p, :], C("ident")[a, a], start=True, stop=True)
                mm.then_inc(S("rows_done"), 1)
                for n, (left, right) in enumerate(((beta, alpha), (alpha, beta), (kappa, alpha), (kappa, rho), (beta, rho))):
                    for p in range(4):
                        for a in halves:
                            at = (n % 2) * 256 + p * CH
                            mm = pe.matmul(bank[2 + n // 2][a, at:at + CH], left[a, p, :], right[a, p, :], start=True, stop=True)
                    if n % 2 or n == 4:
                        mm.then_inc(S("gram_done"), 1)

                def level(*products):
                    for b, left, right in products:
                        for p in range(4):
                            mm = pe.matmul(bank[b][:, p * P:(p + 1) * P], left[:, p, :], right[:, p, :], start=True, stop=True)
                    mm.then_inc(S("inv_done"), 1)

                pe.wait_ge(S("rows_ready"), c + 1)
                pe.wait_ge(S("inv_sum"), 6 * c + 1)
                level((0, AL, A), (1, A, AL))
                pe.wait_ge(S("lk_ready"), c + 1)
                pe.wait_ge(S("z_ready"), c + 1)
                pe.sem_inc(S("wait_held"), 1)
                for p in range(4):
                    for a in halves:
                        out = bank[4][a, 256 + p * CH:256 + (p + 1) * CH]
                        pe.matmul(out, alpha[a, p, :], z_st[a, p, :], start=True, stop=False)
                        mm = pe.matmul(out, lk_t[a, p, :], v_st[a, p, :], start=False, stop=True)
                mm.then_inc(S("g_done"), 1)
                pe.wait_ge(S("inv_copied"), 5 * c + 1)
                level((2, AL2, A2), (3, A2, AL2), (5, AL2, N), (6, A2, NL))
                pe.wait_ge(S("inv_copied"), 5 * c + 2)
                pe.wait_ge(S("inv_sum"), 6 * c + 2)
                level((0, AL4, A4), (1, A4, AL4), (5, AL4, N), (6, A4, NL))
                pe.wait_ge(S("inv_copied"), 5 * c + 3)
                pe.wait_ge(S("inv_sum"), 6 * c + 3)
                level((5, AL8, N), (6, A8, NL))
                pe.wait_ge(S("inv_sum"), 6 * c + 4)
                level((0, AL, N), (1, A, NL))
                pe.wait_ge(S("inv_copied"), 5 * c + 4)
                level((2, NL, A2), (3, N, A4))
                pe.wait_ge(S("inv_sum"), 6 * c + 5)
                level((0, AL, N))
                pe.wait_ge(S("inv_copied"), 5 * c + 5)
                level((1, NL, A2))
                pe.wait_ge(S("inv_sum"), 6 * c + 6)
                pe.wait_ge(S("g_ready"), c + 1)
                for p in range(4):
                    mm = pe.matmul(bank[5][:, p * CH:(p + 1) * CH], N[:, p, :], g_st[:, p, :], start=True, stop=True)
                mm.then_inc(S("s_done"), 1)
                pe.wait_ge(S("s_ready"), c + 1)
                pe.sem_inc(S("wait_held"), 1)
                for b, products in ((6, ((z_st, rho), (v_st, rk_t), (s_neg, rb_t))),
                                    (7, ((kap_st, v_st), (bet_st, s_neg)))):
                    for p in range(4):
                        for a in halves:
                            for n, (left, right) in enumerate(products):
                                mm = pe.matmul(bank[b][a, p * CH:(p + 1) * CH], left[a, p, :], right[a, p, :],
                                               start=(n == 0), stop=(n == len(products) - 1))
                    mm.then_inc(S("step_done"), 1)
            for n in range(2):
                pe.wait_ge(S("y_rw_ready"), n + 1)
                src = (y_rw, rw_tmp)[n]
                for b in range(2):
                    mm = pe.matmul(bank[2 * n + b][:, :], C("blk64"), flat(src)[:, b * 512:(b + 1) * 512], start=True, stop=True)
                mm.then_inc(S("y_rw_summed"), 1)
            pe.wait_ge(S("y_rw_ready"), 3)
            clear_acc(pe, upd["rwkv"])
            for p in range(4):
                arrived(pe, p, "rwkv_out")
                close_into(pe, y_rw[:, p, :], ring[p]).then_inc(freed[p], 1)

        def rwkv_scalar(act):
            with act.Fori(0, 2) as i:
                for n in range(7):
                    multiplied(act, n % 4, "rwkv", i, n // 4)
                    act.activation(raw[:, bass.ds(7 * i + n, 1), 1:1 + T], bank[n][:, 0:T].unsqueeze(1),
                                   ACT.Copy).then_inc(S("rw_evicted"), 1)
            act.wait_ge(S("rw_mixed"), 14)
            act.activation(wa_act[0:HD, :], mixed[0:HD, 12, :], ACT.Tanh)
            act.activation(wa_act[HD:P, :], mixed[HD:P, 12, :], ACT.Copy)
            act.activation(g_act, mixed[:, 13, :], ACT.Sigmoid).then_inc(S("lora_act"), 1)
            for kind, (dst, b0) in enumerate(((log_decay, "w0"), (a_gate, "a0"))):
                act.wait_ge(S("lora_done"), kind + 1)
                for p in range(4):
                    ins = act.activation(dst[:, p, :], bank[2 * kind + p // 2][:, (p % 2) * T:(p % 2 + 1) * T], ACT.Sigmoid,
                                         bias=V(b0, p, p + 1))
                ins.then_inc(S("gates_ready"), 1)
            act.wait_ge(S("lora_done"), 3)
            for b in range(2):
                act.activation(flat(g_gate)[:, b * 512:(b + 1) * 512], bank[4 + b][:, :], ACT.Copy)
            act.wait_ge(S("kk_raw"), 1)
            act.activation(rw_tmp, kk, ACT.Square).then_inc(S("kk_squared"), 1)
            act.wait_ge(S("cum_ready"), 1)
            act.activation(p_now, cum, ACT.Exp)
            act.activation(p_prev, p_prev, ACT.Exp)
            act.activation(p_inv, cum, ACT.Exp, scale=-1.0).then_inc(S("p_ready"), 1)
            act.wait_ge(S("kk_summed"), 1)
            for b in range(2):
                ins = act.activation(flat(rw_tmp)[:, b * 512:(b + 1) * 512], bank[6 + b][:, :], ACT.Sqrt)
            ins.then_inc(S("kk_rooted"), 1)
            with act.Fori(0, RC) as c:
                act.wait_ge(S("rows_done"), c + 1)
                act.activation(area(1536, 512), bank[0][:, :], ACT.Copy)
                act.activation(flat(bet_st), bank[1][:, 0:256], ACT.Copy).then_inc(S("rows_ready"), 1)
                for done, pairs in ((1, ((0, A2), (1, AL2))), (2, ((2, A4), (3, AL4))), (3, ((0, A8), (1, AL8))),
                                    (5, ((0, A2), (1, A4))), (7, ((0, A2),))):
                    act.wait_ge(S("inv_done"), 8 * c + done)
                    for b, dst in pairs:
                        ins = act.activation(flat(dst), bank[b][:, :], ACT.Copy)
                    ins.then_inc(S("inv_copied"), 1)
            act.wait_ge(S("y_centred"), 1)
            act.activation(rw_tmp, y_rw, ACT.Square).then_inc(S("y_rw_ready"), 1)
            act.wait_ge(S("y_rw_summed"), 2)
            for b in range(2):
                ins = act.activation(flat(rw_tmp)[:, b * 512:(b + 1) * 512], bank[2 + b][:, :], ACT.Sqrt, scale=1.0 / HD,
                                     bias=stat[:, 15:16])
            ins.then_inc(S("y_rw_rooted"), 1)

        def rwkv_vector(dve):
            def by_pair(out, x, gain, op1=None, off=None):
                for p in range(4):
                    ins = dve.tensor_scalar(out[:, p, :], x[:, p, :], V(gain, p, p + 1),
                                            V(off, p, p + 1) if off else None, ALU.mult, op1 or ALU.bypass)
                return ins

            dve.memset(raw[:, :, 0:1], 0.0)
            dve.drain()
            with dve.Fori(0, 2) as i:
                for n in range(7):
                    m = bass.ds(7 * i + n, 1)
                    dve.wait_ge(S("rw_evicted"), 7 * i + n + 8)
                    dve.tensor_tensor(mixed[:, m, :], raw[:, m, 0:T], raw[:, m, 1:1 + T], ALU.subtract)
                    dve.drain()
                    dve.scalar_tensor_tensor(mixed[:, m, :], mixed[:, m, :], VD("mu", 7 * i + n), raw[:, m, 1:1 + T],
                                             ALU.mult, ALU.add).then_inc(S("rw_mixed"), 1)
            dve.drain()
            dve.memset(y_rw, 1.0)
            by_pair(kk, K_, "k_k").then_inc(S("kk_raw"), 1)
            dve.drain()
            dve.memset(flat(y_rw).rearrange("p (c s) -> p c s", s=CH)[:, :, 0:1], 0.0)
            dve.wait_ge(S("gates_ready"), 1)
            dve.tensor_scalar(log_decay, log_decay, -math.exp(-0.5), None, ALU.mult)
            dve.drain()
            dve.tensor_tensor_scan(flat(cum), flat(y_rw), flat(log_decay), 0.0, ALU.mult, ALU.add)
            dve.drain()
            dve.tensor_tensor(p_prev, cum, log_decay, ALU.subtract).then_inc(S("cum_ready"), 1)
            dve.wait_ge(S("gates_ready"), 2)
            for p in range(4):
                dve.tensor_scalar(kk_a[:, p, :], a_gate[:, p, :], 1.0, V("k_a", p, p + 1), ALU.subtract, ALU.mult)
            dve.drain()
            dve.scalar_tensor_tensor(flat(K_), flat(kk_a), 1.0, flat(K_), ALU.add, ALU.mult)
            dve.drain()
            dve.tensor_tensor(bonus, R_, K_, ALU.mult)
            dve.drain()
            by_pair(bonus, bonus, "r_k").then_inc(S("rk_ready"), 1)
            dve.wait_ge(S("kk_rooted"), 1)
            dve.tensor_scalar(rw_tmp, rw_tmp, 1e-12, None, ALU.max)
            dve.drain()
            dve.reciprocal(rw_tmp, rw_tmp)
            dve.drain()
            dve.tensor_tensor(kk, kk, rw_tmp, ALU.mult)
            dve.drain()
            dve.tensor_tensor(kk_a, kk, a_gate, ALU.mult)
            dve.wait_ge(S("rk_summed"), 1)
            for b in range(2):
                dve.tensor_tensor(flat(bonus)[:, b * 512:(b + 1) * 512], bank[6 + b][:, :],
                                  flat(V_)[:, b * 512:(b + 1) * 512], ALU.mult)
            for m in (U, UL):
                dve.memset(m, 0.0)
            dve.memset(z_st, 0.0).then_inc(S("z_ready"), 1)
            dve.wait_ge(S("p_ready"), 1)
            dve.drain()

            def over_pairs(mask):
                return mask.unsqueeze(1).broadcast_to([mask.shape[0], 4, mask.shape[1]])

            with dve.Fori(0, RC) as c:
                now = bass.ds(c * CH, CH)
                dve.tensor_tensor(alpha, p_prev[:, :, now], kk[:, :, now], ALU.mult)
                dve.tensor_tensor(beta, p_inv[:, :, now], kk_a[:, :, now], ALU.mult)
                dve.tensor_tensor(kappa, p_inv[:, :, now], K_[:, :, now], ALU.mult)
                dve.tensor_tensor(rho, p_now[:, :, now], R_[:, :, now], ALU.mult)
                dve.tensor_copy(v_now, V_[:, :, now]).then_inc(S("chunk_ready"), 1)
                dve.wait_ge(S("gram_done"), 3 * c + 1)
                for a in halves:
                    for n, (m, mask) in enumerate(((U, "up_strict"), (UL, "low_strict"))):
                        dve.tensor_tensor(m[a, :, a], quarters(bank[2], 8)[a, 4 * n:4 * n + 4, :],
                                          over_pairs(C(mask)[a, :]), ALU.mult)
                dve.drain()
                dve.tensor_tensor(A, U, over_pairs(C("u16")), ALU.mult)
                dve.tensor_tensor(AL, UL, over_pairs(C("l16")), ALU.mult)
                dve.drain()
                dve.tensor_tensor(N, over_pairs(C("ident")), A, ALU.subtract)
                dve.tensor_tensor(NL, over_pairs(C("ident")), AL, ALU.subtract).then_inc(S("inv_sum"), 1)
                dve.wait_ge(S("gram_done"), 3 * c + 3)
                dve.tensor_tensor(lk_t, quarters(bank[3], 8)[:, 0:4, :], over_pairs(C("up_strict")), ALU.mult)
                dve.tensor_tensor(rk_t, quarters(bank[3], 8)[:, 4:8, :], over_pairs(C("up_incl")), ALU.mult)
                dve.tensor_tensor(rb_t, quarters(bank[4], 8)[:, 0:4, :], over_pairs(C("up_incl")), ALU.mult).then_inc(S("lk_ready"), 1)

                def add(done, op, *pairs):
                    dve.wait_ge(S("inv_done"), 8 * c + done)
                    for m, b in pairs:
                        ins = dve.tensor_tensor(m, m, quarters(bank[b]), op)
                    return ins

                add(2, ALU.add, (N, 5), (NL, 6)).then_inc(S("inv_sum"), 1)
                dve.wait_ge(S("g_done"), c + 1)
                dve.tensor_copy(flat(g_st), bank[4][:, 256:512]).then_inc(S("g_ready"), 1)
                add(3, ALU.add, (N, 5), (NL, 6)).then_inc(S("inv_sum"), 1)
                dve.tensor_tensor(A, U, over_pairs(C("u32")), ALU.mult)
                dve.tensor_tensor(AL, UL, over_pairs(C("l32")), ALU.mult)
                add(4, ALU.add, (N, 5), (NL, 6)).then_inc(S("inv_sum"), 1)
                add(6, ALU.subtract, (N, 2), (NL, 3))
                dve.tensor_tensor(AL, UL, over_pairs(C("l64")), ALU.mult).then_inc(S("inv_sum"), 1)
                add(8, ALU.subtract, (N, 1)).then_inc(S("inv_sum"), 1)
                dve.wait_ge(S("s_done"), c + 1)
                dve.tensor_scalar(flat(s_neg), bank[5][:, 0:256], -1.0, None, ALU.mult).then_inc(S("s_ready"), 1)
                dve.wait_ge(S("step_done"), 2 * c + 1)
                dve.tensor_copy(y_rw[:, :, now], bank[6][:, 0:256].rearrange("p (a b) -> p a b", a=4))
                dve.wait_ge(S("step_done"), 2 * c + 2)
                dve.tensor_tensor(flat(z_st), flat(z_st), bank[7][:, 0:256], ALU.add)
                dve.drain()
                end = p_now[:, :, bass.ds(c * CH + CH - 1, 1)]
                dve.tensor_tensor(z_st, z_st, end.broadcast_to([P, 4, CH]), ALU.mult).then_inc(S("z_ready"), 1)
            dve.drain()
            dve.sem_inc(S("y_rw_ready"), 1)
            dve.wait_ge(S("y_rw_summed"), 1)
            for b in range(2):
                part = flat(y_rw)[:, b * 512:(b + 1) * 512]
                ins = dve.scalar_tensor_tensor(part, bank[b][:, :], -1.0 / HD, part, ALU.mult, ALU.add)
            ins.then_inc(S("y_centred"), 1)
            dve.wait_ge(S("y_rw_rooted"), 1)
            dve.reciprocal(rw_tmp, rw_tmp)
            dve.drain()
            dve.tensor_tensor(y_rw, y_rw, rw_tmp, ALU.mult)
            dve.drain()
            by_pair(y_rw, y_rw, "lnw", ALU.add, "lnb")
            dve.drain()
            dve.tensor_tensor(y_rw, y_rw, bonus, ALU.add)
            dve.drain()
            dve.tensor_tensor(y_rw, y_rw, g_gate, ALU.mult).then_inc(S("y_rw_ready"), 1)

        SYNC["rwkv"], TENSOR["rwkv"], SCALAR["rwkv"], VECTOR["rwkv"] = rwkv_sync, rwkv_tensor, rwkv_scalar, rwkv_vector

        def mix_vector(dve):
            if "mla" in stages:
                multiplied(dve, 1, "mla_heads", 3)
            if "rwkv" in stages:
                multiplied(dve, 3, "rwkv_out")
            update_h(dve, 1.0)

        VECTOR["mix"] = mix_vector

        Q_, K2 = slice(0, QK), slice(NOPE, QK)
        uv_all = area(0, 4 * 2 * P)
        pos_i, pos_f = area(1024, T), area(1280, T)
        turns, cos_t, sin_t = area(1536, T), area(2048, T), area(2304, T)
        lat = area(4096, 6, T)
        lat_sq = area(5632, 5, T)
        lat_root = area(6912, 2, T)
        qk_sq, qk_root, qk_norm = (area(7424 + 1024 * n, 2, 512) for n in range(3))
        qk_cos, qk_sin, qk_rope = (area(10496 + 1024 * n, 2, 512) for n in range(3))
        m_prob, m_prob_t = area(13568, 2, 384), area(14336, 2, 384)
        v_pair = area(15104, TT, P)
        mo_sq, mo_root, mo_t = area(15360, T), area(15616, T), area(15872, T)
        m_stat = area(16128, 2, 3, 2)
        blocks = (slice(0, P), slice(P, 384))

        def mla_sync(sp):
            if "rwkv" in stages:
                sp.wait_ge(S("y_rw_ready"), 3)
            sp.dma_start(uv_all.rearrange("p (i n) -> p i n", i=4), io["mla_uv"].rearrange("i p n -> p i n")).then_inc(S("uv_loaded"), 16)
            sp.dma_start(pos_i.bitcast(I32), io["positions"].broadcast_to([P, T])).then_inc(S("pos_loaded"), 16)
            for n in range(6):
                load(sp, n % 4, io["mla_in"][n, :, :], "mla", 0, n // 4)
            with sp.Fori(0, 4) as i:
                load(sp, 0, io["mla_u"][bass.ds(i, 1), :, :], "mla_heads", i)
                load(sp, 1, io["w_o2"][bass.ds(i, 1), :, :], "mla_heads", i)

        def mla_tensor(pe):
            if "rwkv" not in stages:
                clear_acc(pe, upd["mla"])
            for n in range(6):
                arrived(pe, n % 4, "mla", 0, n // 4)
                if n >= 4:
                    pe.wait_ge(S("lat_out"), n - 3)
                project(pe, ROT[n % 4][:, 0:T], n % 4).then_inc(freed[n % 4], 1)
            pe.wait_ge(S("lat_out"), 6)
            pe.wait_ge(S("lat_squared"), 1)
            for b, part in enumerate((range(0, 3), range(3, 5))):
                for c in part:
                    mm = pe.matmul(ROT[b][:, 0:T], C("ones"), lat_sq[:, c, :], start=(c == part[0]), stop=(c == part[-1]))
            mm.then_inc(S("lat_summed"), 1)
            pe.wait_ge(S("lat_ready"), 1)
            pe.wait_ge(S("uv_loaded"), 16)
            with pe.Fori(0, 4) as i:
                arrived(pe, 0, "mla_heads", i)
                pe.wait_ge(S("mo_ready"), i + 1)
                for a in range(2):
                    for c in range(3):
                        at = (3 * a + c) * QK
                        mm = pe.matmul(ROT[a][Q_, 0:T], ring[0][:, at:at + QK], lat[:, c, :], start=(c == 0), stop=(c == 2))
                    pe.matmul(ROT[a][Q_, T:512], C("ident", 0, QK)[K2, :], lat[K2, 5, :], start=True, stop=False)
                    for c in range(2):
                        at = (6 + 2 * a + c) * QK
                        mm = pe.matmul(ROT[a][Q_, T:512], ring[0][:, at:at + QK], lat[:, 3 + c, :], start=False, stop=(c == 1))
                    mm.then_inc(S("mqk_done") if a == 0 else freed[0], 1)
                pe.wait_ge(S("mp_out"), 2 * i + 1)
                for tt in range(TT):
                    for c in range(2):
                        mm = pe.matmul(ROT[2][:, tt * P:(tt + 1) * P], lat[:, 3 + c, tt * P:(tt + 1) * P],
                                       uv_all[:, bass.ds(i * 2 * P + c * P, P)], start=(c == 0), stop=(c == 1))
                mm.then_inc(S("mv_done"), 1)
                for a in range(2):
                    pe.wait_ge(S("mqk_squared"), 2 * i + a + 1)
                    if a == 1:
                        pe.wait_ge(S("mv_out"), i + 1)
                    pe.matmul(ROT[3 - a][Q_, :], C("ones", 0, QK)[Q_, :], qk_sq[Q_, a, :], start=True,
                              stop=True).then_inc(S("mqk_summed"), 1)
                for a in range(2):
                    pe.wait_ge(S("mqk_normed"), 2 * i + a + 1)
                    pe.matmul(ROT[3 - a][Q_, :], C("rot")[Q_, :], qk_norm[Q_, a, :], start=True,
                              stop=True).then_inc(S("mqk_turned"), 1)
                for a in range(2):
                    pe.wait_ge(S("mqk_ready"), 2 * i + a + 1)
                    q, k = qk_rope[Q_, a, 0:T], qk_rope[Q_, a, T:512]
                    pe.matmul(ROT[a][:, 0:P], q[:, 0:P], k[:, 0:P], start=True, stop=True)
                    pe.matmul(ROT[a][:, P:384], q[:, P:T], k, start=True, stop=True).then_inc(S("m_scores"), 1)
                for a in range(2):
                    pe.wait_ge(S("mp_ready"), 2 * i + a + 1)
                    for n in range(3):
                        mm = pe.transpose(ROT[3 - a][:, n * P:(n + 1) * P], m_prob[:, a, n * P:(n + 1) * P], C("ident"))
                    mm.then_inc(S("mp_turned"), 1)
                for a in range(2):
                    pe.wait_ge(S("mp_out"), 2 * i + a + 2)
                    out, vs = ROT[0][a * HD:(a + 1) * HD, :], slice(a * HD, (a + 1) * HD)
                    pe.matmul(out[:, 0:P], v_pair[:, 0, vs], m_prob_t[:, a, 0:P], start=True, stop=True)
                    pe.matmul(out[:, P:T], v_pair[:, 0, vs], m_prob_t[:, a, P:2 * P], start=True, stop=False)
                    mm = pe.matmul(out[:, P:T], v_pair[:, 1, vs], m_prob_t[:, a, 2 * P:384], start=False, stop=True)
                mm.then_inc(S("mo_done"), 1)
                pe.wait_ge(S("mo_squared"), i + 1)
                pe.matmul(ROT[1][:, 0:T], C("blk64"), mo_sq, start=True, stop=True).then_inc(S("mo_summed"), 1)
                arrived(pe, 1, "mla_heads", i)
                pe.wait_ge(S("mo_ready"), i + 2)
                close_into(pe, mo_t, ring[1]).then_inc(freed[1], 1)

        def mla_scalar(act):
            for n in range(6):
                multiplied(act, n % 4, "mla", 0, n // 4)
                act.activation(lat[:, n, :], ROT[n % 4][:, 0:T], ACT.Copy).then_inc(S("lat_out"), 1)
            act.wait_ge(S("lat_out"), 6)
            act.activation(lat_sq, lat[:, 0:5, :], ACT.Square).then_inc(S("lat_squared"), 1)
            act.wait_ge(S("angles_ready"), 1)
            act.activation(sin_t[Q_, :], sin_t[Q_, :], ACT.Sin)
            act.activation(cos_t[Q_, :], cos_t[Q_, :], ACT.Sin).then_inc(S("rope_ready"), 1)
            act.wait_ge(S("lat_summed"), 1)
            act.activation(lat_root[:, 0, :], ROT[0][:, 0:T], ACT.Sqrt, scale=1.0 / MLA_Q, bias=stat[:, 14:15])
            act.activation(lat_root[:, 1, :], ROT[1][:, 0:T], ACT.Sqrt, scale=1.0 / MLA_KV,
                           bias=stat[:, 14:15]).then_inc(S("lat_rooted"), 1)
            with act.Fori(0, 4) as i:
                for a in range(2):
                    if a == 0:
                        act.wait_ge(S("mqk_done"), i + 1)
                    else:
                        multiplied(act, 0, "mla_heads", i)
                    act.activation(qk_sq[Q_, a, :], ROT[a][Q_, :], ACT.Square).then_inc(S("mqk_squared"), 1)
                act.wait_ge(S("mv_done"), i + 1)
                act.activation(v_pair, ROT[2][:, 0:T].rearrange("p (a b) -> p a b", a=TT), ACT.Copy).then_inc(S("mv_out"), 1)
                for a in range(2):
                    act.wait_ge(S("mqk_summed"), 2 * i + a + 1)
                    act.activation(qk_root[Q_, a, :], ROT[3 - a][Q_, :], ACT.Sqrt, scale=1.0 / QK,
                                   bias=stat[Q_, 14:15]).then_inc(S("mqk_rooted"), 1)
                for a in range(2):
                    act.wait_ge(S("m_max"), 2 * i + a + 1)
                    for n, cols in enumerate(blocks):
                        ins = act.activation(m_prob[:, a, cols], m_prob[:, a, cols], ACT.Exp,
                                             bias=m_stat[:, a, 1, n:n + 1], accum_out=m_stat[:, a, 2, n:n + 1])
                    ins.then_inc(S("mp_exp"), 1)
                for a in range(2):
                    act.wait_ge(S("mp_turned"), 2 * i + a + 1)
                    act.activation(m_prob_t[:, a, :], ROT[3 - a][:, 0:384], ACT.Copy).then_inc(S("mp_out"), 1)
                act.wait_ge(S("mo_done"), i + 1)
                act.activation(mo_sq, ROT[0][:, 0:T], ACT.Square).then_inc(S("mo_squared"), 1)
                act.wait_ge(S("mo_summed"), i + 1)
                act.activation(mo_root, ROT[1][:, 0:T], ACT.Sqrt, scale=1.0 / HD, bias=stat[:, 14:15]).then_inc(S("mo_rooted"), 1)

        def mla_vector(dve):
            dve.wait_ge(S("pos_loaded"), 16)
            dve.tensor_copy(pos_f, pos_i.bitcast(I32))
            dve.drain()
            dve.tensor_scalar(pos_f, pos_f, C("inv_freq"), None, ALU.mult)
            dve.drain()
            dve.tensor_scalar(turns, pos_f, 1.0 / (2 * math.pi), 1.5 * 2.0 ** 23, ALU.mult, ALU.add)
            dve.drain()
            dve.tensor_scalar(turns, turns, -1.5 * 2.0 ** 23, None, ALU.add)
            c1 = 6.28125
            c2 = float(np.float32(np.round((2 * math.pi - c1) * 2 ** 21) / 2 ** 21))
            for c in (c1, c2, 2 * math.pi - c1 - c2):
                dve.drain()
                dve.scalar_tensor_tensor(pos_f, turns, -c, pos_f, ALU.mult, ALU.add)
            dve.drain()
            dve.tensor_scalar(sin_t, pos_f, 3.1415925, -3.1415925, ALU.min, ALU.max)
            dve.tensor_scalar(cos_t, pos_f, -1.0, None, ALU.mult)
            dve.drain()
            dve.tensor_tensor(cos_t, cos_t, pos_f, ALU.min)
            dve.drain()
            dve.tensor_scalar(cos_t, cos_t, C("half"), None, ALU.add).then_inc(S("angles_ready"), 1)
            dve.wait_ge(S("lat_rooted"), 1)
            dve.reciprocal(lat_root, lat_root)
            dve.drain()
            for c in range(5):
                gain = V("g_cq", c, c + 1) if c < 3 else V("g_ckv", c - 3, c - 2)
                ins = dve.scalar_tensor_tensor(lat[:, c, :], lat[:, c, :], gain, lat_root[:, c // 3, :], ALU.mult, ALU.mult)
            ins.then_inc(S("lat_ready"), 1)
            dve.wait_ge(S("rope_ready"), 1)

            def twice(t):
                return t[Q_, :].unsqueeze(1).broadcast_to([QK, 2, T])

            def two(t):
                return t.rearrange("p (a b) -> p a b", a=2)

            with dve.Fori(0, 4) as i:
                for a in range(2):
                    dve.wait_ge(S("mqk_rooted"), 2 * i + a + 1)
                    dve.reciprocal(qk_root[Q_, a, :], qk_root[Q_, a, :])
                    dve.drain()
                    for n, gain in enumerate(("g_qnorm", "g_knorm")):
                        cols = slice(n * T, (n + 1) * T)
                        ins = dve.scalar_tensor_tensor(qk_norm[Q_, a, cols], ROT[a][Q_, cols], V(gain)[Q_, :],
                                                       qk_root[Q_, a, cols], ALU.mult, ALU.mult)
                    ins.then_inc(S("mqk_normed"), 1)
                dve.drain()
                for a in range(2):
                    dve.tensor_tensor(two(qk_cos[Q_, a, :]), two(qk_norm[Q_, a, :]), twice(cos_t), ALU.mult)
                    dve.wait_ge(S("mqk_turned"), 2 * i + a + 1)
                    dve.tensor_tensor(two(qk_sin[Q_, a, :]), two(ROT[3 - a][Q_, :]), twice(sin_t), ALU.mult)
                    dve.drain()
                    dve.tensor_tensor(qk_rope[Q_, a, :], qk_cos[Q_, a, :], qk_sin[Q_, a, :], ALU.add).then_inc(S("mqk_ready"), 1)
                for a in range(2):
                    dve.wait_ge(S("m_scores"), 2 * i + a + 1)
                    dve.scalar_tensor_tensor(m_prob[:, a, :], ROT[a][:, 0:384], QK ** -0.5, C("mla_mask"), ALU.mult, ALU.add)
                    dve.drain()
                    for n, cols in enumerate(blocks):
                        dve.reduce_max(m_stat[:, a, 0, n:n + 1], m_prob[:, a, cols], AX.X)
                    dve.drain()
                    dve.tensor_scalar(m_stat[:, a, 1, :], m_stat[:, a, 0, :], -1.0, None, ALU.mult).then_inc(S("m_max"), 1)
                for a in range(2):
                    dve.wait_ge(S("mp_exp"), 2 * i + a + 1)
                    dve.reciprocal(m_stat[:, a, 2, :], m_stat[:, a, 2, :])
                    dve.drain()
                    for n, cols in enumerate(blocks):
                        ins = dve.tensor_scalar(m_prob[:, a, cols], m_prob[:, a, cols], m_stat[:, a, 2, n:n + 1], None, ALU.mult)
                    ins.then_inc(S("mp_ready"), 1)
                dve.wait_ge(S("mo_rooted"), i + 1)
                dve.reciprocal(mo_root, mo_root)
                dve.drain()
                dve.scalar_tensor_tensor(mo_t, ROT[0][:, 0:T], VD("g_out", i), mo_root, ALU.mult, ALU.mult).then_inc(S("mo_ready"), 1)

        SYNC["mla"], TENSOR["mla"], SCALAR["mla"], VECTOR["mla"] = mla_sync, mla_tensor, mla_scalar, mla_vector

        KH = NKEYS // 2
        BODIES = KH // 2
        TG = 8
        peer_area = KH * T
        choice_t = area(peer_area, 3, T)
        one_a = area(peer_area + 768, 2, TG * KH).rearrange("p g (t e) -> p g t e", t=TG)
        one_b = area(peer_area + 1792, 2, TG * NKEYS).rearrange("p g (t e) -> p g t e", t=TG)
        gelu_buf = area(peer_area + 3840, 2, T)
        gated_buf = area(peer_area + 4352, 2, T)
        keys_all = area(4096, PH * 2 * NKEYS)
        pq_t = area(6144, 2, T)
        score = area(6656, 4, NKEYS)
        score2 = area(7168, 4, NKEYS)
        top, top_i, top_f = (area(7680 + 64 * n, 4, TOPK) for n in range(3))
        cand, cand2 = (area(8192 + 512 * n, TT, TOPK * TOPK) for n in range(2))
        best, best_i, best_a, best_b, best_af, best_bf, gate = (area(9216 + 32 * n, TT, TOPK) for n in range(7))
        gate_sum = area(9472, 2, TT)
        pick = area(9728, TT, TOPK, TOPK)
        choice = area(10240, 3, TT, P)
        gates_of = area(0, KH, T)

        def peer_sync(sp):
            sp.wait_ge(S("u_ready"), 4 * norm_no["peer"] + 1)
            sp.dma_start(keys_all.rearrange("p (h n) -> p h n", h=PH), io["keys"].rearrange("h p n -> p h n")).then_inc(S("keys_loaded"), 16)
            with sp.Fori(0, PH) as i:
                for n in range(2):
                    load(sp, n, io["w_pq"][bass.ds(2 * i + n, 1), :, :], "route", i)
            def u(n, i):
                load(sp, 2 * n, io["expert_u"][bass.ds(2 * i + n, 1), :, :], "peer", i)

            def v(n, i):
                load(sp, 2 * n + 1, io["expert_v"][bass.ds(2 * i + n, 1), :, :], "peer", i)

            u(0, 0), v(0, 0), u(1, 0)
            with sp.Fori(0, 2 * BODIES - 1) as i:
                u(0, i + 1), v(1, i), u(1, i + 1), v(0, i + 1)
            v(1, 2 * BODIES - 1)

        def peer_tensor(pe):
            pe.wait_ge(S("keys_loaded"), 16)
            with pe.Fori(0, PH) as i:
                pe.wait_ge(S("pq_out"), 2 * i + 2)
                for n in range(2):
                    arrived(pe, n, "route", i)
                    project(pe, ROT[n][:, 0:T], n).then_inc(freed[n], 1)
                pe.wait_ge(S("pq_out"), 2 * i + 4)
                pe.wait_ge(S("score_out"), i + 1)
                for tt in range(TT):
                    for n in range(2):
                        at = (2 * tt + n) * P
                        mm = pe.matmul(ROT[2][:, at:at + P], pq_t[:, n, tt * P:(tt + 1) * P],
                                       keys_all[:, bass.ds((2 * i + n) * NKEYS, NKEYS)], start=True, stop=True)
                mm.then_inc(S("score_done"), 1)
            pe.wait_ge(S("chosen"), 1)
            for k in range(3):
                for tt in range(TT):
                    mm = pe.transpose(ROT[k][:, tt * P:(tt + 1) * P], choice[:, k, tt, :], C("ident"))
            mm.then_inc(S("choice_turned"), 1)
            pe.wait_ge(S("choice_ready"), 1)

            def up(n, i):
                pe.wait_ge(S("gelu_out"), 2 * i + n + 1)
                project_split(pe, ROT[n][:, 0:T], 2 * n, "peer", i)

            def down(n, i, last=False):
                pe.wait_ge(S("gated"), 2 * i + n + 3)
                close_split(pe, n, 2 * n + 1, "peer", i, last)

            for k in range(2):
                with pe.Fori(0, T // TG // 2) as i:
                    for g in range(2):
                        pe.wait_ge(S("one_hot"), k * T // TG + 2 * i + g + 3)
                        pe.wait_ge(S("gates_out"), k * T // TG + 2 * i + g + 1)
                        for t in range(TG):
                            mm = pe.matmul(ROT[2 + g][:, t * KH:(t + 1) * KH], one_b[:, g, t, :], one_a[:, g, t, :],
                                           start=True, stop=True)
                        mm.then_inc(S("gates_done"), 1)
                if k == 0:
                    clear_acc(pe, upd["peer"])
                first, end = k * BODIES, (k + 1) * BODIES - 1
                up(0, first)
                with pe.Fori(first, end) as i:
                    up(1, i)
                    down(0, i)
                    up(0, i + 1)
                    down(1, i)
                up(1, end)
                down(0, end)
                down(1, end, last=(k == 1))

        def peer_scalar(act):
            with act.Fori(0, PH) as i:
                for n in range(2):
                    multiplied(act, n, "route", i)
                    act.activation(pq_t[:, n, :], ROT[n][:, 0:T], ACT.Copy).then_inc(S("pq_out"), 1)
                act.wait_ge(S("best_ready"), i + 1)
                act.activation(gate, gate, ACT.Exp).then_inc(S("gate_exp"), 1)

            def step(n, i, ahead=True, more=True):
                split_done(act, 2 * n, "peer", i)
                act.wait_ge(S("gated"), 2 * i + n + 1)
                act.activation(gelu_buf[:, n, :], ROT[n][:, 0:T], ACT.Gelu).then_inc(S("gelu_out"), 1)
                if ahead:
                    make_hi(act, 2 * n, "peer", i + 1)
                if ahead or more:
                    make_hi(act, 3 - 2 * n, "peer", i + n)

            make_hi(act, 0, "peer", 0)
            make_hi(act, 1, "peer", 0)
            make_hi(act, 2, "peer", 0)
            for k in range(2):
                with act.Fori(0, T // TG // 2) as i:
                    for g in range(2):
                        act.wait_ge(S("gates_done"), k * T // TG + 2 * i + g + 3)
                        out = gates_of[:, :, bass.ds(2 * TG * i + TG * g, TG)].rearrange("p b t -> p t b")
                        act.activation(out, ROT[2 + g][:, :].rearrange("p (t b) -> p t b", t=TG),
                                       ACT.Copy).then_inc(S("gates_out"), 1)
                with act.Fori(k * BODIES, (k + 1) * BODIES - k) as i:
                    step(0, i)
                    step(1, i)
            step(0, 2 * BODIES - 1, ahead=False)
            step(1, 2 * BODIES - 1, ahead=False, more=False)

        def peer_vector(dve):
            def as_int(t):
                return t.bitcast(U32)

            def top16(values, indices, src, less, rows):
                for r in rows:
                    dve.max(values[:, r, 0:8], src[:, r, :])
                dve.drain()
                for r in rows:
                    dve.max_index(as_int(indices)[:, r, 0:8], values[:, r, 0:8], src[:, r, :])
                    dve.match_replace(less[:, r, :], values[:, r, 0:8], src[:, r, :], -3e38)
                dve.drain()
                for r in rows:
                    dve.max(values[:, r, 8:16], less[:, r, :])
                dve.drain()
                for r in rows:
                    dve.max_index(as_int(indices)[:, r, 8:16], values[:, r, 8:16], less[:, r, :])
                dve.drain()

            with dve.Fori(0, PH) as i:
                dve.wait_ge(S("score_done"), i + 1)
                dve.tensor_copy(flat(score), ROT[2][:, :]).then_inc(S("score_out"), 1)
                dve.drain()
                top16(top, top_i, score, score2, range(4))
                dve.tensor_copy(flat(top_f), as_int(flat(top_i)))
                for tt in range(TT):
                    dve.tensor_tensor(cand[:, tt, :].rearrange("p (a b) -> p a b", a=TOPK), spread(top[:, 2 * tt, :], TOPK),
                                      top[:, 2 * tt + 1, :].unsqueeze(1).broadcast_to([P, TOPK, TOPK]), ALU.add)
                dve.drain()
                top16(best, best_i, cand, cand2, range(TT))
                dve.tensor_tensor(gate, best, best[:, :, 0:1].broadcast_to([P, TT, TOPK]), ALU.subtract).then_inc(S("best_ready"), 1)
                dve.tensor_scalar(as_int(flat(best_a)), as_int(flat(best_i)), 4, None, ALU.logical_shift_right)
                dve.tensor_scalar(as_int(flat(best_b)), as_int(flat(best_i)), 15, None, ALU.bitwise_and)
                dve.drain()
                dve.tensor_copy(flat(best_af), as_int(flat(best_a)))
                dve.tensor_copy(flat(best_bf), as_int(flat(best_b)))
                dve.drain()
                for n, at in enumerate((best_af, best_bf)):
                    for tt in range(TT):
                        dve.tensor_tensor(pick[:, tt, :, :], spread(at[:, tt, :], TOPK),
                                          C("iota", 0, TOPK).unsqueeze(1).broadcast_to([P, TOPK, TOPK]), ALU.is_equal)
                    dve.drain()
                    for tt in range(TT):
                        dve.tensor_tensor(pick[:, tt, :, :], pick[:, tt, :, :],
                                          top_f[:, 2 * tt + n, :].unsqueeze(1).broadcast_to([P, TOPK, TOPK]), ALU.mult)
                    dve.drain()
                    dve.reduce_sum(choice[:, n, :, bass.ds(TOPK * i, TOPK)], pick, AX.X)
                    dve.drain()
                dve.wait_ge(S("gate_exp"), i + 1)
                dve.reduce_sum(gate_sum[:, 0, :], gate, AX.X)
                dve.drain()
                dve.reciprocal(gate_sum[:, 1, :], gate_sum[:, 0, :])
                dve.drain()
                dve.tensor_tensor(choice[:, 2, :, bass.ds(TOPK * i, TOPK)], gate, spread(gate_sum[:, 1, :], TOPK), ALU.mult)
                dve.drain()
            dve.sem_inc(S("chosen"), 1)
            dve.wait_ge(S("choice_turned"), 1)
            for k in range(3):
                ins = dve.tensor_copy(choice_t[:, k, :], ROT[k][:, 0:T])
            ins.then_inc(S("choice_ready"), 1)
            dve.drain()

            def step(n, i, ahead=True, more=True):
                dve.wait_ge(S("gelu_out"), 2 * i + n + 3)
                dve.wait_ge(split_read[2 * n + 1], use_split("peer", 2 * n + 1, i) + 1)
                gates = gates_of[:, bass.ds(2 * (i - first) + n, 1), :]
                dve.tensor_tensor(x_hi[:, n, :], gelu_buf[:, n, :], gates, ALU.mult)
                dve.tensor_tensor(gated_buf[:, n, :], gelu_buf[:, n, :], gates, ALU.mult)
                dve.drain()
                dve.tensor_tensor(x_lo[:, n, :], gated_buf[:, n, :], x_hi[:, n, :].bitcast(F32),
                                  ALU.subtract).then_inc(S("gated"), 1)
                if ahead:
                    make_lo(dve, 2 * n, "peer", i + 1)
                if ahead or more:
                    make_lo(dve, 3 - 2 * n, "peer", i + n)

            make_lo(dve, 0, "peer", 0)
            make_lo(dve, 1, "peer", 0)
            make_lo(dve, 2, "peer", 0)
            for k in range(2):
                first = k * BODIES
                with dve.Fori(0, T // TG // 2) as i:
                    for g in range(2):
                        dve.wait_ge(S("gates_done"), k * T // TG + 2 * i + g + 1)
                        tokens = bass.ds(2 * TG * i + TG * g, TG)
                        dve.tensor_tensor(one_b[:, g, :, :], C("iota").unsqueeze(1).broadcast_to([P, TG, NKEYS]),
                                          spread(choice_t[:, 1, tokens], NKEYS), ALU.is_equal)
                        for t in range(TG):
                            tok = bass.ds(2 * TG * i + TG * g + t, 1)
                            ins = dve.tensor_scalar(one_a[:, g, t, :], C("iota", k * KH, (k + 1) * KH),
                                                    choice_t[:, 0, tok], choice_t[:, 2, tok], ALU.is_equal, ALU.mult)
                        ins.then_inc(S("one_hot"), 1)
                dve.wait_ge(S("gates_out"), (k + 1) * T // TG + 2)
                with dve.Fori(first, first + BODIES - k) as i:
                    step(0, i)
                    step(1, i)
            step(0, 2 * BODIES - 1, ahead=False)
            step(1, 2 * BODIES - 1, ahead=False, more=False)
            split_done(dve, 3, "peer", 2 * BODIES - 1)
            update_h(dve, 1.0)

        SYNC["peer"], TENSOR["peer"], SCALAR["peer"], VECTOR["peer"] = peer_sync, peer_tensor, peer_scalar, peer_vector
        block = ctx.enter_context(nc.Block())

        @block.sync
        def _(sp):
            sp.dma_start(con[:, :], io["consts"]).then_inc(S("in_loaded"), 16)
            sp.dma_start(vec[:, :], io["vecs"]).then_inc(S("in_loaded"), 16)
            sp.dma_start(h[:, :, :], io["x"].rearrange("(a p) d -> p a d", p=P)).then_inc(S("h_loaded"), 16)
            for s in stages:
                if s.startswith("ffn"):
                    ffn_sync(sp, int(s[3]))
                elif s in SYNC:
                    SYNC[s](sp)
            sp.wait_ge(S("h_updated"), 4 * len(sums) + 1)
            sp.dma_start(io["out"].rearrange("(a p) d -> p a d", p=P), h[:, :, :]).then_inc(S("out_stored"), 16)
            sp.wait_ge(S("out_stored"), 16)

        @block.gpsimd
        def _(pool):
            pool.memset(zeros[:, :], 0.0).then_inc(S("pool_setup"), 1)
            pool.wait_ge(S("pool_setup"), 1)
            for sem, n in [(f, 1) for f in freed + split_read] + [(S("hid_ready"), 2), (S("h_updated"), 1), (S("ssm_evicted"), 4), (S("y_taken"), 1),
                                                   (S("scored"), 4), (S("p_turned_out"), 2), (S("o_ready"), 1), (S("rw_evicted"), 7),
                                                   (S("mo_ready"), 1), (S("mp_out"), 1), (S("pq_out"), 2), (S("score_out"), 1),
                                                   (S("gates_out"), 2), (S("gates_done"), 2), (S("one_hot"), 2),
                                                   (S("gelu_out"), 2), (S("gated"), 2)]:
                pool.sem_inc(sem, n)
            for s in stages:
                if s in POOL:
                    POOL[s](pool)

        @block.scalar
        def _(act):
            act.wait_ge(S("stat_ready"), 1)
            for s in stages:
                if s in norm_no:
                    norm_scalar(act, norm_no[s], upd[s], s in SPLIT_STAGES)
                if s.startswith("ffn"):
                    ffn_scalar(act, int(s[3]))
                elif s in SCALAR:
                    SCALAR[s](act)

        @block.vector
        def _(dve):
            dve.memset(stat[:, 14:15], EPS)
            dve.memset(stat[:, 15:16], LN_EPS).then_inc(S("stat_ready"), 1)
            dve.wait_ge(S("in_loaded"), 32)
            for s in stages:
                if s in norm_no:
                    norm_vector(dve, norm_no[s], GAIN[s], s in SPLIT_STAGES)
                if s.startswith("ffn"):
                    ffn_vector(dve, int(s[3]))
                elif s in VECTOR:
                    VECTOR[s](dve)

        @block.tensor
        def _(pe):
            pe.wait_ge(S("in_loaded"), 32)
            for s in stages:
                if s in norm_no:
                    norm_tensor(pe, norm_no[s], s in SPLIT_STAGES)
                if s.startswith("ffn"):
                    ffn_tensor(pe, int(s[3]), upd[s])
                elif s in TENSOR:
                    TENSOR[s](pe)


def pack(x):
    def cols(v):
        v = np.asarray(v).reshape(-1)
        return v.reshape(-1, P).T

    def pad(v):
        v = np.asarray(v).reshape(-1)
        return np.concatenate([v, np.zeros(P - len(v), v.dtype)]).reshape(P, 1)

    inner = GROUPS * GI
    order = []
    for g in range(GROUPS):
        order += [inner + g * P, inner + GROUPS * P + g * P] + [g * GI + k * P for k in range(4)]
    conv_w, conv_b = x["ssm_conv_w"][0], x["ssm_conv_b"][0]
    ffn_norm = x["ffn_norm"].reshape(4, D)
    v = {
        "g_ffn0": cols(ffn_norm[0]), "g_ffn1": cols(ffn_norm[1]), "g_ffn2": cols(ffn_norm[2]),
        "g_ffn3": cols(ffn_norm[3]), "g_ssm": cols(x["ssm_norm"]), "g_kv": cols(x["kv_norm"]),
        "g_attn": cols(x["attn_norm"]), "g_mix": cols(x["g_mix_2"]), "g_peer": cols(x["g_ffn_2"]),
        "conv_w": np.concatenate([conv_w[:, o:o + P].T for o in order], 1),
        "conv_b": np.stack([conv_b[o:o + P] for o in order], 1),
        "d_skip": cols(np.repeat(x["ssm_d"][0], HD)), "g_gate": cols(x["ssm_gate_norm"]),
        "dt_bias": pad(x["ssm_dt_bias"]), "a_log": pad(x["ssm_a_log"]),
        "k_norm": np.tile(x["k_norm"], 2)[:, None], "q_norm": np.tile(x["q_norm"][0], 2)[:, None],
        "sinks": np.tile(x["sinks"], (P, 1)),
        "g_cq": cols(x["g_cq_2"]), "g_ckv": cols(x["g_ckv_2"]),
        "g_qnorm": pad(x["g_qnorm_2"]), "g_knorm": pad(x["g_knorm_2"]), "g_out": cols(x["g_attn_out_2"]),
        "mu": cols(x["rwkv_mu_2"]), "w0": cols(x["w0_2"]), "a0": cols(x["a0_2"]), "k_k": cols(x["k_k_2"]),
        "k_a": cols(x["k_a_2"]), "r_k": cols(x["r_k_2"]), "lnw": cols(x["ln_x_w_2"]), "lnb": cols(x["ln_x_b_2"]),
    }
    for name, (_, n) in VECS.items():
        assert v[name].shape == (P, n), (name, v[name].shape)
    w_in = x["ssm_w_in"][0]
    xbc = tiles(w_in[:, inner:inner + inner + 2 * GROUPS * P])
    z = tiles(w_in[:, 0:inner])
    group_tiles = np.stack([
        np.concatenate([xbc[[16 + g, 20 + g] + [4 * g + k for k in range(4)]], z[4 * g:4 * g + 4]])
        for g in range(GROUPS)])
    w_kv = x["w_kv"]
    kv = np.concatenate([w_kv[:, 0:64], w_kv[:, 0:64], w_kv[:, 64:128], w_kv[:, 64:128], w_kv[:, 128:256]], 1)
    w_in2 = x["w_in_2"][0]
    rope_cols = np.concatenate([w_in2[:, 0:MLA_Q + MLA_KV], np.zeros((D, NOPE), np.float32),
                                w_in2[:, MLA_Q + MLA_KV:MLA_Q + MLA_KV + ROPE], np.zeros((D, ROPE), np.float32)], 1)
    uq = x["w_uq_2"][0].reshape(3, P, PH, QK).transpose(2, 1, 0, 3).reshape(PH, P, 3 * QK)
    uk = x["w_uk_2"][0].reshape(2, P, PH, NOPE).transpose(2, 1, 0, 3)
    uk = np.concatenate([uk, np.zeros((PH, P, 2, ROPE), uk.dtype)], 3).reshape(PH, P, 2 * QK)
    uv = x["w_uv_2"][0].reshape(2, P, 4, P).transpose(2, 1, 0, 3).reshape(4, P, 2 * P)
    return {
        "x": x["x"][0], "positions": x["positions_2"].reshape(1, T), "consts": constants(),
        "vecs": np.concatenate([v[name] for name in VECS], 1),
        "w1": np.stack([tiles(w) for w in x["ffn_w1"].reshape(4, D, FF)]),
        "w3": np.stack([tiles(w) for w in x["ffn_w3"].reshape(4, D, FF)]),
        "w2": x["ffn_w2"].reshape(4, FC, P, D),
        "ssm_in": group_tiles, "ssm_dt": tiles(w_in[:, 5120:5152], 32)[0],
        "ssm_out": x["ssm_w_out"].reshape(GROUPS, 4, P, D),
        "w_kv": tiles(kv), "w_q": tiles(x["w_q"][0]), "w_o": x["w_o"].reshape(8, P, D),
        "rel_bias": x["rel_bias"],
        "mla_in": tiles(rope_cols), "rwkv_in": tiles(w_in2[:, 672:]),
        "mla_u": np.concatenate([
            uq.reshape(4, 2, P, 3 * QK).transpose(0, 2, 1, 3).reshape(4, P, 6 * QK),
            uk.reshape(4, 2, P, 2 * QK).transpose(0, 2, 1, 3).reshape(4, P, 4 * QK)], 2),
        "mla_uv": uv,
        "w_wa": np.concatenate([x["w2_2"][0], x["a2_2"][0]], 0), "w_g": x["g2_2"][0],
        "w_o2": x["w_o_2"].reshape(8, P, D),
        "w_pq": tiles(x["w_pq_2"][0]),
        "keys": x["sub_keys_2"][0].transpose(0, 3, 1, 2).reshape(PH, P, 2 * NKEYS),
        "expert_u": x["expert_u_2"][0].reshape(NKEYS, NKEYS, DC, P).transpose(0, 3, 2, 1).reshape(NKEYS, P, D),
        "expert_v": x["expert_v_2"][0].reshape(NKEYS, NKEYS, D),
    }


def kernel(**inputs):
    import concourse.bacc as bacc
    from concourse.bass_utils import run_bass_kernel_spmd

    nc = bacc.Bacc("TRN2", target_bir_lowering=False, num_devices=1)
    arrays = {f"in_{k}": np.ascontiguousarray(v) for k, v in pack({k: np.asarray(v) for k, v in inputs.items()}).items()}
    io = {k[3:]: nc.dram_tensor(k, a.shape, mybir.dt.from_np(a.dtype), kind="ExternalInput").ap()
          for k, a in arrays.items()}
    io["out"] = nc.dram_tensor("out", (T, D), F32, kind="ExternalOutput").ap()
    program(nc, io)
    r = run_bass_kernel_spmd(nc, [arrays], core_ids=[0])
    return r.results[0]["out"].reshape(1, T, D)
```

```python
import math
from contextlib import ExitStack

import numpy as np

import concourse.bass as bass
from concourse import mybir

F32 = mybir.dt.float32
F32R = mybir.dt.float32r
BF16 = mybir.dt.bfloat16
I32 = mybir.dt.int32
U32 = mybir.dt.uint32
ALU = mybir.AluOpType
ACT = mybir.ActivationFunctionType
AX = mybir.AxisListType

P = 128
T = 256
TT = T // P
D = 1024
DC = D // P
FF = 2816
FC = FF // P
EPS = 1e-6
NEG = -1e30
GROUPS = 4
GHEADS = 8
HD = 64
GI = GHEADS * HD
CONV = 4
WINDOW = 128
BUCKETS = 32
MAX_DIST = WINDOW
MLA_Q, MLA_KV, ROPE, NOPE = 384, 256, 32, 64
QK = ROPE + NOPE
THETA = 10000.0
LN_EPS = 64e-5
RC = 4
CH = T // RC
PH = 8
TOPK = 16
NKEYS = 128
SLOTS = 4



def layout(items):
    at, out = 0, {}
    for name, n in items:
        out[name] = (at, n)
        at += n
    return out, at


CONSTS, N_CONSTS = layout([
    ("ident", P), ("ones", P), ("blk64", P), ("causal", 384), ("mla_mask", 384),
    ("up_strict", CH), ("up_incl", CH), ("whole", CH), ("low_strict", CH),
    ("u16", P), ("l16", P), ("u32", P), ("l32", P), ("l64", P),
    ("iota", P), ("rot", QK), ("onehot", 384), ("outside", 384), ("half", 1),
    ("inv_freq", 1), ("is_rope", 1), ("not_rope", 1),
])


def constants():
    c = np.zeros((P, N_CONSTS), np.float32)

    def put(name, a):
        at, n = CONSTS[name]
        a = np.asarray(a, np.float32).reshape(a.shape[0], n)
        c[:a.shape[0], at:at + n] = a

    i = np.arange(P)
    put("ident", np.eye(P))
    put("ones", np.ones((P, P)))
    same = (i[:, None] // HD) == (i[None, :] // HD)
    put("blk64", same)
    late = i[None, :] >= i[:, None]
    put("causal", np.concatenate([late, np.ones((P, P)), late], 1))
    tok = np.arange(T)
    mask = np.stack([np.where(tok[None, :] // 64 <= (b * P + i)[:, None] // 64, 0, NEG) for b in range(TT)], 1)
    put("mla_mask", np.concatenate([mask[:, 0, 0:P], mask[:, 1, :]], 1))
    r, t = (i % CH)[:, None], np.arange(CH)[None, :]
    put("up_strict", r < t)
    put("up_incl", r <= t)
    put("whole", np.ones((P, CH)))
    put("low_strict", r > t)
    a, b = i[:, None], i[None, :]
    for n, lo in ((16, 1), (32, 16), (64, 32)):
        level = (a // n == b // n) & ((a // lo != b // lo) if lo > 1 else True) & (a < b)
        put(f"l{n}", level.T)
        if n < 64:
            put(f"u{n}", level)
    put("iota", np.tile(np.arange(P), (P, 1)))
    half = ROPE // 2
    rot = np.zeros((QK, QK))
    for j in range(half):
        rot[NOPE + half + j, NOPE + j] = -1
        rot[NOPE + j, NOPE + half + j] = 1
    put("rot", rot)
    y = np.arange(384)
    dist = 255 - y
    inside = (dist >= 0) & (dist < WINDOW)
    exact = BUCKETS // 2
    nf = np.maximum(dist, 1).astype(np.float32)
    large = exact + (np.log(nf / np.float32(exact)) / np.float32(math.log(MAX_DIST / exact))
                     * np.float32(BUCKETS - exact)).astype(np.int32)
    bucket = np.where(np.maximum(dist, 0) < exact, np.maximum(dist, 0), np.minimum(large, BUCKETS - 1))
    put("onehot", (np.arange(BUCKETS)[:, None] == bucket[None, :]) & inside[None, :])
    put("outside", np.tile(np.where(inside, 0, NEG), (P, 1)))
    put("half", np.full((P, 1), math.pi / 2))
    inv = (np.float32(THETA) ** (-np.arange(half, dtype=np.float32) / np.float32(half))).astype(np.float32)
    put("inv_freq", np.concatenate([np.zeros(NOPE), inv, inv])[:, None])
    put("is_rope", (np.arange(QK) >= NOPE)[:, None])
    put("not_rope", (np.arange(QK) < NOPE)[:, None])
    return c


VECS, N_VECS = layout([
    ("g_ffn0", DC), ("g_ffn1", DC), ("g_ffn2", DC), ("g_ffn3", DC), ("g_ssm", DC), ("g_kv", DC),
    ("g_attn", DC), ("g_mix", DC), ("g_peer", DC),
    ("conv_w", GROUPS * 6 * CONV), ("conv_b", GROUPS * 6), ("d_skip", GROUPS * 4), ("g_gate", GROUPS * 4),
    ("dt_bias", 1), ("a_log", 1), ("k_norm", 1), ("q_norm", 1), ("sinks", 16),
    ("g_cq", 3), ("g_ckv", 2), ("g_qnorm", 1), ("g_knorm", 1), ("g_out", 4),
    ("mu", 14), ("w0", 4), ("a0", 4), ("k_k", 4), ("k_a", 4), ("r_k", 4), ("lnw", 4), ("lnb", 4),
])


def tiles(w, width=P):
    k, n = w.shape[0] // P, w.shape[1] // width
    return w.reshape(k, P, n, width).transpose(2, 1, 0, 3).reshape(n, P, k * width)


KH = NKEYS // 2
PRE = (3 * PH, 8)
RING_PLAN = {
    **{f"ffn{k}": (FC // 2, [2, 2, 1, 1]) for k in range(4)},
    "dt": (1, [0, 0, 0, 1]),
    "ssm_first": (1, [2, 2, 1, 1]),
    "ssm": (GROUPS - 1, [3, 3, 2, 2]),
    "ssm_last": (1, [1, 1, 1, 1]),
    "ssm_out": (GROUPS, [1, 1, 1, 1]),
    "kv": (1, [1, 1, 1, 0]),
    "attn": (4, [1, 1, 0, 0]),
    "attn_out": (2, [1, 1, 1, 1]),
    "rwkv": (2, [2, 2, 2, 1]),
    "mla": (1, [2, 2, 1, 1]),
    "mla_heads": (2, [1, 1, 0, 0]),
    "mix_out": (2, [1, 1, 1, 1]),
    "route": (PH, [1, 1, 2, 1]),
    "peer_v0": (PRE[0] // 2, [0, 1, 0, 1]),
    "peer_b0": ((KH - PRE[0]) // 2, [1, 1, 1, 1]),
    "peer_u1": (PRE[1] // 2, [1, 0, 1, 0]),
    "peer_v1": (PRE[1] // 2, [0, 1, 0, 1]),
    "peer_b1": ((KH - PRE[1]) // 2, [1, 1, 1, 1]),
}
SPLIT_STAGES = ("ffn0", "ffn1", "ffn2", "ffn3", "ssm", "rwkv", "peer")
LOG_AND_EXP = "natural_log_exp_and_others"
OUT_RINGS = ("ssm_out", "attn_out", "mix_out")
SPLIT_RINGS = SPLIT_STAGES + ("ssm_first", "ssm_last", "mla", "peer_v0", "peer_b0", "peer_v1", "peer_b1") + OUT_RINGS
RING_OF = {"ssm": ("dt", "ssm_first", "ssm", "ssm_last", "ssm_out"), "attn": ("attn", "attn_out"), "mla": ("mla", "mla_heads"), "mix": ("mix_out",),
           "peer": ("route", "peer_v0", "peer_b0", "peer_u1", "peer_v1", "peer_b1")}
LEAD = {**{f"ffn{k}": [(0, f"ffn{k}"), (1, f"ffn{k}"), (2, f"ffn{k}")] for k in range(4)},
        "ssm": [(0, "ssm_first"), (1, "ssm_first"), (2, "ssm_first")],
        "rwkv": [(n, "rwkv") for n in range(4)]}
STAGES = ["ffn0", "ssm", "ffn1", "kv", "ffn2", "attn", "ffn3", "rwkv", "mla", "mix", "peer"]


def program(nc, io, stages=STAGES):
    norm_no = {s: n for n, s in enumerate([s for s in stages if s not in ("mla", "mix")])}
    sums = [s for s in stages if s not in ("kv", "rwkv", "mla")]
    upd = {s: len([x for x in stages[:stages.index(s)] if x in sums]) for s in stages}
    ffn_no = {s: n for n, s in enumerate([s for s in stages if s.startswith("ffn")])}
    split_norms = {norm_no[s]: len([x for x in SPLIT_STAGES if x in stages and norm_no[x] < norm_no[s]]) for s in norm_no}
    ring_order = [r for s in stages for r in RING_OF.get(s, (s,))]

    def use(stage, slot, i=0, nth=0):
        before = sum(RING_PLAN[r][0] * RING_PLAN[r][1][slot] for r in ring_order[:ring_order.index(stage)])
        return before + nth + i * RING_PLAN[stage][1][slot]

    def use_split(stage, slot, i=0, nth=0):
        order = [r for r in ring_order if r in SPLIT_RINGS]
        before = sum(RING_PLAN[r][0] * RING_PLAN[r][1][slot] for r in order[:order.index(stage)])
        return before + nth + i * RING_PLAN[stage][1][slot]

    ctx = ExitStack()
    sems = {}

    def S(name):
        if name not in sems:
            sems[name] = ctx.enter_context(nc.semaphore(name))
        return sems[name]

    def sb(name, shape, dt=F32):
        return ctx.enter_context(nc.sbuf_tensor(name, shape, dt))

    with ctx:
        con = sb("con", [P, N_CONSTS])
        vec = sb("vec", [P, N_VECS])
        h = sb("h", [P, TT, D])
        u_t = sb("u_t", [P, DC, T])
        ring = [sb(f"ring{s}", [P, D]) for s in range(SLOTS)]
        w_hi = [sb(f"w_hi{s}", [P, D], F32R) for s in range(SLOTS)]
        w_lo = [sb(f"w_lo{s}", [P, D], F32R) for s in range(SLOTS)]
        u_hi, u_lo = sb("u_hi", [P, DC, T], F32R), sb("u_lo", [P, DC, T], F32R)
        x_hi, x_lo = sb("x_hi", [P, 2, T], F32R), sb("x_lo", [P, 2, T], F32R)
        zeros = sb("zeros", [P, 512], BF16)
        stat = sb("stat", [P, 16])
        credit = sb("credit", [P, 1])
        arena = sb("arena", [P, 28064])
        bank = [ctx.enter_context(nc.psum_tensor(f"bank{i}", [P, 512], F32)) for i in range(8)]
        ACC = bank[0:4]
        UP = bank[4:6]
        TP = bank[6:8]
        ROT = bank[4:8]

        def C(name, a=0, b=None):
            at, n = CONSTS[name]
            return con[:, at + a:at + (n if b is None else b)]

        def V(name, a=0, b=None):
            at, n = VECS[name]
            return vec[:, at + a:at + (n if b is None else b)]

        def VD(name, start, n=1):
            return vec[:, bass.ds(VECS[name][0] + start, n)]

        def area(at, *shape):
            n = int(np.prod(shape))
            a = arena[:, at:at + n]
            if len(shape) == 2:
                a = a.rearrange("p (a b) -> p a b", a=shape[0])
            if len(shape) == 3:
                a = a.rearrange("p (a b c) -> p a b c", a=shape[0], b=shape[1])
            return a

        def spread(col, n):
            return col.unsqueeze(2).broadcast_to([col.shape[0], col.shape[1], n])

        full = [S(f"slot_full{s}") for s in range(SLOTS)]
        freed = [S(f"slot_freed{s}") for s in range(SLOTS)]
        hi_made = [S(f"hi_made{s}") for s in range(SLOTS)]
        split_read = [S(f"split_read{s}") for s in range(SLOTS)]

        def load(sp, slot, src, stage, i=0, nth=0):
            sp.wait_ge(freed[slot], use(stage, slot, i, nth) + 1)
            sp.dma_start(ring[slot][:, 0:src.shape[-1]], src).then_inc(full[slot], 16)

        def arrived(pe, slot, stage, i=0, nth=0):
            pe.wait_ge(full[slot], (use(stage, slot, i, nth) + 1) * 16)

        def multiplied(eng, slot, stage, i=0, nth=0):
            eng.wait_ge(freed[slot], use(stage, slot, i, nth) + 2)

        def make_hi(act, slot, stage, i, nth=0):
            act.wait_ge(full[slot], (use(stage, slot, i, nth) + 1) * 16)
            act.wait_ge(split_read[slot], use_split(stage, slot, i, nth) + 1)
            act.activation(w_hi[slot][:, :], ring[slot][:, :], ACT.Copy).then_inc(hi_made[slot], 1)

        def make_lo(dve, slot, stage, i, nth=0):
            dve.wait_ge(hi_made[slot], use_split(stage, slot, i, nth) + 1)
            dve.tensor_tensor(w_lo[slot][:, :], ring[slot][:, :], w_hi[slot][:, :].bitcast(F32),
                              ALU.subtract).then_inc(freed[slot], 1)

        def lead_scalar(act, stage):
            for slot, ring_stage in LEAD.get(stage, ()):
                make_hi(act, slot, ring_stage, 0)

        def lead_vector(dve, before):
            after = stages[stages.index(before) + 1:][:1] if before else stages[:1]
            for slot, ring_stage in LEAD.get(after[0], ()) if after else ():
                make_lo(dve, slot, ring_stage, 0)

        def split_done(eng, slot, stage, i, nth=0):
            eng.wait_ge(split_read[slot], use_split(stage, slot, i, nth) + 2)

        def passes(pe, out, left, right, start, stop):
            for n, (a, b) in enumerate(((0, 0), (0, 1), (1, 0))):
                mm = pe.matmul(out, left[a], right[b], start=start and n == 0, stop=stop and n == 2,
                               skip_group_check=True)
            return mm

        def project_split(pe, out, slot, stage, i, nth=0, first=False):
            multiplied(pe, slot, stage, i, nth)
            for c in range(DC):
                cols = slice(c * P, (c + 1) * P)
                if first and c % (DC // 2) == 0:
                    u_split_ready(pe, stage, 2 + c // 2)
                mm = passes(pe, out, (w_hi[slot][:, cols], w_lo[slot][:, cols]), (u_hi[:, c, :], u_lo[:, c, :]),
                            c == 0, c == DC - 1)
            return mm.then_inc(split_read[slot], 1)

        def close_split(pe, b, slot, stage, i, last=False):
            multiplied(pe, slot, stage, i)
            for q in range(4):
                rows, cols = slice((q // 2) * P, (q // 2 + 1) * P), slice((q % 2) * 512, (q % 2 + 1) * 512)
                mm = passes(pe, ACC[q][:, :], (x_hi[:, b, rows], x_lo[:, b, rows]),
                            (w_hi[slot][:, cols], w_lo[slot][:, cols]), False, last)
            return mm.then_inc(split_read[slot], 1)

        def project(pe, out, slot, width=P):
            for c in range(DC):
                mm = pe.matmul(out, ring[slot][:, c * width:(c + 1) * width], u_t[:, c, :],
                               start=(c == 0), stop=(c == DC - 1))
            return mm

        def close_into(pe, left, right, last=False):
            for q in range(4):
                mm = pe.matmul(ACC[q][:, :], left[:, (q // 2) * P:(q // 2 + 1) * P],
                               right[:, (q % 2) * 512:(q % 2 + 1) * 512],
                               start=False, stop=last, skip_group_check=True)
            return mm

        def clear_acc(pe, updates):
            pe.wait_ge(S("h_updated"), 4 * updates + 1)
            for q in range(4):
                pe.matmul(ACC[q][:, :], zeros[:, 0:P], zeros[:, :], start=True, stop=False,
                          skip_group_check=True)


        def out_sync(sp, stage, weight):
            with sp.Fori(0, RING_PLAN[stage][0]) as i:
                for n in range(4):
                    load(sp, n, weight[bass.ds(4 * i + n, 1), :, :], stage, i)

        def left_no(stage, i, n):
            order = [r for r in ring_order if r in OUT_RINGS]
            return sum(4 * RING_PLAN[r][0] for r in order[:order.index(stage)]) + 4 * i + n

        def out_tensor(pe, stage, updates):
            bodies = RING_PLAN[stage][0]

            def body(i, last):
                for n in range(4):
                    pe.wait_ge(S("left_ready"), left_no(stage, i, n) + 1)
                    close_split(pe, n % 2, n, stage, i, last and n == 3)

            clear_acc(pe, updates)
            with pe.Fori(0, bodies - 1) as i:
                body(i, False)
            body(bodies - 1, True)

        def out_scalar(act, stage, src):
            with act.Fori(0, RING_PLAN[stage][0]) as i:
                for n in range(4):
                    make_hi(act, n, stage, i)
                    before = (n + 2) % 4
                    act.wait_ge(split_read[before], use_split(stage, before, i) + (1 if n < 2 else 2))
                    act.activation(x_hi[:, n % 2:n % 2 + 1, :], src[:, bass.ds(4 * i + n, 1), :],
                                   ACT.Copy).then_inc(S("left_hi"), 1)

        def out_vector(dve, stage, src):
            bodies = RING_PLAN[stage][0]
            with dve.Fori(0, bodies) as i:
                for n in range(4):
                    make_lo(dve, n, stage, i)
                    dve.wait_ge(S("left_hi"), left_no(stage, i, n) + 1)
                    dve.tensor_tensor(x_lo[:, n % 2:n % 2 + 1, :], src[:, bass.ds(4 * i + n, 1), :],
                                      x_hi[:, n % 2:n % 2 + 1, :].bitcast(F32), ALU.subtract).then_inc(S("left_ready"), 1)
            lead_vector(dve, stage.removesuffix("_out"))
            split_done(dve, 3, stage, bodies - 1)
            update_h(dve, 1.0)

        def rstd(act, out, src, n, eps):
            act.activation(out, src, ACT.Ln, scale=1.0 / n, bias=eps)
            act.drain()
            return act.activation(out, out, ACT.Exp, scale=-0.5)

        norm_square = area(0, 2, D)
        norm_u = area(2 * D, 2, D)

        def norm_scalar(act, m, updates, split):
            act.preload_act_table_set(LOG_AND_EXP)
            act.wait_ge(S("h_loaded"), 16)
            act.wait_ge(S("in_loaded"), 32)
            for tt in range(TT):
                act.wait_ge(S("h_updated"), max(4 * updates - 2 + 2 * tt + 1, 1))
                act.activation(norm_square[:, tt, :], h[:, tt, :], ACT.Square, accum_out=stat[:, tt:tt + 1])
                act.drain()
                rstd(act, stat[:, 4 + tt:5 + tt], stat[:, tt:tt + 1], D, stat[:, 14:15]).then_inc(S("norm_root"), 1)
            if split:
                for q in range(4):
                    act.wait_ge(S("u_ready"), 4 * m + q + 1)
                    act.activation(quarter(u_hi, q), quarter(u_t, q), ACT.Copy).then_inc(S("u_hi_made"), 1)

        def quarter(u, q):
            return u[:, 4 * (q % 2):4 * (q % 2) + 4, (q // 2) * P:(q // 2 + 1) * P]

        def norm_vector(dve, m, gain, split):
            def lo(q):
                dve.wait_ge(S("u_hi_made"), 4 * split_norms[m] + q + 1)
                dve.tensor_tensor(quarter(u_lo, q), quarter(u_t, q), quarter(u_hi, q).bitcast(F32),
                                  ALU.subtract).then_inc(S("u_split"), 1)

            for tt in range(TT):
                dve.wait_ge(S("norm_root"), 2 * m + tt + 1)
                dve.tensor_scalar(norm_u[:, tt, :], h[:, tt, :], stat[:, 4 + tt:5 + tt], None,
                                  ALU.mult).then_inc(S("norm_rows"), 1)
            for q in range(4):
                half = q % 2
                dve.wait_ge(S("norm_turned"), 4 * m + q + 1)
                dve.tensor_tensor(quarter(u_t, q), TP[q % 2][:, :].rearrange("p (c t) -> p c t", c=4),
                                  spread(V(gain, 4 * half, 4 * half + 4), P), ALU.mult).then_inc(S("u_ready"), 1)
                for done in ((), (0,), (2,), (1, 3))[q] if split else ():
                    lo(done)

        def norm_tensor(pe, m, split):
            for q in range(4):
                tt, half = q // 2, q % 2
                pe.wait_ge(S("norm_rows"), 2 * m + tt + 1)
                if q >= 2:
                    pe.wait_ge(S("u_ready"), 4 * m + q - 1)
                for c in range(4):
                    at = (4 * half + c) * P
                    mm = pe.transpose(TP[q % 2][:, c * P:(c + 1) * P], norm_u[:, tt, at:at + P], C("ident"))
                mm.then_inc(S("norm_turned"), 1)
            if not split:
                pe.wait_ge(S("u_ready"), 4 * m + 4)

        def u_split_ready(pe, stage, quarters=4):
            pe.wait_ge(S("u_split"), 4 * split_norms[norm_no[stage]] + quarters)

        def update_h(dve, scale):
            for q in range(4):
                part = h[:, q // 2, (q % 2) * 512:(q % 2 + 1) * 512]
                dve.scalar_tensor_tensor(part, ACC[q][:, :], scale, part, ALU.mult,
                                         ALU.add).then_inc(S("h_updated"), 1)

        silu_buf = area(4 * D, 2, T)
        hid_buf = area(4 * D + 2 * T, 2, T)

        def ffn_tile(kind, k, i, b):
            return (2 + b, f"ffn{k}", i, 0) if kind == 2 else (kind, f"ffn{k}", i, b)

        def ffn_next(k, i, b):
            return (0, i + 1, b), (1, i + 1, b), (2, i + b, 1 - b)

        def ffn_sync(sp, k):
            def tile(kind, i, b):
                load(sp, ffn_tile(kind, k, i, b)[0], io[("w1", "w3", "w2")[kind]][k, bass.ds(2 * i + b, 1), :, :],
                     *ffn_tile(kind, k, i, b)[1:])

            for kind, b in ((0, 0), (1, 0), (2, 0), (0, 1), (1, 1)):
                tile(kind, 0, b)
            with sp.Fori(0, FC // 2 - 1) as i:
                for b in range(2):
                    for ahead in ffn_next(k, i, b):
                        tile(*ahead)
            tile(2, FC // 2 - 1, 1)

        def ffn_tensor(pe, k, updates):
            stage = f"ffn{k}"
            base = FC * ffn_no[stage]

            def up(b, i, first=False):
                pe.wait_ge(S("hid_ready"), base + 2 * i + b + 1)
                for n in range(2):
                    project_split(pe, UP[b][:, n * T:(n + 1) * T], *ffn_tile(n, k, i, b), first=first and n == 0)

            def down(b, i, last=False):
                pe.wait_ge(S("hid_ready"), base + 2 * i + b + 3)
                close_split(pe, b, 2 + b, stage, i, last)

            clear_acc(pe, updates)
            up(0, 0, first=True)
            with pe.Fori(0, FC // 2 - 1) as i:
                up(1, i)
                down(0, i)
                up(0, i + 1)
                down(1, i)
            up(1, FC // 2 - 1)
            down(0, FC // 2 - 1)
            down(1, FC // 2 - 1, last=True)

        def ffn_scalar(act, k):
            def silu(b, i):
                split_done(act, *ffn_tile(1, k, i, b))
                act.activation(silu_buf[:, b, :], UP[b][:, 0:T], ACT.Silu).then_inc(S("silu_ready"), 1)

            act.preload_act_table(ACT.Silu)
            for kind in range(2):
                make_hi(act, *ffn_tile(kind, k, 0, 1))
            with act.Fori(0, FC // 2 - 1) as i:
                for b in range(2):
                    silu(b, i)
                    for kind, *at in ffn_next(k, i, b):
                        make_hi(act, *ffn_tile(kind, k, *at))
            silu(0, FC // 2 - 1)
            make_hi(act, *ffn_tile(2, k, FC // 2 - 1, 1))
            silu(1, FC // 2 - 1)

        def ffn_vector(dve, k):
            stage = f"ffn{k}"
            base = FC * ffn_no[stage]

            def gate(b, i):
                dve.wait_ge(S("silu_ready"), base + 2 * i + b + 1)
                dve.wait_ge(split_read[2 + b], use_split(stage, 2 + b, i) + 1)
                dve.tensor_tensor(x_hi[:, b, :], silu_buf[:, b, :], UP[b][:, T:2 * T], ALU.mult)
                dve.tensor_tensor(hid_buf[:, b, :], silu_buf[:, b, :], UP[b][:, T:2 * T], ALU.mult)
                dve.drain()
                dve.tensor_tensor(x_lo[:, b, :], hid_buf[:, b, :], x_hi[:, b, :].bitcast(F32),
                                  ALU.subtract).then_inc(S("hid_ready"), 1)

            for kind in range(2):
                make_lo(dve, *ffn_tile(kind, k, 0, 1))
            with dve.Fori(0, FC // 2 - 1) as i:
                for b in range(2):
                    gate(b, i)
                    for kind, *at in ffn_next(k, i, b):
                        make_lo(dve, *ffn_tile(kind, k, *at))
            gate(0, FC // 2 - 1)
            make_lo(dve, *ffn_tile(2, k, FC // 2 - 1, 1))
            gate(1, FC // 2 - 1)
            lead_vector(dve, stage)
            split_done(dve, 3, stage, FC // 2 - 1)
            update_h(dve, 0.5)

        GAIN = {"ffn0": "g_ffn0", "ssm": "g_ssm", "ffn1": "g_ffn1", "kv": "g_kv", "ffn2": "g_ffn2", "attn": "g_attn",
                "ffn3": "g_ffn3", "rwkv": "g_mix", "peer": "g_peer"}
        SYNC, POOL, SCALAR, VECTOR, TENSOR = {}, {}, {}, {}, {}

        x_pad = area(4096, 6, 260)
        conv = area(5696, 6, T)
        z_act = area(7232, 4, T)
        xdt = area(8256, TT, GI)
        cb = area(9280, 384)
        decay = area(9664, GHEADS, 384)
        y_grp = area(12736, 4, T)
        y_sq = area(13760, 4, T)
        y_all = area(0, 4 * GROUPS, T)
        y_root = area(15808, T)
        acum_all = area(16384, 4 * GHEADS, T)
        dt_work = area(24576, 5, T)
        dt_cols = area(25856, 4, 32)
        acum_dram = nc.dram_tensor("acum_dram", (32, T), F32, kind="Internal").ap()
        H32 = slice(0, 32)

        def ssm_sync(sp):
            load(sp, 3, io["ssm_dt"], "dt")
            for n in range(6):
                load(sp, n % 4, io["ssm_in"][0, n, :, :], "ssm_first", 0, n // 4)
            with sp.Fori(0, GROUPS - 1) as i:
                for n in range(10):
                    src = io["ssm_in"][bass.ds(i, 1), 6 + n, :, :] if n < 4 else io["ssm_in"][bass.ds(i + 1, 1), n - 4, :, :]
                    load(sp, n % 4, src, "ssm", i, n // 4)
            for n in range(4):
                load(sp, n, io["ssm_in"][GROUPS - 1, 6 + n, :, :], "ssm_last")
            out_sync(sp, "ssm_out", io["ssm_out"])

        def ssm_pool(pool):
            pool.wait_ge(S("acum_ready"), 1)
            pool.dma_start(acum_dram, dt_work[H32, 4, :]).then_inc(S("acum_stored"), 16)
            pool.wait_ge(S("acum_stored"), 16)
            for i in range(GROUPS):
                if i:
                    pool.wait_ge(S("decay_ready"), 2 * i - 1)
                rows = slice(GHEADS * i, GHEADS * (i + 1))
                pool.dma_start(acum_all[:, rows, :], acum_dram[rows, :].unsqueeze(0).broadcast_to([P, GHEADS, T])).then_inc(
                    S("acum_spread"), 16)


        def place(n, i):
            if isinstance(i, int) and i < 0:
                return (n - 4) % 4, "ssm_first", 0, (n - 4) // 4
            return n % 4, "ssm", i, n // 4

        def next_place(n, i):
            if isinstance(i, int) and i < 0:
                return place(n + 4, i) if n < 6 else place((2, 3, 0, 1)[n - 6], 0)
            return place(n + 4, i) if n < 6 else place((2, 3, 0, 1)[n - 6], i + 1)

        def ssm_tensor(pe):
            arrived(pe, 3, "dt")
            pe.wait_ge(S("u_ready"), 4 * norm_no["ssm"] + 4)
            project(pe, UP[0][H32, 0:T], 3, 32).then_inc(freed[3], 1)
            u_split_ready(pe, "ssm")

            def project_place(n, i):
                pe.wait_ge(S("ssm_evicted"), 10 * i + 6 + n + (3 if n < 2 else 1))
                slot, stage, body, nth = place(n, i)
                project_split(pe, bank[slot][:, 0:T], slot, stage, body, nth)

            for n in range(4, 10):
                project_place(n, -1)
            pe.wait_ge(S("acum_ready"), 1)
            for n in range(4):
                src = dt_work[H32, 4 if n < 2 else 2, (n % 2) * P:(n % 2 + 1) * P]
                mm = pe.transpose(TP[0][:, n * 32:(n + 1) * 32], src, C("ident", 0, 32)[H32, :])
            mm.then_inc(S("dt_turned"), 1)
            pe.wait_ge(S("dt_cols_ready"), 1)

            def body(i, more=True):
                def ahead(*places):
                    for n in places if more else ():
                        project_place(n, i)

                for n in range(4):
                    project_place(n, i)
                pe.wait_ge(S("y_normed"), i + 1)
                pe.wait_ge(S("conv_act"), 6 * i + 6)
                for tt in range(TT):
                    for k in range(4):
                        mm = pe.transpose(TP[tt][:, k * P:(k + 1) * P], conv[:, 2 + k, tt * P:(tt + 1) * P], C("ident"))
                    mm.then_inc(S("x_turned"), 1)
                ahead(4, 5)
                pe.wait_ge(S("xdt_ready"), 2 * i + 1)
                pe.matmul(TP[0][:, 0:T], conv[:, 0, 0:P], conv[:, 1, :], start=True, stop=True)
                pe.matmul(TP[0][:, T:384], conv[:, 0, P:T], conv[:, 1, P:T], start=True,
                          stop=True).then_inc(S("cb_done"), 1)
                ahead(6, 7)
                pe.wait_ge(S("xdt_ready"), 2 * i + 2)
                for r in range(GHEADS):
                    pe.wait_ge(S("scores_ready"), 2 * i + r // 4 + 1)
                    k, a = r // 2, (r % 2) * HD
                    out = ROT[k][a:a + HD, 0:T]
                    pe.matmul(out, xdt[:, 0, r * HD:(r + 1) * HD], decay[:, r, 0:T], start=True, stop=False,
                              skip_group_check=True)
                    mm = pe.matmul(out[:, P:T], xdt[:, 1, r * HD:(r + 1) * HD], decay[:, r, T:384], start=False,
                                   stop=True, skip_group_check=True)
                    if r % 2:
                        mm.then_inc(S("y_done"), 1)
                ahead(8)
                pe.wait_ge(S("y_squared"), i + 1)
                for k in range(4):
                    mm = pe.matmul(TP[1][:, 0:T], C("ones"), y_sq[:, k, :], start=(k == 0), stop=(k == 3))
                mm.then_inc(S("y_summed"), 1)
                ahead(9)

            with pe.Fori(0, GROUPS - 1) as i:
                body(i)
            body(GROUPS - 1, more=False)
            out_tensor(pe, "ssm_out", upd["ssm"])

        def ssm_scalar(act):
            make_hi(act, *place(7, -1))
            act.wait_ge(S("dt_raw"), 1)
            act.activation(dt_work[H32, 1, :], dt_work[H32, 0, :], ACT.Abs)
            act.drain()
            act.activation(dt_work[H32, 1, :], dt_work[H32, 1, :], ACT.Exp, scale=-1.0)
            act.activation(stat[H32, 6:7], V("a_log")[H32, :], ACT.Exp)
            act.drain()
            act.activation(dt_work[H32, 1, :], dt_work[H32, 1, :], ACT.Ln, bias=C("ones", 0, 1)[H32, :]).then_inc(S("dt_log"), 1)

            def evict(n, i, more=True):
                slot, stage, body, nth = place(n, i)
                split_done(act, slot, stage, body, nth)
                src = bank[slot][:, 0:T]
                if n < 4:
                    act.activation(z_act[:, n, :], src, ACT.Silu).then_inc(S("ssm_evicted"), 1)
                else:
                    act.activation(x_pad[:, n - 4, CONV - 1:CONV - 1 + T], src, ACT.Copy).then_inc(S("ssm_evicted"), 1)
                if more:
                    make_hi(act, *next_place(n, i))

            def conv_silu(i, *tiles_of):
                for n in tiles_of:
                    act.wait_ge(S("conv_done"), 6 * i + n + 1)
                    act.activation(conv[:, n, :], conv[:, n, :], ACT.Silu).then_inc(S("conv_act"), 1)

            def body(i, more=True):
                def ahead(*places):
                    for n in places if more else ():
                        evict(n, i)

                act.preload_act_table(ACT.Silu)
                evict(0, i, more)
                evict(1, i, more)
                conv_silu(i, 0, 1)
                evict(2, i, more)
                evict(3, i, more)
                conv_silu(i, 2, 3, 4, 5)
                act.preload_act_table_set(LOG_AND_EXP)
                for b in range(2):
                    act.wait_ge(S("decay_ready"), 2 * i + b + 1)
                    part = decay[:, 4 * b:4 * b + 4, :]
                    act.activation(part, part, ACT.Exp).then_inc(S("decay_exp"), 1)
                ahead(4, 5, 6, 7)
                act.wait_ge(S("y_gated"), i + 1)
                act.activation(y_sq[:, :, :], y_grp[:, :, :], ACT.Square).then_inc(S("y_squared"), 1)
                ahead(8)
                act.wait_ge(S("y_summed"), i + 1)
                rstd(act, y_root, TP[1][:, 0:T], GI, stat[:, 14:15]).then_inc(S("y_rooted"), 1)
                ahead(9)

            for n in range(4, 10):
                evict(n, -1)
            with act.Fori(0, GROUPS - 1) as i:
                body(i)
            body(GROUPS - 1, more=False)
            act.wait_ge(S("y_normed"), GROUPS + 1)
            out_scalar(act, "ssm_out", y_all)

        def ssm_vector(dve):
            dve.memset(x_pad[:, :, 0:CONV - 1], 0.0)
            dve.memset(dt_work[H32, 3, :], 1.0)
            dve.drain()
            multiplied(dve, 3, "dt")
            dve.tensor_scalar(dt_work[H32, 0, :], UP[0][H32, 0:T], V("dt_bias")[H32, :], None,
                              ALU.add).then_inc(S("dt_raw"), 1)
            dve.drain()
            dve.tensor_scalar(dt_work[H32, 2, :], dt_work[H32, 0, :], 0.0, None, ALU.max)
            dve.wait_ge(S("dt_log"), 1)
            dve.drain()
            dve.tensor_tensor(dt_work[H32, 2, :], dt_work[H32, 2, :], dt_work[H32, 1, :], ALU.add)
            dve.drain()
            dve.tensor_scalar(dt_work[H32, 0, :], dt_work[H32, 2, :], stat[H32, 6:7], -1.0, ALU.mult, ALU.mult)
            dve.drain()
            dve.tensor_tensor_scan(dt_work[H32, 4, :], dt_work[H32, 3, :], dt_work[H32, 0, :], 0.0, ALU.mult,
                                   ALU.add).then_inc(S("acum_ready"), 1)
            make_lo(dve, *place(7, -1))
            for n in range(4, 10):
                make_lo(dve, *next_place(n, -1))
            dve.wait_ge(S("dt_turned"), 1)
            dve.tensor_copy(dt_cols[:, :, :], TP[0][:, 0:P].rearrange("p (a b) -> p a b", a=4)).then_inc(S("dt_cols_ready"), 1)
            dve.drain()

            def decays(i):
                for r in range(GHEADS):
                    row = acum_all[:, bass.ds(GHEADS * i + r, 1), :]
                    for tt in range(TT):
                        last = dve.tensor_scalar(decay[:, r:r + 1, 0:T] if tt == 0 else decay[:, r:r + 1, T:384],
                                                 row if tt == 0 else acum_all[:, bass.ds(GHEADS * i + r, 1), P:T],
                                                 dt_cols[:, tt, bass.ds(GHEADS * i + r, 1)], 0.0,
                                                 ALU.subtract, ALU.min)
                    if r % 4 == 3:
                        last.then_inc(S("decay_ready"), 1)

            def convolve(i, tiles_of):
                for tap in range(CONV):
                    for n in tiles_of:
                        col = (i * 6 + n) * CONV + tap
                        if tap == 0:
                            dve.wait_ge(S("ssm_evicted"), 10 * i + n + 5)
                            dve.tensor_scalar(conv[:, n, :], x_pad[:, n, 0:T], VD("conv_w", col),
                                              VD("conv_b", i * 6 + n), ALU.mult, ALU.add)
                        else:
                            ins = dve.scalar_tensor_tensor(conv[:, n, :], x_pad[:, n, tap:tap + T],
                                                           VD("conv_w", col), conv[:, n, :], ALU.mult, ALU.add)
                            if tap == CONV - 1:
                                ins.then_inc(S("conv_done"), 1)
                    dve.drain()

            def body(i, more=True):
                def lo_after(*places):
                    for n in places if more else ():
                        make_lo(dve, *next_place(n, i))

                convolve(i, range(2, 6))
                lo_after(0, 1, 2)
                dve.wait_ge(S("acum_spread"), 16 * (i + 1))
                decays(i)
                lo_after(3)
                for tt in range(TT):
                    dve.wait_ge(S("x_turned"), 2 * i + tt + 1)
                    dt_of = dt_cols[:, 2 + tt, bass.ds(GHEADS * i, GHEADS)]
                    dve.tensor_tensor(xdt[:, tt, :].rearrange("p (r q) -> p r q", r=GHEADS),
                                      TP[tt][:, :].rearrange("p (r q) -> p r q", r=GHEADS),
                                      spread(dt_of, HD), ALU.mult).then_inc(S("xdt_ready"), 1)
                dve.wait_ge(S("cb_done"), i + 1)
                dve.tensor_tensor(cb[:, :], TP[0][:, 0:384], C("causal"), ALU.mult)
                dve.drain()
                for b in range(2):
                    dve.wait_ge(S("decay_exp"), 2 * i + b + 1)
                    part = decay[:, 4 * b:4 * b + 4, :]
                    dve.tensor_tensor(part, part, cb.unsqueeze(1).broadcast_to([P, 4, 384]),
                                      ALU.mult).then_inc(S("scores_ready"), 1)
                lo_after(4, 5)
                for k in range(4):
                    dve.wait_ge(S("y_done"), 4 * i + k + 1)
                    dve.scalar_tensor_tensor(y_grp[:, k, :], conv[:, 2 + k, :], VD("d_skip", 4 * i + k),
                                             ROT[k][:, 0:T], ALU.mult, ALU.add)
                dve.drain()
                dve.wait_ge(S("ssm_evicted"), 10 * i + 14)
                dve.tensor_tensor(y_grp[:, :, :], y_grp[:, :, :], z_act[:, :, :], ALU.mult).then_inc(S("y_gated"), 1)
                lo_after(6, 7, 8)
                if more:
                    convolve(i + 1, range(0, 2))
                dve.wait_ge(S("y_rooted"), i + 1)
                for k in range(4):
                    ins = dve.scalar_tensor_tensor(y_all[:, bass.ds(4 * i + k, 1), :], y_grp[:, k:k + 1, :],
                                                   VD("g_gate", 4 * i + k), y_root.unsqueeze(1), ALU.mult, ALU.mult)
                ins.then_inc(S("y_normed"), 1)
                lo_after(9)

            convolve(0, range(0, 2))
            with dve.Fori(0, GROUPS - 1) as i:
                body(i)
            body(GROUPS - 1, more=False)
            out_vector(dve, "ssm_out", y_all)

        POOL["ssm"] = ssm_pool
        SYNC["ssm"], TENSOR["ssm"], SCALAR["ssm"], VECTOR["ssm"] = ssm_sync, ssm_tensor, ssm_scalar, ssm_vector

        k_all = area(5200, 4, T)
        v_all = area(6224, 4, P)
        k_sq = area(6736, 2, T)
        k_root = area(7248, 2, T)
        rel = area(7760, 16)
        bias_line = area(7776, 384)
        bias_all = area(8192, 16, 384)
        line_dram = nc.dram_tensor("line_dram", (16, 384), F32, kind="Internal").ap()
        bias_dram = nc.dram_tensor("bias_dram", (16, P * 384), F32, kind="Internal").ap()

        def kv_sync(sp):
            sp.wait_ge(S("u_ready"), 4 * norm_no["kv"] + 1)
            sp.dma_start(rel[0:BUCKETS, :], io["rel_bias"]).then_inc(S("rel_loaded"), 16)
            for n in range(3):
                load(sp, n, io["w_kv"][n, :, :], "kv")

        def kv_pool(pool):
            pool.wait_ge(S("line_ready"), 1)
            pool.dma_start(line_dram, bias_line[0:16, :]).then_inc(S("line_moved"), 16)
            pool.wait_ge(S("line_moved"), 16)
            pool.dma_start(bias_all[:, :, :], line_dram.unsqueeze(0).broadcast_to([P, 16, 384])).then_inc(S("line_moved"), 16)
            pool.wait_ge(S("line_moved"), 32)
            pool.dma_start(bias_dram.rearrange("h (p y) -> p h y", p=P), bias_all[:, :, :]).then_inc(S("bias_stored"), 16)

        def kv_tensor(pe):
            for n in range(2):
                arrived(pe, n, "kv")
                project(pe, ROT[n][:, 0:T], n).then_inc(freed[n], 1)
            arrived(pe, 2, "kv")
            for tt in range(TT):
                for c in range(DC):
                    mm = pe.matmul(ROT[2][:, tt * P:(tt + 1) * P], u_t[:, c, tt * P:(tt + 1) * P],
                                   ring[2][:, c * P:(c + 1) * P], start=(c == 0), stop=(c == DC - 1))
            mm.then_inc(freed[2], 1)
            pe.wait_ge(S("rel_loaded"), 16)
            pe.matmul(ACC[0][0:16, 0:384], rel[0:BUCKETS, :], C("onehot")[0:BUCKETS, :], start=True,
                      stop=True).then_inc(S("line_done"), 1)
            pe.wait_ge(S("k_squared"), 2)
            pe.matmul(ROT[3][:, :], C("blk64"), k_sq.rearrange("p a b -> p (a b)"), start=True,
                      stop=True).then_inc(S("k_summed"), 1)

        def kv_scalar(act):
            for n in range(2):
                multiplied(act, n, "kv")
                act.activation(k_sq[:, n, :], ROT[n][:, 0:T], ACT.Square).then_inc(S("k_squared"), 1)
            act.wait_ge(S("k_summed"), 1)
            rstd(act, k_root, ROT[3][:, :].rearrange("p (a b) -> p a b", a=2), HD, stat[:, 14:15]).then_inc(S("k_rooted"), 1)

        def kv_vector(dve):
            dve.wait_ge(S("line_done"), 1)
            dve.tensor_tensor(bias_line[0:16, :], ACC[0][0:16, 0:384], C("outside")[0:16, :],
                              ALU.add).then_inc(S("line_ready"), 1)
            multiplied(dve, 2, "kv")
            for i in range(4):
                vs = slice((i // 2) * HD, (i // 2 + 1) * HD)
                dve.tensor_copy(v_all[:, i, :].rearrange("p (a b) -> p a b", a=TT),
                                ROT[2][:, 0:T].rearrange("p (a b) -> p a b", a=TT)[:, :, vs])
            dve.wait_ge(S("k_rooted"), 1)
            for i in range(4):
                dve.scalar_tensor_tensor(k_all[:, i, :], ROT[i // 2][:, 0:T], V("k_norm"), k_root[:, i // 2, :],
                                         ALU.mult, ALU.mult).then_inc(S("k_ready"), 1)
            lead_vector(dve, "kv")

        POOL["kv"] = kv_pool
        SYNC["kv"], TENSOR["kv"], SCALAR["kv"], VECTOR["kv"] = kv_sync, kv_tensor, kv_scalar, kv_vector

        at_sq = area(8192, 2, T)
        at_root = area(8704, 2, T)
        q_t = area(9216, 2, T)
        bias_tile = area(9728, 2, 2, 384)
        prob = area(11264, 2, 2, 384)
        prob_t = area(12800, 2, 2, 384)
        at_stat = area(14336, 2, 6, 4)
        at_v = area(14400, 2, P)
        at_k = area(16704, 2, T)
        o_all = area(14656, 8, T)

        def attn_sync(sp):
            sp.wait_ge(S("bias_stored"), 16)
            sp.wait_ge(S("u_ready"), 4 * norm_no["attn"] + 1)
            with sp.Fori(0, 4) as i:
                for b in range(2):
                    load(sp, b, io["w_q"][bass.ds(2 * i + b, 1), :, :], "attn", i)
                    sp.wait_ge(S("scored"), 4 * i + 2 * b + 2)
                    for a in range(2):
                        table = bias_dram[bass.ds(4 * i + 2 * b + a, 1), 127:127 + P * 383].rearrange(
                            "h (q y) -> q (h y)", y=383)
                        sp.dma_start(bias_tile[:, b, a, 0:P], table[:, P:2 * P]).then_inc(S(f"bias_loaded{b}"), 16)
                        sp.dma_start(bias_tile[:, b, a, P:384], table[:, 0:2 * P]).then_inc(S(f"bias_loaded{b}"), 16)
            out_sync(sp, "attn_out", io["w_o"])

        def attn_tensor(pe):
            def queries(b, i):
                j = 2 * i + b
                arrived(pe, b, "attn", i)
                pe.wait_ge(S("p_turned_out"), 2 * j + 2)
                project(pe, bank[4 * b][:, 0:T], b).then_inc(freed[b], 1)

            def query_sums(b, i):
                pe.wait_ge(S("q_squared"), 2 * i + b + 1)
                pe.matmul(bank[4 * b + 1][:, 0:T], C("blk64"), at_sq[:, b, :], start=True, stop=True).then_inc(S("q_summed"), 1)

            def scores(b, i):
                j = 2 * i + b
                pe.wait_ge(S("q_ready"), j + 1)
                pe.wait_ge(S("o_ready"), j + 1)
                for a in range(2):
                    hs = slice(a * HD, (a + 1) * HD)
                    out = bank[4 * b + 2 + a]
                    pe.matmul(out[:, 0:P], q_t[hs, b, 0:P], at_k[hs, b, 0:P], start=True, stop=True)
                    pe.matmul(out[:, P:384], q_t[hs, b, P:T], at_k[hs, b, :], start=True,
                              stop=True).then_inc(S("scores_done"), 1)

            def turn(b, i):
                for a in range(2):
                    pe.wait_ge(S("prob_ready"), 2 * (2 * i + b) + 1 + a)
                    for n in range(3):
                        mm = pe.transpose(bank[4 * b + a][:, n * P:(n + 1) * P], prob[:, b, a, n * P:(n + 1) * P], C("ident"))
                    mm.then_inc(S("p_turned"), 1)

            def outputs(b, i):
                for a in range(2):
                    pe.wait_ge(S("p_turned_out"), 2 * (2 * i + b) + 5 + a)
                    out = bank[4 * b + 2][a * HD:(a + 1) * HD, :]
                    v = at_v[:, b, :]
                    pe.matmul(out[:, 0:P], v[:, 0:HD], prob_t[:, b, a, 0:P], start=True, stop=True)
                    pe.matmul(out[:, P:T], v[:, 0:HD], prob_t[:, b, a, P:2 * P], start=True, stop=False)
                    mm = pe.matmul(out[:, P:T], v[:, HD:P], prob_t[:, b, a, 2 * P:384], start=False, stop=True)
                mm.then_inc(S("o_done"), 1)

            def step(b, i):
                nb, ni = 1 - b, i + b
                queries(nb, ni)
                turn(b, i)
                query_sums(nb, ni)
                outputs(b, i)
                scores(nb, ni)

            pe.wait_ge(S("h_updated"), 4 * upd["attn"] + 1)
            pe.wait_ge(S("k_ready"), 4)
            queries(0, 0)
            query_sums(0, 0)
            scores(0, 0)
            with pe.Fori(0, 3) as i:
                step(0, i)
                step(1, i)
            step(0, 3)
            turn(1, 3)
            outputs(1, 3)
            pe.wait_ge(S("o_ready"), 8 + 2)
            out_tensor(pe, "attn_out", upd["attn"])

        def attn_scalar(act):
            def square(b, i):
                multiplied(act, b, "attn", i)
                act.activation(at_sq[:, b, :], bank[4 * b][:, 0:T], ACT.Square).then_inc(S("q_squared"), 1)

            def root(b, i):
                act.wait_ge(S("q_summed"), 2 * i + b + 1)
                rstd(act, at_root[:, b, :], bank[4 * b + 1][:, 0:T], HD, stat[:, 14:15]).then_inc(S("q_rooted"), 1)

            def step(b, i, more=True):
                j1 = 2 * i + b + 1
                nb, ni = 1 - b, i + b
                act.wait_ge(S("max_ready"), j1)
                st = at_stat[:, b, :, :]
                for n in range(4):
                    cols = slice(0, P) if n % 2 == 0 else slice(P, 384)
                    act.activation(prob[:, b, n // 2, cols], prob[:, b, n // 2, cols], ACT.Exp,
                                   bias=st[:, 1, n:n + 1], accum_out=st[:, 3, n:n + 1])
                act.activation(st[:, 4, :], st[:, 2, :], ACT.Exp).then_inc(S("prob_exp"), 1)
                if more:
                    square(nb, ni)
                act.activation(at_v[:, b:b + 1, :], v_all[:, bass.ds(i, 1), :], ACT.Copy)
                for a in range(2):
                    act.wait_ge(S("p_turned"), 2 * j1 - 1 + a)
                    act.activation(prob_t[:, b, a, :], bank[4 * b + a][:, 0:384], ACT.Copy).then_inc(S("p_turned_out"), 1)
                if more:
                    root(nb, ni)
                act.wait_ge(S("o_done"), j1)
                act.activation(o_all[:, bass.ds(2 * i + b, 1), :], bank[4 * b + 2][:, 0:T].unsqueeze(1),
                               ACT.Copy).then_inc(S("o_ready"), 1)

            square(0, 0)
            root(0, 0)
            with act.Fori(0, 3) as i:
                step(0, i)
                step(1, i)
            step(0, 3)
            step(1, 3, more=False)
            act.wait_ge(S("o_ready"), 8 + 2)
            out_scalar(act, "attn_out", o_all)

        def attn_vector(dve):
            def query(b, i):
                dve.tensor_copy(at_k[:, b:b + 1, :], k_all[:, bass.ds(i, 1), :])
                dve.wait_ge(S("q_rooted"), 2 * i + b + 1)
                dve.scalar_tensor_tensor(q_t[:, b, :], bank[4 * b][:, 0:T], V("q_norm"), at_root[:, b, :],
                                         ALU.mult, ALU.mult).then_inc(S("q_ready"), 1)

            def step(b, i, more=True):
                j1 = 2 * i + b + 1
                st = at_stat[:, b, :, :]
                dve.wait_ge(S(f"bias_loaded{b}"), 64 * i + 64)
                for a in range(2):
                    dve.wait_ge(S("scores_done"), 2 * j1 - 1 + a)
                    dve.scalar_tensor_tensor(prob[:, b, a, :], bank[4 * b + 2 + a][:, 0:384], HD ** -0.5,
                                             bias_tile[:, b, a, :], ALU.mult, ALU.add).then_inc(S("scored"), 1)
                dve.drain()
                for n in range(4):
                    cols = slice(0, P) if n % 2 == 0 else slice(P, 384)
                    dve.reduce_max(st[:, 0, n:n + 1], prob[:, b, n // 2, cols], AX.X)
                dve.drain()
                sink = spread(VD("sinks", 4 * i + 2 * b, 2), 2)
                view = st.rearrange("p s (a n) -> p s a n", a=2)
                dve.tensor_tensor(view[:, 0, :, :], view[:, 0, :, :], sink, ALU.max)
                dve.drain()
                dve.tensor_tensor(view[:, 2, :, :], sink, view[:, 0, :, :], ALU.subtract)
                dve.tensor_scalar(st[:, 1, :], st[:, 0, :], -1.0, None, ALU.mult)
                dve.drain()
                dve.sem_inc(S("max_ready"), 1)
                dve.wait_ge(S("prob_exp"), j1)
                dve.tensor_tensor(st[:, 3, :], st[:, 3, :], st[:, 4, :], ALU.add)
                dve.drain()
                dve.reciprocal(st[:, 5, :], st[:, 3, :])
                dve.drain()
                for n in range(4):
                    cols = slice(0, P) if n % 2 == 0 else slice(P, 384)
                    ins = dve.tensor_scalar(prob[:, b, n // 2, cols], prob[:, b, n // 2, cols],
                                            st[:, 5, n:n + 1], None, ALU.mult)
                    if n % 2:
                        ins.then_inc(S("prob_ready"), 1)
                if more:
                    query(1 - b, i + b)

            query(0, 0)
            with dve.Fori(0, 3) as i:
                step(0, i)
                step(1, i)
            step(0, 3)
            step(1, 3, more=False)
            out_vector(dve, "attn_out", o_all)

        SYNC["attn"], TENSOR["attn"], SCALAR["attn"], VECTOR["attn"] = attn_sync, attn_tensor, attn_scalar, attn_vector

        raw = area(5200, 14, 260)
        mixed = area(8840, 14, T)
        R_, K_, V_ = mixed[:, 0:4, :], mixed[:, 4:8, :], mixed[:, 8:12, :]
        w_wa, w_g = area(0, 512), area(512, 512)
        wa_act, g_act = area(1024, T), area(1280, T)
        log_decay, cum = area(12424, 4, T), area(13448, 4, T)
        p_now, p_prev, p_inv = area(14472, 4, T), area(15496, 4, T), area(16520, 4, T)
        a_gate, g_gate = area(17544, 4, T), area(18568, 4, T)
        kk, kk_a = area(19592, 4, T), area(20616, 4, T)
        rw_tmp, bonus, y_rw = area(21640, 4, T), area(22664, 4, T), area(23688, 4, T)
        rights = area(26504, 4, 3, CH)
        alpha, rho = rights[:, :, 0, :], rights[:, :, 1, :]
        beta = area(24712, 4, CH)
        diag_alpha, diag_beta, diag_kappa, diag_v = (area(at, 4, P) for at in (24968, 0, 512, 1024))
        (U, UL, A, AL, A2, AL2, A4) = (area(5200 + 512 * n, 4, P) for n in range(7))
        (AL4, A8, AL8, N) = (area(12424 + 512 * n, 4, P) for n in range(4))
        NL = area(25992, 4, P)
        v_st = area(1536, 4, CH)
        of_kappa, of_beta = area(1792, 4, 3, CH), area(2560, 4, 2, CH)
        lk_t, rk_t, kap_st = (of_kappa[:, :, n, :] for n in range(3))
        rb_t, bet_st = (of_beta[:, :, n, :] for n in range(2))
        g_st, s_neg, z_st = (area(3072 + 256 * n, 4, CH) for n in range(3))
        halves = (slice(0, HD), slice(HD, P))

        def quarters(b, n=4):
            return b[:, :].rearrange("p (a b) -> p a b", a=n)

        def flat(t):
            return t.rearrange("p a b -> p (a b)")

        def rwkv_sync(sp):
            for n in range(4):
                load(sp, n, io["rwkv_in"][n, :, :], "rwkv")
            sp.wait_ge(S("u_ready"), 4 * norm_no["rwkv"] + 4)
            sp.dma_start(w_wa, io["w_wa"]).then_inc(S("lora_loaded"), 16)
            sp.dma_start(w_g, io["w_g"]).then_inc(S("lora_loaded"), 16)
            for n in range(4, 14):
                load(sp, n % 7 % 4, io["rwkv_in"][n, :, :], "rwkv", n // 7, n % 7 // 4)

        def rwkv_tensor(pe):
            pe.wait_ge(S("h_updated"), 4 * upd["rwkv"] + 1)
            u_split_ready(pe, "rwkv")
            with pe.Fori(0, 2) as i:
                for n in range(7):
                    pe.wait_ge(S("rw_evicted"), 7 * i + n + 1)
                    project_split(pe, bank[n][:, 0:T], n % 4, "rwkv", i, n // 4)
            pe.wait_ge(S("rw_evicted"), 21)
            pe.wait_ge(S("lora_act"), 1)
            pe.wait_ge(S("lora_loaded"), 32)
            for kind in range(3):
                for p in range(4):
                    cols = slice(p * P, (p + 1) * P)
                    left, right = ((w_wa[0:HD, cols], wa_act[0:HD, :]), (w_wa[HD:P, cols], wa_act[HD:P, :]),
                                   (w_g[:, cols], g_act))[kind]
                    mm = pe.matmul(bank[2 * kind + p // 2][:, (p % 2) * T:(p % 2 + 1) * T], left, right,
                                   start=True, stop=True)
                mm.then_inc(S("lora_done"), 1)
            pe.wait_ge(S("kk_squared"), 1)
            for n in range(2):
                mm = pe.matmul(bank[6 + n][:, :], C("blk64"), flat(rw_tmp)[:, n * 512:(n + 1) * 512], start=True, stop=True)
            mm.then_inc(S("head_sums"), 1)
            pe.wait_ge(S("rk_ready"), 1)
            pe.wait_ge(S("kk_rooted"), 1)
            for n in range(2):
                mm = pe.matmul(bank[6 + n][:, :], C("blk64"), flat(bonus)[:, n * 512:(n + 1) * 512], start=True, stop=True)
            mm.then_inc(S("head_sums"), 1)
            with pe.Fori(0, RC) as c:
                def gram(banks, left):
                    for p in range(4):
                        mm = pe.matmul(bank[banks[p // 2]][:, (p % 2) * 192:(p % 2 + 1) * 192], left[:, p, :],
                                       rights[:, p, :, :].rearrange("p a b -> p (a b)"), start=True, stop=True)
                    mm.then_inc(S("gram_done"), 1)

                pe.wait_ge(S("chunk_ready"), 2 * c + 1)
                gram((2, 3), diag_beta)
                pe.wait_ge(S("diag_ready"), c + 1)
                pe.wait_ge(S("chunk_ready"), 2 * c + 2)
                for p in range(4):
                    mm = pe.matmul(bank[5][:, p * CH:(p + 1) * CH], diag_alpha[:, p, :], beta[:, p, :], start=True, stop=True)
                mm.then_inc(S("gram_done"), 1)
                for p in range(4):
                    mm = pe.matmul(bank[4][:, p * CH:(p + 1) * CH], diag_v[:, p, :], rights[:, p, 2, :], start=True, stop=True)
                mm.then_inc(S("rows_done"), 1)
                gram((6, 7), diag_kappa)

                def level(*products):
                    for b, left, right in products:
                        for p in range(4):
                            mm = pe.matmul(bank[b][:, p * P:(p + 1) * P], left[:, p, :], right[:, p, :], start=True, stop=True)
                    mm.then_inc(S("inv_done"), 1)

                pe.wait_ge(S("inv_sum"), 6 * c + 1)
                level((0, AL, A), (1, A, AL))
                pe.wait_ge(S("lk_ready"), c + 1)
                pe.wait_ge(S("rows_ready"), c + 1)
                pe.wait_ge(S("z_ready"), c + 1)
                pe.sem_inc(S("wait_held"), 1)
                for p in range(4):
                    for a in halves:
                        out = bank[4][a, 256 + p * CH:256 + (p + 1) * CH]
                        pe.matmul(out, alpha[a, p, :], z_st[a, p, :], start=True, stop=False)
                        mm = pe.matmul(out, lk_t[a, p, :], v_st[a, p, :], start=False, stop=True)
                mm.then_inc(S("g_done"), 1)
                pe.wait_ge(S("inv_copied"), 5 * c + 1)
                level((2, AL2, A2), (3, A2, AL2), (5, AL2, N), (6, A2, NL))
                pe.wait_ge(S("inv_copied"), 5 * c + 2)
                pe.wait_ge(S("inv_sum"), 6 * c + 2)
                level((0, AL4, A4), (1, A4, AL4), (5, AL4, N), (6, A4, NL))
                pe.wait_ge(S("inv_copied"), 5 * c + 3)
                pe.wait_ge(S("inv_sum"), 6 * c + 3)
                level((5, AL8, N), (6, A8, NL))
                pe.wait_ge(S("inv_sum"), 6 * c + 4)
                level((0, AL, N), (1, A, NL))
                pe.wait_ge(S("inv_copied"), 5 * c + 4)
                level((2, NL, A2), (3, N, A4))
                pe.wait_ge(S("inv_sum"), 6 * c + 5)
                level((0, AL, N))
                pe.wait_ge(S("inv_copied"), 5 * c + 5)
                level((1, NL, A2))
                pe.wait_ge(S("inv_sum"), 6 * c + 6)
                pe.wait_ge(S("g_ready"), c + 1)
                for p in range(4):
                    mm = pe.matmul(bank[5][:, p * CH:(p + 1) * CH], N[:, p, :], g_st[:, p, :], start=True, stop=True)
                mm.then_inc(S("s_done"), 1)
                pe.wait_ge(S("s_ready"), c + 1)
                pe.sem_inc(S("wait_held"), 1)
                for b, products in ((6, ((z_st, rho), (v_st, rk_t), (s_neg, rb_t))),
                                    (7, ((kap_st, v_st), (bet_st, s_neg)))):
                    for p in range(4):
                        for a in halves:
                            for n, (left, right) in enumerate(products):
                                mm = pe.matmul(bank[b][a, p * CH:(p + 1) * CH], left[a, p, :], right[a, p, :],
                                               start=(n == 0), stop=(n == len(products) - 1))
                    mm.then_inc(S("step_done"), 1)
            for n in range(2):
                pe.wait_ge(S("y_rw_ready"), n + 1)
                src = (y_rw, rw_tmp)[n]
                for b in range(2):
                    mm = pe.matmul(bank[2 * n + b][:, :], C("blk64"), flat(src)[:, b * 512:(b + 1) * 512], start=True, stop=True)
                mm.then_inc(S("y_rw_summed"), 1)

        def next_rwkv(n, i):
            n, i = (n + 4, i) if n < 3 else ((3, 0, 1, 2)[n - 3], i + 1)
            return (n % 4, "rwkv", i, n // 4) if i < 2 else None

        def rwkv_scalar(act):
            for i in range(2):
                for n in range(7):
                    split_done(act, n % 4, "rwkv", i, n // 4)
                    act.activation(raw[:, 7 * i + n, 1:1 + T], bank[n][:, 0:T], ACT.Copy).then_inc(S("rw_evicted"), 1)
                    if next_rwkv(n, i):
                        make_hi(act, *next_rwkv(n, i))
            act.wait_ge(S("rw_mixed"), 14)
            act.activation(wa_act[0:HD, :], mixed[0:HD, 12, :], ACT.Tanh)
            act.activation(wa_act[HD:P, :], mixed[HD:P, 12, :], ACT.Copy)
            act.activation(g_act, mixed[:, 13, :], ACT.Sigmoid).then_inc(S("lora_act"), 1)
            for kind, (dst, b0) in enumerate(((log_decay, "w0"), (a_gate, "a0"))):
                act.wait_ge(S("lora_done"), kind + 1)
                for p in range(4):
                    ins = act.activation(dst[:, p, :], bank[2 * kind + p // 2][:, (p % 2) * T:(p % 2 + 1) * T], ACT.Sigmoid,
                                         bias=V(b0, p, p + 1))
                ins.then_inc(S("gates_ready"), 1)
            act.wait_ge(S("lora_done"), 3)
            for b in range(2):
                act.activation(flat(g_gate)[:, b * 512:(b + 1) * 512], bank[4 + b][:, :], ACT.Copy)
            act.wait_ge(S("kk_steps"), 1)
            act.activation(rw_tmp, kk, ACT.Square).then_inc(S("kk_squared"), 1)
            act.wait_ge(S("kk_steps"), 2)
            act.activation(p_now, cum, ACT.Exp)
            act.activation(p_prev, p_prev, ACT.Exp)
            act.activation(p_inv, cum, ACT.Exp, scale=-1.0).then_inc(S("p_ready"), 1)
            act.preload_act_table_set(LOG_AND_EXP)
            act.wait_ge(S("kk_steps"), 3)
            act.activation(rw_tmp, rw_tmp, ACT.Ln)
            act.drain()
            act.activation(rw_tmp, rw_tmp, ACT.Exp, scale=-0.5).then_inc(S("kk_rooted"), 1)
            act.wait_ge(S("diag_zeroed"), 1)
            act.drain()
            with act.Fori(0, RC) as c:
                for a in halves:
                    act.activation(diag_v[a, :, a], V_[a, :, bass.ds(c * CH, CH)], ACT.Copy)
                act.wait_ge(S("alpha_ready"), c + 1)
                for a in halves:
                    ins = act.activation(diag_alpha[a, :, a], alpha[a, :, :], ACT.Copy)
                ins.then_inc(S("diag_ready"), 1)
                act.wait_ge(S("rows_done"), c + 1)
                act.activation(flat(v_st), bank[4][:, 0:256], ACT.Copy).then_inc(S("rows_ready"), 1)
                for done, pairs in ((1, ((0, A2), (1, AL2))), (2, ((2, A4), (3, AL4))), (3, ((0, A8), (1, AL8))),
                                    (5, ((0, A2), (1, A4))), (7, ((0, A2),))):
                    act.wait_ge(S("inv_done"), 8 * c + done)
                    for b, dst in pairs:
                        ins = act.activation(flat(dst), bank[b][:, :], ACT.Copy)
                    ins.then_inc(S("inv_copied"), 1)
            for n in range(4):
                make_hi(act, n, "mla", 0)
            act.wait_ge(S("y_centred"), 1)
            act.activation(rw_tmp, y_rw, ACT.Square).then_inc(S("y_rw_ready"), 1)
            act.wait_ge(S("y_rw_summed"), 2)
            for b in range(2):
                ins = rstd(act, flat(rw_tmp)[:, b * 512:(b + 1) * 512], bank[2 + b][:, :], HD, stat[:, 15:16])
            ins.then_inc(S("y_rw_rooted"), 1)

        def rwkv_vector(dve):
            def by_pair(out, x, gain, op1=None, off=None):
                for p in range(4):
                    ins = dve.tensor_scalar(out[:, p, :], x[:, p, :], V(gain, p, p + 1),
                                            V(off, p, p + 1) if off else None, ALU.mult, op1 or ALU.bypass)
                return ins

            dve.memset(raw[:, :, 0:1], 0.0)
            dve.drain()
            for i in range(2):
                for n in range(7):
                    m = 7 * i + n
                    dve.wait_ge(S("rw_evicted"), 7 * i + n + 8)
                    dve.tensor_tensor(mixed[:, m, :], raw[:, m, 0:T], raw[:, m, 1:1 + T], ALU.subtract)
                    dve.drain()
                    dve.scalar_tensor_tensor(mixed[:, m, :], mixed[:, m, :], V("mu", m, m + 1), raw[:, m, 1:1 + T],
                                             ALU.mult, ALU.add).then_inc(S("rw_mixed"), 1)
                    if next_rwkv(n, i):
                        make_lo(dve, *next_rwkv(n, i))
            dve.drain()
            dve.memset(y_rw, 1.0)
            by_pair(kk, K_, "k_k").then_inc(S("kk_steps"), 1)
            dve.drain()
            dve.memset(flat(y_rw).rearrange("p (c s) -> p c s", s=CH)[:, :, 0:1], 0.0)
            dve.wait_ge(S("gates_ready"), 1)
            dve.tensor_scalar(log_decay, log_decay, -math.exp(-0.5), None, ALU.mult)
            dve.drain()
            dve.tensor_tensor_scan(flat(cum), flat(y_rw), flat(log_decay), 0.0, ALU.mult, ALU.add)
            dve.drain()
            dve.tensor_tensor(p_prev, cum, log_decay, ALU.subtract).then_inc(S("kk_steps"), 1)
            dve.wait_ge(S("gates_ready"), 2)
            for p in range(4):
                dve.tensor_scalar(kk_a[:, p, :], a_gate[:, p, :], 1.0, V("k_a", p, p + 1), ALU.subtract, ALU.mult)
            dve.drain()
            dve.scalar_tensor_tensor(flat(K_), flat(kk_a), 1.0, flat(K_), ALU.add, ALU.mult)
            dve.drain()
            dve.tensor_tensor(bonus, R_, K_, ALU.mult)
            dve.drain()
            by_pair(bonus, bonus, "r_k").then_inc(S("rk_ready"), 1)
            dve.wait_ge(S("head_sums"), 1)
            for b in range(2):
                ins = dve.tensor_scalar(flat(rw_tmp)[:, b * 512:(b + 1) * 512], bank[6 + b][:, :], 1e-24, None, ALU.max)
            ins.then_inc(S("kk_steps"), 1)
            dve.wait_ge(S("kk_rooted"), 1)
            dve.tensor_tensor(kk, kk, rw_tmp, ALU.mult)
            dve.drain()
            dve.tensor_tensor(kk_a, kk, a_gate, ALU.mult)
            dve.wait_ge(S("head_sums"), 2)
            for b in range(2):
                dve.tensor_tensor(flat(bonus)[:, b * 512:(b + 1) * 512], bank[6 + b][:, :],
                                  flat(V_)[:, b * 512:(b + 1) * 512], ALU.mult)
            for m in (U, UL):
                dve.memset(m, 0.0)
            dve.memset(z_st, 0.0).then_inc(S("z_ready"), 1)
            dve.wait_ge(S("p_ready"), 1)
            dve.drain()

            def over_pairs(mask, n=4):
                return mask.unsqueeze(1).broadcast_to([mask.shape[0], n, mask.shape[1]])

            def pairs_of(b):
                return bank[b][:, 0:384].rearrange("p (q n t) -> p q n t", q=2, n=3)

            masks = con[:, CONSTS["up_strict"][0]:CONSTS["up_strict"][0] + 3 * CH]
            for a in halves:
                dve.tensor_copy(rights[a, :, 2, :], over_pairs(C("ident")[a, a]))
            dve.wait_ge(S("diag_zeroed"), 1)
            dve.drain()

            with dve.Fori(0, RC) as c:
                now = bass.ds(c * CH, CH)
                dve.tensor_tensor(alpha, p_prev[:, :, now], kk[:, :, now], ALU.mult).then_inc(S("alpha_ready"), 1)
                dve.tensor_tensor(rho, p_now[:, :, now], R_[:, :, now], ALU.mult)
                for left, x in ((diag_beta, kk_a), (diag_kappa, K_)):
                    for a in halves:
                        ins = dve.tensor_tensor(left[a, :, a], p_inv[a, :, now], x[a, :, now], ALU.mult)
                    if left is diag_beta:
                        ins.then_inc(S("chunk_ready"), 1)
                dve.tensor_tensor(beta, p_inv[:, :, now], kk_a[:, :, now], ALU.mult).then_inc(S("chunk_ready"), 1)
                dve.wait_ge(S("gram_done"), 3 * c + 1)
                for a in halves:
                    for b in range(2):
                        dve.tensor_tensor(U[a, 2 * b:2 * b + 2, a], pairs_of(2 + b)[a, :, 0, :],
                                          over_pairs(C("up_strict")[a, :], 2), ALU.mult)
                dve.wait_ge(S("gram_done"), 3 * c + 2)
                for a in halves:
                    dve.tensor_tensor(UL[a, :, a], quarters(bank[5], 8)[a, 0:4, :], over_pairs(C("low_strict")[a, :]), ALU.mult)
                dve.drain()
                dve.tensor_tensor(A, U, over_pairs(C("u16")), ALU.mult)
                dve.tensor_tensor(AL, UL, over_pairs(C("l16")), ALU.mult)
                dve.drain()
                dve.tensor_tensor(N, over_pairs(C("ident")), A, ALU.subtract)
                dve.tensor_tensor(NL, over_pairs(C("ident")), AL, ALU.subtract).then_inc(S("inv_sum"), 1)
                for b in range(2):
                    dve.tensor_tensor(of_beta[:, 2 * b:2 * b + 2, :, :].rearrange("p q n t -> p q (n t)"),
                                      pairs_of(2 + b)[:, :, 1:3, :].rearrange("p q n t -> p q (n t)"),
                                      over_pairs(masks[:, CH:3 * CH], 2), ALU.mult)
                dve.wait_ge(S("gram_done"), 3 * c + 3)
                for b in range(2):
                    ins = dve.tensor_tensor(of_kappa[:, 2 * b:2 * b + 2, :, :].rearrange("p q n t -> p q (n t)"),
                                            pairs_of(6 + b).rearrange("p q n t -> p q (n t)"), over_pairs(masks, 2), ALU.mult)
                ins.then_inc(S("lk_ready"), 1)

                def add(done, op, *pairs):
                    dve.wait_ge(S("inv_done"), 8 * c + done)
                    for m, b in pairs:
                        ins = dve.tensor_tensor(m, m, quarters(bank[b]), op)
                    return ins

                add(2, ALU.add, (N, 5), (NL, 6)).then_inc(S("inv_sum"), 1)
                dve.wait_ge(S("g_done"), c + 1)
                dve.tensor_copy(flat(g_st), bank[4][:, 256:512]).then_inc(S("g_ready"), 1)
                add(3, ALU.add, (N, 5), (NL, 6)).then_inc(S("inv_sum"), 1)
                dve.tensor_tensor(A, U, over_pairs(C("u32")), ALU.mult)
                dve.tensor_tensor(AL, UL, over_pairs(C("l32")), ALU.mult)
                add(4, ALU.add, (N, 5), (NL, 6)).then_inc(S("inv_sum"), 1)
                add(6, ALU.subtract, (N, 2), (NL, 3))
                dve.tensor_tensor(AL, UL, over_pairs(C("l64")), ALU.mult).then_inc(S("inv_sum"), 1)
                add(8, ALU.subtract, (N, 1)).then_inc(S("inv_sum"), 1)
                dve.wait_ge(S("s_done"), c + 1)
                dve.tensor_scalar(flat(s_neg), bank[5][:, 0:256], -1.0, None, ALU.mult).then_inc(S("s_ready"), 1)
                dve.wait_ge(S("step_done"), 2 * c + 1)
                dve.tensor_copy(y_rw[:, :, now], bank[6][:, 0:256].rearrange("p (a b) -> p a b", a=4))
                dve.wait_ge(S("step_done"), 2 * c + 2)
                dve.tensor_tensor(flat(z_st), flat(z_st), bank[7][:, 0:256], ALU.add)
                dve.drain()
                end = p_now[:, :, bass.ds(c * CH + CH - 1, 1)]
                dve.tensor_tensor(z_st, z_st, end.broadcast_to([P, 4, CH]), ALU.mult).then_inc(S("z_ready"), 1)
            dve.drain()
            dve.sem_inc(S("y_rw_ready"), 1)
            for n in range(2):
                make_lo(dve, n, "mla", 0)
            dve.wait_ge(S("y_rw_summed"), 1)
            for b in range(2):
                part = flat(y_rw)[:, b * 512:(b + 1) * 512]
                ins = dve.scalar_tensor_tensor(part, bank[b][:, :], -1.0 / HD, part, ALU.mult, ALU.add)
            ins.then_inc(S("y_centred"), 1)
            for n in range(2, 4):
                make_lo(dve, n, "mla", 0)
            dve.wait_ge(S("y_rw_rooted"), 1)
            dve.tensor_tensor(y_rw, y_rw, rw_tmp, ALU.mult)
            dve.drain()
            by_pair(y_rw, y_rw, "lnw", ALU.add, "lnb")
            dve.drain()
            dve.tensor_tensor(y_rw, y_rw, bonus, ALU.add)
            dve.drain()
            dve.tensor_tensor(y_rw, y_rw, g_gate, ALU.mult).then_inc(S("y_rw_ready"), 1)

        def rwkv_pool(pool):
            pool.wait_ge(S("lora_done"), 3)
            for m in (diag_alpha, diag_beta, diag_kappa):
                pool.memset(m, 0.0)
            pool.memset(diag_v, 0.0).then_inc(S("diag_zeroed"), 1)

        POOL["rwkv"] = rwkv_pool
        SYNC["rwkv"], TENSOR["rwkv"], SCALAR["rwkv"], VECTOR["rwkv"] = rwkv_sync, rwkv_tensor, rwkv_scalar, rwkv_vector

        Q_, K2 = slice(0, QK), slice(NOPE, QK)
        uv_all = area(0, 4 * 2 * P)
        pos_i, pos_f = area(1024, T), area(1280, T)
        turns, cos_t, sin_t = area(1536, T), area(2048, T), area(2304, T)
        lat = area(4096, 6, T)
        lat_sq = area(5632, 5, T)
        lat_root = area(6912, 2, T)
        qk_sq, qk_root, qk_norm = (area(7424 + 1024 * n, 2, 512) for n in range(3))
        qk_cos, qk_sin, qk_rope = (area(10496 + 1024 * n, 2, 512) for n in range(3))
        m_prob, m_prob_t = area(13568, 2, 384), area(14336, 2, 384)
        v_pairs = area(15104, 2, TT, P)
        mo_sq, mo_root = area(15616, T), area(15872, T)
        m_stat = area(16128, 2, 3, 2)
        mix_all = area(22664, 8, T)
        blocks = (slice(0, P), slice(P, 384))

        def mla_sync(sp):
            for n in range(4):
                load(sp, n, io["mla_in"][n, :, :], "mla")
            sp.wait_ge(S("y_rw_ready"), 1)
            sp.dma_start(uv_all.rearrange("p (i n) -> p i n", i=4), io["mla_uv"].rearrange("i p n -> p i n")).then_inc(S("mla_loaded"), 16)
            sp.dma_start(pos_i.bitcast(I32), io["positions"].broadcast_to([P, T])).then_inc(S("mla_loaded"), 16)
            for n in range(4, 6):
                load(sp, n % 4, io["mla_in"][n, :, :], "mla", 0, n // 4)
            for i in range(4):
                load(sp, i % 2, io["mla_u"][i, :, :], "mla_heads", i // 2)


        def mla_tensor(pe):
            for n in range(6):
                if n >= 4:
                    pe.wait_ge(S("lat_out"), n - 3)
                project_split(pe, ROT[n % 4][:, 0:T], n % 4, "mla", 0, n // 4)
            pe.wait_ge(S("lat_out"), 6)
            pe.wait_ge(S("lat_steps"), 2)
            for b, part in enumerate((range(0, 3), range(3, 5))):
                for c in part:
                    mm = pe.matmul(ROT[b][:, 0:T], C("ones"), lat_sq[:, c, :], start=(c == part[0]), stop=(c == part[-1]))
            mm.then_inc(S("lat_summed"), 1)
            pe.wait_ge(S("lat_ready"), 1)
            pe.wait_ge(S("mla_loaded"), 32)

            def group(i):
                return bank[4 * (i % 2):4 * (i % 2) + 4]

            def heads(i):
                G, slot = group(i), i % 2
                arrived(pe, slot, "mla_heads", i // 2)
                if i >= 2:
                    pe.wait_ge(S("mo_ready"), i - 1)
                for a in range(2):
                    for c in range(3):
                        at = (3 * a + c) * QK
                        mm = pe.matmul(G[a][Q_, 0:T], ring[slot][:, at:at + QK], lat[:, c, :], start=(c == 0), stop=(c == 2))
                    pe.matmul(G[a][Q_, T:512], C("ident", 0, QK)[K2, :], lat[K2, 5, :], start=True, stop=False)
                    for c in range(2):
                        at = (6 + 2 * a + c) * QK
                        mm = pe.matmul(G[a][Q_, T:512], ring[slot][:, at:at + QK], lat[:, 3 + c, :], start=False, stop=(c == 1))
                    mm.then_inc(S("mqk_done") if a == 0 else freed[slot], 1)
                for tt in range(TT):
                    for c in range(2):
                        at = i * 2 * P + c * P
                        mm = pe.matmul(G[2][:, tt * P:(tt + 1) * P], lat[:, 3 + c, tt * P:(tt + 1) * P],
                                       uv_all[:, at:at + P], start=(c == 0), stop=(c == 1))
                mm.then_inc(S("mv_done"), 1)

            def squares(i):
                for a in range(2):
                    pe.wait_ge(S("mqk_squared"), 2 * i + a + 1)
                    if a == 1:
                        pe.wait_ge(S("mv_out"), i + 1)
                    pe.matmul(group(i)[3 - a][Q_, :], C("ones", 0, QK)[Q_, :], qk_sq[Q_, a, :], start=True,
                              stop=True).then_inc(S("mqk_summed"), 1)

            def turn_halves(i):
                for a in range(2):
                    pe.wait_ge(S("mqk_normed"), 2 * i + a + 1)
                    pe.matmul(group(i)[3 - a][Q_, :], C("rot")[Q_, :], qk_norm[Q_, a, :], start=True,
                              stop=True).then_inc(S("mqk_turned"), 1)

            def scores(i):
                for a in range(2):
                    pe.wait_ge(S("mqk_ready"), 2 * i + a + 1)
                    q, k = qk_rope[Q_, a, 0:T], qk_rope[Q_, a, T:512]
                    out = group(i)[a]
                    pe.matmul(out[:, 0:P], q[:, 0:P], k[:, 0:P], start=True, stop=True)
                    pe.matmul(out[:, P:384], q[:, P:T], k, start=True, stop=True).then_inc(S("m_scores"), 1)

            def turn_probs(i):
                for a in range(2):
                    pe.wait_ge(S("mp_ready"), 2 * i + a + 1)
                    for n in range(3):
                        mm = pe.transpose(group(i)[3 - a][:, n * P:(n + 1) * P], m_prob[:, a, n * P:(n + 1) * P], C("ident"))
                    mm.then_inc(S("mp_turned"), 1)

            def outputs(i):
                for a in range(2):
                    pe.wait_ge(S("mp_out"), 2 * i + a + 1)
                    out, vs = group(i)[0][a * HD:(a + 1) * HD, :], slice(a * HD, (a + 1) * HD)
                    v = v_pairs[:, i % 2, :, :]
                    pe.matmul(out[:, 0:P], v[:, 0, vs], m_prob_t[:, a, 0:P], start=True, stop=True)
                    pe.matmul(out[:, P:T], v[:, 0, vs], m_prob_t[:, a, P:2 * P], start=True, stop=False)
                    mm = pe.matmul(out[:, P:T], v[:, 1, vs], m_prob_t[:, a, 2 * P:384], start=False, stop=True)
                mm.then_inc(S("mo_done"), 1)

            def output_squares(i):
                pe.wait_ge(S("mo_squared"), i + 1)
                pe.matmul(group(i)[1][:, 0:T], C("blk64"), mo_sq, start=True, stop=True).then_inc(S("mo_summed"), 1)

            heads(0)
            squares(0)
            turn_halves(0)
            scores(0)
            for i in range(4):
                more = i < 3
                if more:
                    heads(i + 1)
                turn_probs(i)
                if more:
                    squares(i + 1)
                outputs(i)
                if more:
                    turn_halves(i + 1)
                output_squares(i)
                if more:
                    scores(i + 1)

        def mla_scalar(act):
            for n in range(6):
                split_done(act, n % 4, "mla", 0, n // 4)
                act.activation(lat[:, n, :], ROT[n % 4][:, 0:T], ACT.Copy).then_inc(S("lat_out"), 1)
                if n < 2:
                    make_hi(act, n, "mla", 0, 1)
            act.wait_ge(S("angles_ready"), 1)
            act.activation(sin_t[Q_, :], sin_t[Q_, :], ACT.Sin)
            act.activation(cos_t[Q_, :], cos_t[Q_, :], ACT.Sin).then_inc(S("lat_steps"), 1)
            act.wait_ge(S("lat_out"), 6)
            act.activation(lat_sq, lat[:, 0:5, :], ACT.Square).then_inc(S("lat_steps"), 1)
            act.preload_act_table_set(LOG_AND_EXP)
            act.wait_ge(S("lat_summed"), 1)
            rstd(act, lat_root[:, 0, :], ROT[0][:, 0:T], MLA_Q, stat[:, 14:15])
            rstd(act, lat_root[:, 1, :], ROT[1][:, 0:T], MLA_KV, stat[:, 14:15]).then_inc(S("lat_steps"), 1)

            def group(i):
                return bank[4 * (i % 2):4 * (i % 2) + 4]

            def square(i):
                for a in range(2):
                    if a == 0:
                        act.wait_ge(S("mqk_done"), i + 1)
                    else:
                        multiplied(act, i % 2, "mla_heads", i // 2)
                    act.activation(qk_sq[Q_, a, :], group(i)[a][Q_, :], ACT.Square).then_inc(S("mqk_squared"), 1)
                act.wait_ge(S("mv_done"), i + 1)
                act.activation(v_pairs[:, i % 2, :, :], group(i)[2][:, 0:T].rearrange("p (a b) -> p a b", a=TT),
                               ACT.Copy).then_inc(S("mv_out"), 1)

            def root(i):
                for a in range(2):
                    act.wait_ge(S("mqk_summed"), 2 * i + a + 1)
                    rstd(act, qk_root[Q_, a, :], group(i)[3 - a][Q_, :], QK, stat[Q_, 14:15]).then_inc(S("mqk_rooted"), 1)

            square(0)
            root(0)
            for i in range(4):
                for a in range(2):
                    act.wait_ge(S("m_max"), 2 * i + a + 1)
                    for n, cols in enumerate(blocks):
                        ins = act.activation(m_prob[:, a, cols], m_prob[:, a, cols], ACT.Exp,
                                             bias=m_stat[:, a, 1, n:n + 1], accum_out=m_stat[:, a, 2, n:n + 1])
                    ins.then_inc(S("mp_exp"), 1)
                if i < 3:
                    square(i + 1)
                for a in range(2):
                    act.wait_ge(S("mp_turned"), 2 * i + a + 1)
                    act.activation(m_prob_t[:, a, :], group(i)[3 - a][:, 0:384], ACT.Copy).then_inc(S("mp_out"), 1)
                if i < 3:
                    root(i + 1)
                act.wait_ge(S("mo_done"), i + 1)
                act.activation(mo_sq, group(i)[0][:, 0:T], ACT.Square).then_inc(S("mo_squared"), 1)
                act.wait_ge(S("mo_summed"), i + 1)
                rstd(act, mo_root, group(i)[1][:, 0:T], HD, stat[:, 14:15]).then_inc(S("mo_rooted"), 1)

        def mla_vector(dve):
            dve.wait_ge(S("mla_loaded"), 32)
            dve.tensor_copy(pos_f, pos_i.bitcast(I32))
            dve.drain()
            dve.tensor_scalar(pos_f, pos_f, C("inv_freq"), None, ALU.mult)
            dve.drain()
            dve.tensor_scalar(turns, pos_f, 1.0 / (2 * math.pi), 1.5 * 2.0 ** 23, ALU.mult, ALU.add)
            dve.drain()
            dve.tensor_scalar(turns, turns, -1.5 * 2.0 ** 23, None, ALU.add)
            c1 = 6.28125
            c2 = float(np.float32(np.round((2 * math.pi - c1) * 2 ** 21) / 2 ** 21))
            for c in (c1, c2, 2 * math.pi - c1 - c2):
                dve.drain()
                dve.scalar_tensor_tensor(pos_f, turns, -c, pos_f, ALU.mult, ALU.add)
            dve.drain()
            dve.tensor_scalar(sin_t, pos_f, 3.1415925, -3.1415925, ALU.min, ALU.max)
            dve.tensor_scalar(cos_t, pos_f, -1.0, None, ALU.mult)
            dve.drain()
            dve.tensor_tensor(cos_t, cos_t, pos_f, ALU.min)
            dve.drain()
            dve.tensor_scalar(cos_t, cos_t, C("half"), None, ALU.add).then_inc(S("angles_ready"), 1)
            for n in range(2):
                make_lo(dve, n, "mla", 0, 1)
            dve.wait_ge(S("lat_steps"), 3)
            for c in range(5):
                gain = V("g_cq", c, c + 1) if c < 3 else V("g_ckv", c - 3, c - 2)
                ins = dve.scalar_tensor_tensor(lat[:, c, :], lat[:, c, :], gain, lat_root[:, c // 3, :], ALU.mult, ALU.mult)
            ins.then_inc(S("lat_ready"), 1)
            dve.wait_ge(S("lat_steps"), 1)

            def twice(t):
                return t[Q_, :].unsqueeze(1).broadcast_to([QK, 2, T])

            def two(t):
                return t.rearrange("p (a b) -> p a b", a=2)

            def group(i):
                return bank[4 * (i % 2):4 * (i % 2) + 4]

            def queries_keys(i):
                for a in range(2):
                    dve.wait_ge(S("mqk_rooted"), 2 * i + a + 1)
                    for n, gain in enumerate(("g_qnorm", "g_knorm")):
                        cols = slice(n * T, (n + 1) * T)
                        ins = dve.scalar_tensor_tensor(qk_norm[Q_, a, cols], group(i)[a][Q_, cols], V(gain)[Q_, :],
                                                       qk_root[Q_, a, cols], ALU.mult, ALU.mult)
                    ins.then_inc(S("mqk_normed"), 1)
                dve.drain()
                for a in range(2):
                    dve.tensor_tensor(two(qk_cos[Q_, a, :]), two(qk_norm[Q_, a, :]), twice(cos_t), ALU.mult)
                    dve.wait_ge(S("mqk_turned"), 2 * i + a + 1)
                    dve.tensor_tensor(two(qk_sin[Q_, a, :]), two(group(i)[3 - a][Q_, :]), twice(sin_t), ALU.mult)
                    dve.drain()
                    dve.tensor_tensor(qk_rope[Q_, a, :], qk_cos[Q_, a, :], qk_sin[Q_, a, :], ALU.add).then_inc(S("mqk_ready"), 1)

            queries_keys(0)
            for i in range(4):
                for a in range(2):
                    dve.wait_ge(S("m_scores"), 2 * i + a + 1)
                    dve.scalar_tensor_tensor(m_prob[:, a, :], group(i)[a][:, 0:384], QK ** -0.5, C("mla_mask"), ALU.mult, ALU.add)
                    dve.drain()
                    for n, cols in enumerate(blocks):
                        dve.reduce_max(m_stat[:, a, 0, n:n + 1], m_prob[:, a, cols], AX.X)
                    dve.drain()
                    dve.tensor_scalar(m_stat[:, a, 1, :], m_stat[:, a, 0, :], -1.0, None, ALU.mult).then_inc(S("m_max"), 1)
                for a in range(2):
                    dve.wait_ge(S("mp_exp"), 2 * i + a + 1)
                    dve.reciprocal(m_stat[:, a, 2, :], m_stat[:, a, 2, :])
                    dve.drain()
                    for n, cols in enumerate(blocks):
                        ins = dve.tensor_scalar(m_prob[:, a, cols], m_prob[:, a, cols], m_stat[:, a, 2, n:n + 1], None, ALU.mult)
                    ins.then_inc(S("mp_ready"), 1)
                if i < 3:
                    queries_keys(i + 1)
                dve.wait_ge(S("mo_rooted"), i + 1)
                dve.scalar_tensor_tensor(mix_all[:, i, :], group(i)[0][:, 0:T], V("g_out", i, i + 1), mo_root, ALU.mult,
                                         ALU.mult).then_inc(S("mo_ready"), 1)

        SYNC["mla"], TENSOR["mla"], SCALAR["mla"], VECTOR["mla"] = mla_sync, mla_tensor, mla_scalar, mla_vector

        def mix_sync(sp):
            out_sync(sp, "mix_out", io["w_o2"])

        def mix_tensor(pe):
            pe.wait_ge(S("mo_ready"), 4)
            out_tensor(pe, "mix_out", upd["mix"])

        def mix_scalar(act):
            act.wait_ge(S("mo_ready"), 4)
            out_scalar(act, "mix_out", mix_all)

        def mix_vector(dve):
            out_vector(dve, "mix_out", mix_all)

        SYNC["mix"], TENSOR["mix"], SCALAR["mix"], VECTOR["mix"] = mix_sync, mix_tensor, mix_scalar, mix_vector

        TG = 8
        POOL_TG = 4
        peer_area = KH * T
        choice_t = area(peer_area, 3, T)
        one_a_flat = area(peer_area + 768, 2, TG * KH)
        one_a = one_a_flat.rearrange("p g (t e) -> p g t e", t=TG)
        one_b = area(peer_area + 1792, 2, TG * NKEYS).rearrange("p g (t e) -> p g t e", t=TG)
        gelu_buf = area(peer_area + 3840, 2, T)
        gated_buf = area(peer_area + 4352, 2, T)
        pre_gelu = area(peer_area + 4864, PRE[0], T)
        blocks_b = [RING_PLAN[f"peer_b{k}"][0] for k in range(2)]

        def block_no(k, ring, i, n):
            return 2 * i + n + (PRE[k] if ring[5] == "b" else 0)
        keys_all = area(4096, PH * 2 * NKEYS)
        pq_t = area(6144, 2, T)
        score = area(6656, 4, NKEYS)
        score2 = area(7168, 4, NKEYS)
        top, top_i, top_f = (area(7680 + 64 * n, 4, TOPK) for n in range(3))
        cand, cand2 = (area(8192 + 512 * n, TT, TOPK * TOPK) for n in range(2))
        best, best_i, best_a, best_b, best_af, best_bf, gate = (area(9216 + 32 * n, TT, TOPK) for n in range(7))
        gate_sum = area(9472, 2, TT)
        pick = area(9728, TT, TOPK, TOPK)
        choice = area(10240, 3, TT, P)
        gates_of = area(0, KH, T)

        def peer_sync(sp):
            def u(n, k, i):
                src = io["expert_u"][bass.ds(k * KH + PRE[k] + 2 * i + n, 1), :, :]
                load(sp, 2 * n, src, f"peer_b{k}", i)

            def v(n, k, ring, i):
                src = io["expert_v"][bass.ds(k * KH + block_no(k, ring, i, n), 1), :, :]
                load(sp, 2 * n + 1, src, ring, i)

            def route(i, more=True):
                if more:
                    queries(i + 1)
                for n in range(3):
                    load(sp, 2 + n % 2, io["expert_u"][bass.ds(3 * i + n, 1), :, :], "route", i, n // 2)

            def queries(i):
                for n in range(2):
                    load(sp, n, io["w_pq"][bass.ds(2 * i + n, 1), :, :], "route", i)

            queries(0)
            sp.wait_ge(S("h_updated"), 4 * upd["peer"] + 1)
            sp.dma_start(keys_all.rearrange("p (h n) -> p h n", h=PH), io["keys"].rearrange("h p n -> p h n")).then_inc(S("keys_loaded"), 16)
            with sp.Fori(0, PH - 1) as i:
                route(i)
            route(PH - 1, more=False)
            v(0, 0, "peer_v0", 0)
            for k in range(2):
                if k == 1:
                    with sp.Fori(0, PRE[1] // 2) as i:
                        for n in range(2):
                            load(sp, 2 * n, io["expert_u"][bass.ds(KH + 2 * i + n, 1), :, :], "peer_u1", i)
                u(0, k, 0)
                u(1, k, 0)
                for ring in (f"peer_v{k}", f"peer_b{k}"):
                    with sp.Fori(0, RING_PLAN[ring][0] - (ring[5] == "b")) as i:
                        if ring[5] == "b":
                            u(0, k, i + 1)
                        v(1, k, ring, i)
                        if ring[5] == "b":
                            u(1, k, i + 1)
                        v(0, k, ring, i + 1)
                v(1, k, f"peer_b{k}", blocks_b[k] - 1)
                if k == 0:
                    v(0, 1, "peer_v1", 0)

        def peer_tensor(pe):
            def queries(i):
                pe.wait_ge(S("pq_out"), 2 * i + 2)
                for n in range(2):
                    arrived(pe, n, "route", i)
                    project(pe, ROT[n][:, 0:T], n).then_inc(freed[n], 1)

            def head(i, more=True):
                pe.wait_ge(S("pq_out"), 2 * i + 4)
                pe.wait_ge(S("score_out"), i + 1)
                for tt in range(TT):
                    for n in range(2):
                        at = (2 * tt + n) * P
                        mm = pe.matmul(ROT[2][:, at:at + P], pq_t[:, n, tt * P:(tt + 1) * P],
                                       keys_all[:, bass.ds((2 * i + n) * NKEYS, NKEYS)], start=True, stop=True)
                mm.then_inc(S("score_done"), 1)
                if more:
                    queries(i + 1)
                for n in range(3):
                    arrived(pe, 2 + n % 2, "route", i, n // 2)
                    pe.wait_ge(S("pre_gelu"), 3 * i + n + 1)
                    project(pe, bank[n][:, 0:T], 2 + n % 2).then_inc(freed[2 + n % 2], 1)

            pe.wait_ge(S("u_ready"), 4 * norm_no["peer"] + 4)
            pe.wait_ge(S("keys_loaded"), 16)
            queries(0)
            with pe.Fori(0, PH - 1) as i:
                head(i)
            head(PH - 1, more=False)
            pe.wait_ge(S("choice_ready"), 1)
            for k in range(3):
                for tt in range(TT):
                    mm = pe.transpose(ROT[k][:, tt * P:(tt + 1) * P], choice[:, k, tt, :], C("ident"))
            mm.then_inc(S("choice_turned"), 1)
            pe.wait_ge(S("choice_ready"), 2)
            u_split_ready(pe, "peer")

            def up(n, k, i):
                pe.wait_ge(S("gelu_out"), 2 * (i + k * blocks_b[0]) + n + 1)
                project_split(pe, ROT[n][:, 0:T], 2 * n, f"peer_b{k}", i)

            def down(n, k, ring, i, last=False):
                pe.wait_ge(S("gated"), k * KH + block_no(k, ring, i, n) + 3)
                close_split(pe, n, 2 * n + 1, ring, i, last)

            for k in range(2):
                with pe.Fori(0, 4) as i:
                    for n in range(2):
                        if k == 1:
                            arrived(pe, 2 * n, "peer_u1", i)
                            pe.wait_ge(S("pre_gelu"), 2 * i + n + PRE[0] + 2)
                            project(pe, ROT[n][:, 0:T], 2 * n).then_inc(freed[2 * n], 1)
                        for q in range(4):
                            g, token = q % 2, 8 * TG * i + (k * T + (4 * n + q) * TG)
                            pe.wait_ge(S("one_hot"), token + 3 * TG)
                            pe.wait_ge(S("pool_gated"), token + TG)
                            pe.wait_ge(S("gates_out"), token + TG)
                            for t in range(TG):
                                cols = slice(t * KH, min(t + 2, TG) * KH)
                                mm = pe.matmul(ROT[2 + g][:, cols], one_b[:, g, t, :], one_a_flat[:, g, cols],
                                               start=True, stop=True)
                            mm.then_inc(S("gates_done"), TG)
                if k == 0:
                    pe.wait_ge(S("pre_gelu"), PRE[0] + 3)
                    clear_acc(pe, upd["peer"])
                else:
                    pe.wait_ge(S("pre_gelu"), PRE[0] + PRE[1] + 3)
                v_ring, b_ring, end = f"peer_v{k}", f"peer_b{k}", blocks_b[k] - 1
                with pe.Fori(0, PRE[k] // 2) as i:
                    down(0, k, v_ring, i)
                    down(1, k, v_ring, i)
                up(0, k, 0)
                with pe.Fori(0, end) as i:
                    up(1, k, i)
                    down(0, k, b_ring, i)
                    up(0, k, i + 1)
                    down(1, k, b_ring, i)
                up(1, k, end)
                down(0, k, b_ring, end)
                down(1, k, b_ring, end, last=(k == 1))

        def peer_scalar(act):
            def queries(i):
                for n in range(2):
                    multiplied(act, n, "route", i)
                    act.activation(pq_t[:, n, :], ROT[n][:, 0:T], ACT.Copy).then_inc(S("pq_out"), 1)

            def head(i, more=True):
                def pre(n):
                    multiplied(act, 2 + n % 2, "route", i, n // 2)
                    act.activation(pre_gelu[:, bass.ds(3 * i + n, 1), :], bank[n][:, 0:T].unsqueeze(1),
                                   ACT.Gelu).then_inc(S("pre_gelu"), 1)

                if more:
                    queries(i + 1)
                act.wait_ge(S("best_ready"), i + 1)
                act.activation(gate, gate, ACT.Exp).then_inc(S("gate_exp"), 1)
                for n in range(3):
                    pre(n)

            queries(0)
            with act.Fori(0, PH - 1) as i:
                head(i)
            head(PH - 1, more=False)

            def step(n, k, i, ahead=True, more=True):
                b_ring = f"peer_b{k}"
                split_done(act, 2 * n, b_ring, i)
                act.wait_ge(S("gated"), k * KH + block_no(k, b_ring, i, n) + 1)
                act.activation(gelu_buf[:, n, :], ROT[n][:, 0:T], ACT.Gelu).then_inc(S("gelu_out"), 1)
                if ahead:
                    make_hi(act, 2 * n, b_ring, i + 1)
                if more:
                    make_hi(act, 3 - 2 * n, b_ring, i + n)

            make_hi(act, 1, "peer_v0", 0)
            for k in range(2):
                v_ring, b_ring, end = f"peer_v{k}", f"peer_b{k}", blocks_b[k] - 1
                if k == 0:
                    make_hi(act, 0, b_ring, 0)
                    make_hi(act, 2, b_ring, 0)
                act.preload_act_table(ACT.Gelu)
                with act.Fori(0, 4) as i:
                    for n in range(2):
                        for q in range(4):
                            g, token = q % 2, 8 * TG * i + (4 * n + q) * TG
                            act.wait_ge(S("gates_done"), token + (k * T + 3 * TG))
                            out = gates_of[:, :, bass.ds(token, TG)].rearrange("p b t -> p t b")
                            act.activation(out, ROT[2 + g][:, :].rearrange("p (t b) -> p t b", t=TG),
                                           ACT.Copy).then_inc(S("gates_out"), TG)
                        if k == 1:
                            multiplied(act, 2 * n, "peer_u1", i)
                            act.activation(pre_gelu[:, bass.ds(2 * i + n, 1), :], ROT[n][:, 0:T].unsqueeze(1),
                                           ACT.Gelu).then_inc(S("pre_gelu"), 1)
                if k == 1:
                    make_hi(act, 0, b_ring, 0)
                    make_hi(act, 2, b_ring, 0)
                with act.Fori(0, PRE[k] // 2) as i:
                    make_hi(act, 3, v_ring, i)
                    make_hi(act, 1, v_ring, i + 1)
                with act.Fori(0, end) as i:
                    step(0, k, i)
                    step(1, k, i)
                step(0, k, end, ahead=False)
                step(1, k, end, ahead=False, more=(k == 0))

        def peer_pool(pool):
            for k in range(2):
                with pool.Fori(0, T - 2 * TG + 1, 2 * TG) as token:
                    for g in range(2):
                        pool.wait_ge(S("first_keys"), token + (k * T + TG * (g + 1)))
                        gated = one_a[:, g, TG - POOL_TG:TG, :]
                        share = choice_t[:, 2, bass.ds(token + (TG * (g + 1) - POOL_TG), POOL_TG)]
                        pool.tensor_tensor(gated, gated, spread(share, KH), ALU.mult).then_inc(S("pool_gated"), TG)

        def peer_vector(dve):
            def as_int(t):
                return t.bitcast(U32)

            def top16(values, indices, src, less, rows):
                for r in rows:
                    dve.max(values[:, r, 0:8], src[:, r, :])
                dve.drain()
                for r in rows:
                    dve.max_index(as_int(indices)[:, r, 0:8], values[:, r, 0:8], src[:, r, :])
                    dve.match_replace(less[:, r, :], values[:, r, 0:8], src[:, r, :], -3e38)
                dve.drain()
                for r in rows:
                    dve.max(values[:, r, 8:16], less[:, r, :])
                dve.drain()
                for r in rows:
                    dve.max_index(as_int(indices)[:, r, 8:16], values[:, r, 8:16], less[:, r, :])
                dve.drain()

            with dve.Fori(0, PH) as i:
                dve.wait_ge(S("score_done"), i + 1)
                dve.tensor_copy(flat(score), ROT[2][:, :]).then_inc(S("score_out"), 1)
                dve.drain()
                top16(top, top_i, score, score2, range(4))
                dve.tensor_copy(flat(top_f), as_int(flat(top_i)))
                for tt in range(TT):
                    dve.tensor_tensor(cand[:, tt, :].rearrange("p (a b) -> p a b", a=TOPK), spread(top[:, 2 * tt, :], TOPK),
                                      top[:, 2 * tt + 1, :].unsqueeze(1).broadcast_to([P, TOPK, TOPK]), ALU.add)
                dve.drain()
                top16(best, best_i, cand, cand2, range(TT))
                dve.tensor_tensor(gate, best, best[:, :, 0:1].broadcast_to([P, TT, TOPK]), ALU.subtract).then_inc(S("best_ready"), 1)
                dve.tensor_scalar(as_int(flat(best_a)), as_int(flat(best_i)), 4, None, ALU.logical_shift_right)
                dve.tensor_scalar(as_int(flat(best_b)), as_int(flat(best_i)), 15, None, ALU.bitwise_and)
                dve.drain()
                dve.tensor_copy(flat(best_af), as_int(flat(best_a)))
                dve.tensor_copy(flat(best_bf), as_int(flat(best_b)))
                dve.drain()
                for n, at in enumerate((best_af, best_bf)):
                    for tt in range(TT):
                        dve.tensor_tensor(pick[:, tt, :, :], spread(at[:, tt, :], TOPK),
                                          C("iota", 0, TOPK).unsqueeze(1).broadcast_to([P, TOPK, TOPK]), ALU.is_equal)
                    dve.drain()
                    for tt in range(TT):
                        dve.tensor_tensor(pick[:, tt, :, :], pick[:, tt, :, :],
                                          top_f[:, 2 * tt + n, :].unsqueeze(1).broadcast_to([P, TOPK, TOPK]), ALU.mult)
                    dve.drain()
                    dve.reduce_sum(choice[:, n, :, bass.ds(TOPK * i, TOPK)], pick, AX.X)
                    dve.drain()
                dve.wait_ge(S("gate_exp"), i + 1)
                dve.reduce_sum(gate_sum[:, 0, :], gate, AX.X)
                dve.drain()
                dve.reciprocal(gate_sum[:, 1, :], gate_sum[:, 0, :])
                dve.drain()
                dve.tensor_tensor(choice[:, 2, :, bass.ds(TOPK * i, TOPK)], gate, spread(gate_sum[:, 1, :], TOPK), ALU.mult)
                dve.drain()
            dve.sem_inc(S("choice_ready"), 1)
            dve.wait_ge(S("choice_turned"), 1)
            for k in range(3):
                ins = dve.tensor_copy(choice_t[:, k, :], ROT[k][:, 0:T])
            ins.then_inc(S("choice_ready"), 1)
            dve.drain()

            def gate_block(n, k, ring, i, src):
                dve.wait_ge(split_read[2 * n + 1], use_split(ring, 2 * n + 1, i) + 1)
                gates = gates_of[:, bass.ds(block_no(k, ring, i, n), 1), :]
                dve.tensor_tensor(x_hi[:, n:n + 1, :], src, gates, ALU.mult)
                dve.tensor_tensor(gated_buf[:, n:n + 1, :], src, gates, ALU.mult)
                dve.drain()
                dve.tensor_tensor(x_lo[:, n, :], gated_buf[:, n, :], x_hi[:, n, :].bitcast(F32),
                                  ALU.subtract).then_inc(S("gated"), 1)

            def step(n, k, i, ahead=True, more=True):
                b_ring = f"peer_b{k}"
                dve.wait_ge(S("gelu_out"), 2 * (i + k * blocks_b[0]) + n + 3)
                gate_block(n, k, b_ring, i, gelu_buf[:, n:n + 1, :])
                if ahead:
                    make_lo(dve, 2 * n, b_ring, i + 1)
                if more:
                    make_lo(dve, 3 - 2 * n, b_ring, i + n)

            make_lo(dve, 1, "peer_v0", 0)
            for k in range(2):
                v_ring, b_ring, end = f"peer_v{k}", f"peer_b{k}", blocks_b[k] - 1
                if k == 0:
                    make_lo(dve, 0, b_ring, 0)
                    make_lo(dve, 2, b_ring, 0)
                with dve.Fori(0, T - 2 * TG + 1, 2 * TG) as token:
                    for g in range(2):
                        now = bass.ds(token + TG * g, TG)
                        dve.wait_ge(S("gates_done"), token + (k * T + TG * (g + 1)))
                        first_key, second_key, share = (choice_t[:, n, now] for n in range(3))
                        first_keys = C("iota", k * KH, (k + 1) * KH).unsqueeze(1).broadcast_to([P, TG, KH])
                        dve.tensor_tensor(one_a[:, g, :, :], first_keys, spread(first_key, KH),
                                          ALU.is_equal).then_inc(S("first_keys"), TG)
                        dve.tensor_tensor(one_b[:, g, :, :], C("iota").unsqueeze(1).broadcast_to([P, TG, NKEYS]),
                                          spread(second_key, NKEYS), ALU.is_equal)
                        dve.drain()
                        gated = one_a[:, g, 0:TG - POOL_TG, :]
                        dve.tensor_tensor(gated, gated, spread(share[:, 0:TG - POOL_TG], KH),
                                          ALU.mult).then_inc(S("one_hot"), TG)
                dve.wait_ge(S("gates_out"), (k + 1) * T + 2 * TG)
                dve.wait_ge(S("pre_gelu"), (PRE[0], PRE[0] + PRE[1])[k] + 3)
                if k == 1:
                    make_lo(dve, 0, b_ring, 0)
                    make_lo(dve, 2, b_ring, 0)

                def gate_ahead(n, i):
                    gate_block(n, k, v_ring, i, pre_gelu[:, bass.ds(2 * i + n, 1), :])

                gate_ahead(0, 0)
                with dve.Fori(0, PRE[k] // 2 - 1) as i:
                    gate_ahead(1, i)
                    make_lo(dve, 3, v_ring, i)
                    gate_ahead(0, i + 1)
                    make_lo(dve, 1, v_ring, i + 1)
                gate_ahead(1, PRE[k] // 2 - 1)
                make_lo(dve, 3, v_ring, PRE[k] // 2 - 1)
                make_lo(dve, 1, v_ring, PRE[k] // 2)
                with dve.Fori(0, end) as i:
                    step(0, k, i)
                    step(1, k, i)
                step(0, k, end, ahead=False)
                step(1, k, end, ahead=False, more=(k == 0))
            split_done(dve, 3, "peer_b1", blocks_b[1] - 1)
            update_h(dve, 1.0)

        POOL["peer"] = peer_pool
        SYNC["peer"], TENSOR["peer"], SCALAR["peer"], VECTOR["peer"] = peer_sync, peer_tensor, peer_scalar, peer_vector
        block = ctx.enter_context(nc.Block())

        @block.sync
        def _(sp):
            sp.dma_start(con[:, :], io["consts"]).then_inc(S("in_loaded"), 16)
            sp.dma_start(vec[:, :], io["vecs"]).then_inc(S("in_loaded"), 16)
            sp.dma_start(h[:, :, :], io["x"].rearrange("(a p) d -> p a d", p=P)).then_inc(S("h_loaded"), 16)
            for s in stages:
                if s.startswith("ffn"):
                    ffn_sync(sp, int(s[3]))
                elif s in SYNC:
                    SYNC[s](sp)
            sp.wait_ge(S("h_updated"), 4 * len(sums) + 1)
            sp.dma_start(io["out"].rearrange("(a p) d -> p a d", p=P), h[:, :, :]).then_inc(S("out_stored"), 16)
            sp.wait_ge(S("out_stored"), 16)

        @block.gpsimd
        def _(pool):
            pool.memset(zeros[:, :], 0.0).then_inc(S("pool_setup"), 1)
            pool.wait_ge(S("pool_setup"), 1)
            for sem, n in [(f, 1) for f in freed + split_read] + [(S("hid_ready"), 2), (S("h_updated"), 1), (S("ssm_evicted"), 4), (S("y_normed"), 1),
                                                   (S("scored"), 4), (S("p_turned_out"), 4), (S("o_ready"), 2), (S("rw_evicted"), 7),
                                                   (S("pq_out"), 2), (S("score_out"), 1),
                                                   (S("gates_out"), 16), (S("gates_done"), 16), (S("one_hot"), 16),
                                                   (S("gelu_out"), 2), (S("pre_gelu"), 3), (S("gated"), 2)]:
                pool.sem_inc(sem, n)
            for s in stages:
                if s in POOL:
                    POOL[s](pool)

        @block.scalar
        def _(act):
            act.wait_ge(S("stat_ready"), 1)
            for s in stages:
                if s in norm_no:
                    lead_scalar(act, s)
                    norm_scalar(act, norm_no[s], upd[s], s in SPLIT_STAGES)
                if s.startswith("ffn"):
                    ffn_scalar(act, int(s[3]))
                elif s in SCALAR:
                    SCALAR[s](act)

        @block.vector
        def _(dve):
            dve.memset(stat[:, 14:15], EPS)
            dve.memset(stat[:, 15:16], LN_EPS).then_inc(S("stat_ready"), 1)
            dve.wait_ge(S("in_loaded"), 32)
            lead_vector(dve, None)
            for s in stages:
                if s in norm_no:
                    norm_vector(dve, norm_no[s], GAIN[s], s in SPLIT_STAGES)
                if s.startswith("ffn"):
                    ffn_vector(dve, int(s[3]))
                elif s in VECTOR:
                    VECTOR[s](dve)

        @block.tensor
        def _(pe):
            pe.wait_ge(S("in_loaded"), 32)
            for s in stages:
                if s in norm_no:
                    norm_tensor(pe, norm_no[s], s in SPLIT_STAGES)
                if s.startswith("ffn"):
                    ffn_tensor(pe, int(s[3]), upd[s])
                elif s in TENSOR:
                    TENSOR[s](pe)


def pack(x):
    def cols(v):
        v = np.asarray(v).reshape(-1)
        return v.reshape(-1, P).T

    def pad(v):
        v = np.asarray(v).reshape(-1)
        return np.concatenate([v, np.zeros(P - len(v), v.dtype)]).reshape(P, 1)

    inner = GROUPS * GI
    order = []
    for g in range(GROUPS):
        order += [inner + g * P, inner + GROUPS * P + g * P] + [g * GI + k * P for k in range(4)]
    conv_w, conv_b = x["ssm_conv_w"][0], x["ssm_conv_b"][0]
    ffn_norm = x["ffn_norm"].reshape(4, D)
    v = {
        "g_ffn0": cols(ffn_norm[0]), "g_ffn1": cols(ffn_norm[1]), "g_ffn2": cols(ffn_norm[2]),
        "g_ffn3": cols(ffn_norm[3]), "g_ssm": cols(x["ssm_norm"]), "g_kv": cols(x["kv_norm"]),
        "g_attn": cols(x["attn_norm"]), "g_mix": cols(x["g_mix_2"]), "g_peer": cols(x["g_ffn_2"]),
        "conv_w": np.concatenate([conv_w[:, o:o + P].T for o in order], 1),
        "conv_b": np.stack([conv_b[o:o + P] for o in order], 1),
        "d_skip": cols(np.repeat(x["ssm_d"][0], HD)), "g_gate": cols(x["ssm_gate_norm"]),
        "dt_bias": pad(x["ssm_dt_bias"]), "a_log": pad(x["ssm_a_log"]),
        "k_norm": np.tile(x["k_norm"], 2)[:, None], "q_norm": np.tile(x["q_norm"][0], 2)[:, None],
        "sinks": np.tile(x["sinks"], (P, 1)),
        "g_cq": cols(x["g_cq_2"]), "g_ckv": cols(x["g_ckv_2"]),
        "g_qnorm": pad(x["g_qnorm_2"]), "g_knorm": pad(x["g_knorm_2"]), "g_out": cols(x["g_attn_out_2"]),
        "mu": cols(x["rwkv_mu_2"]), "w0": cols(x["w0_2"]), "a0": cols(x["a0_2"]), "k_k": cols(x["k_k_2"]),
        "k_a": cols(x["k_a_2"]), "r_k": cols(x["r_k_2"]), "lnw": cols(x["ln_x_w_2"]), "lnb": cols(x["ln_x_b_2"]),
    }
    for name, (_, n) in VECS.items():
        assert v[name].shape == (P, n), (name, v[name].shape)
    w_in = x["ssm_w_in"][0]
    xbc = tiles(w_in[:, inner:inner + inner + 2 * GROUPS * P])
    z = tiles(w_in[:, 0:inner])
    group_tiles = np.stack([
        np.concatenate([xbc[[16 + g, 20 + g] + [4 * g + k for k in range(4)]], z[4 * g:4 * g + 4]])
        for g in range(GROUPS)])
    w_kv = x["w_kv"]
    kv = np.concatenate([w_kv[:, 0:64], w_kv[:, 0:64], w_kv[:, 64:128], w_kv[:, 64:128], w_kv[:, 128:256]], 1)
    w_in2 = x["w_in_2"][0]
    rope_cols = np.concatenate([w_in2[:, 0:MLA_Q + MLA_KV], np.zeros((D, NOPE), np.float32),
                                w_in2[:, MLA_Q + MLA_KV:MLA_Q + MLA_KV + ROPE], np.zeros((D, ROPE), np.float32)], 1)
    uq = x["w_uq_2"][0].reshape(3, P, PH, QK).transpose(2, 1, 0, 3).reshape(PH, P, 3 * QK)
    uk = x["w_uk_2"][0].reshape(2, P, PH, NOPE).transpose(2, 1, 0, 3)
    uk = np.concatenate([uk, np.zeros((PH, P, 2, ROPE), uk.dtype)], 3).reshape(PH, P, 2 * QK)
    uv = x["w_uv_2"][0].reshape(2, P, 4, P).transpose(2, 1, 0, 3).reshape(4, P, 2 * P)
    return {
        "x": x["x"][0], "positions": x["positions_2"].reshape(1, T), "consts": constants(),
        "vecs": np.concatenate([v[name] for name in VECS], 1),
        "w1": np.stack([tiles(w) for w in x["ffn_w1"].reshape(4, D, FF)]),
        "w3": np.stack([tiles(w) for w in x["ffn_w3"].reshape(4, D, FF)]),
        "w2": x["ffn_w2"].reshape(4, FC, P, D),
        "ssm_in": group_tiles, "ssm_dt": tiles(w_in[:, 5120:5152], 32)[0],
        "ssm_out": x["ssm_w_out"].reshape(4 * GROUPS, P, D),
        "w_kv": tiles(kv), "w_q": tiles(x["w_q"][0]), "w_o": x["w_o"].reshape(8, P, D),
        "rel_bias": x["rel_bias"],
        "mla_in": tiles(rope_cols), "rwkv_in": tiles(w_in2[:, 672:]),
        "mla_u": np.concatenate([
            uq.reshape(4, 2, P, 3 * QK).transpose(0, 2, 1, 3).reshape(4, P, 6 * QK),
            uk.reshape(4, 2, P, 2 * QK).transpose(0, 2, 1, 3).reshape(4, P, 4 * QK)], 2),
        "mla_uv": uv,
        "w_wa": np.concatenate([x["w2_2"][0], x["a2_2"][0]], 0), "w_g": x["g2_2"][0],
        "w_o2": x["w_o_2"].reshape(8, P, D),
        "w_pq": tiles(x["w_pq_2"][0]),
        "keys": x["sub_keys_2"][0].transpose(0, 3, 1, 2).reshape(PH, P, 2 * NKEYS),
        "expert_u": x["expert_u_2"][0].reshape(NKEYS, NKEYS, DC, P).transpose(0, 3, 2, 1).reshape(NKEYS, P, D),
        "expert_v": x["expert_v_2"][0].reshape(NKEYS, NKEYS, D),
    }


def kernel(**inputs):
    import concourse.bacc as bacc
    from concourse.bass_utils import run_bass_kernel_spmd

    nc = bacc.Bacc("TRN2", target_bir_lowering=False, num_devices=1)
    arrays = {f"in_{k}": np.ascontiguousarray(v) for k, v in pack({k: np.asarray(v) for k, v in inputs.items()}).items()}
    io = {k[3:]: nc.dram_tensor(k, a.shape, mybir.dt.from_np(a.dtype), kind="ExternalInput").ap()
          for k, a in arrays.items()}
    io["out"] = nc.dram_tensor("out", (T, D), F32, kind="ExternalOutput").ap()
    program(nc, io)
    r = run_bass_kernel_spmd(nc, [arrays], core_ids=[0])
    return r.results[0]["out"].reshape(1, T, D)
```
